# Optimizing a Trainium2 kernel written in Bass

```python
import math
import jax, jax.numpy as jnp
from jax import lax
import numpy as np

D_MODEL = 1024
BATCH = 1
SEQ = 128
DEPTH = 1
DEC_BATCH = 1
DEC_SEQ = 1024
PAST_LEN = 128

GRID_W = 64
N_DIR = 2
N_DN_HEADS = 8
DN_HEAD_DIM = 128
D_DN = N_DN_HEADS * DN_HEAD_DIM
D_RG = 1024
N_RG_BLOCKS = 8
RG_BLOCK = D_RG // N_RG_BLOCKS
D_MIX = D_DN + D_RG
CONV_W = 4
CONV_PAD_L = 2
CONV_PAD_R = CONV_W - 1 - CONV_PAD_L
CHUNK = 64
RG_C = 8.0
EPS = 1e-6
OFF_Z = 3 * D_DN
OFF_B = 4 * D_DN
OFF_A = OFF_B + N_DIR * N_DN_HEADS
OFF_RX = OFF_A + N_DIR * N_DN_HEADS
OFF_RG = OFF_RX + D_RG
D_IN = OFF_RG + D_RG

kernel_name = 'hybrid_deltanet_rglru_diffusion_step'

def rmsnorm(x, w):
    xf = x.astype(jnp.float32)
    y = xf * lax.rsqrt(jnp.mean(xf * xf, axis=-1, keepdims=True) + EPS)
    return (y * w.astype(jnp.float32)).astype(x.dtype)

def l2norm(x):
    return x * lax.rsqrt(jnp.sum(x * x, axis=-1, keepdims=True) + EPS)

def short_conv(x, w):
    t = x.shape[1]
    xp = jnp.pad(x, ((0, 0), (CONV_PAD_L, CONV_PAD_R), (0, 0)))
    return sum(xp[:, j:j + t, :] * w[j] for j in range(CONV_W))

def grid_pos_embed(n_tok, dtype):
    rows = n_tok // GRID_W
    r = jnp.repeat(jnp.arange(rows, dtype=jnp.float32), GRID_W)
    col = jnp.tile(jnp.arange(GRID_W, dtype=jnp.float32), rows)
    quarter = D_MODEL // 4
    freqs = jnp.exp(-math.log(10000.0) * jnp.arange(quarter, dtype=jnp.float32) / quarter)
    ar = r[:, None] * freqs[None]
    ac = col[:, None] * freqs[None]
    pe = jnp.concatenate([jnp.sin(ar), jnp.cos(ar), jnp.sin(ac), jnp.cos(ac)], axis=-1)
    return pe.astype(dtype)

def gated_delta_chunked(q, k, v, g, beta, s0):
    b, t, h, dk = q.shape
    dv = v.shape[-1]
    n = t // CHUNK

    def chunks(a):
        return jnp.moveaxis(a.reshape((b, n, CHUNK, h) + a.shape[3:]), 3, 1)

    q = chunks(q) * (dk ** -0.5)
    k = chunks(k)
    v = chunks(v)
    beta = chunks(beta)
    g = jnp.cumsum(chunks(g), axis=-1)
    tril = jnp.tril(jnp.ones((CHUNK, CHUNK), dtype=bool))
    strict = jnp.tril(jnp.ones((CHUNK, CHUNK), dtype=bool), -1)
    decay = jnp.exp(jnp.where(tril, g[..., :, None] - g[..., None, :], -jnp.inf))
    kk = jnp.einsum('bhncd,bhnsd->bhncs', k * beta[..., None], k) * decay
    tmat = jnp.where(strict, kk, 0.0) + jnp.eye(CHUNK, dtype=jnp.float32)
    rhs = jnp.concatenate([v * beta[..., None], k * (beta * jnp.exp(g))[..., None]], axis=-1)
    sol = lax.linalg.triangular_solve(tmat, rhs, left_side=True, lower=True, unit_diagonal=True)
    u, w = sol[..., :dv], sol[..., dv:]
    attn = jnp.where(tril, jnp.einsum('bhncd,bhnsd->bhncs', q, k) * decay, 0.0)
    q_dec = q * jnp.exp(g)[..., None]
    k_dec = k * jnp.exp(g[..., -1:] - g)[..., None]
    g_last = jnp.exp(g[..., -1])

    def step(s, xs):
        u_i, w_i, attn_i, qd_i, kd_i, gl_i = xs
        v_new = u_i - jnp.einsum('bhcd,bhde->bhce', w_i, s)
        o = jnp.einsum('bhcd,bhde->bhce', qd_i, s) + jnp.einsum('bhcs,bhse->bhce', attn_i, v_new)
        s = s * gl_i[..., None, None] + jnp.einsum('bhcd,bhce->bhde', kd_i, v_new)
        return s, o

    xs = tuple(jnp.moveaxis(a, 2, 0) for a in (u, w, attn, q_dec, k_dec, g_last))
    s_fin, o = lax.scan(step, s0, xs)
    o = jnp.moveaxis(jnp.moveaxis(o, 0, 2), 1, 3).reshape(b, t, h, dv)
    return o, s_fin

def delta_branch(qkv, z, b_raw, a_raw, conv_w, a_log, dt_bias, norm_w, s0):
    bsz, t, _ = qkv.shape
    qkv = jax.nn.silu(short_conv(qkv, conv_w)).astype(jnp.float32)
    q, k, v = jnp.split(qkv.reshape(bsz, t, 3, N_DN_HEADS, DN_HEAD_DIM), 3, axis=2)
    q, k, v = l2norm(q[:, :, 0]), l2norm(k[:, :, 0]), v[:, :, 0]
    beta = jax.nn.sigmoid(b_raw.astype(jnp.float32))
    g = -jnp.exp(a_log) * jax.nn.softplus(a_raw.astype(jnp.float32) + dt_bias)
    s0 = s0.astype(jnp.float32)
    o_f, s_f = gated_delta_chunked(q, k, v, g[:, :, 0], beta[:, :, 0], s0[:, 0])
    flip = lambda a: jnp.flip(a, axis=1)
    o_b, s_b = gated_delta_chunked(flip(q), flip(k), flip(v), flip(g[:, :, 1]), flip(beta[:, :, 1]), s0[:, 1])
    o = rmsnorm(o_f + flip(o_b), norm_w) * jax.nn.silu(z.astype(jnp.float32).reshape(bsz, t, N_DN_HEADS, DN_HEAD_DIM))
    return o.reshape(bsz, t, D_DN), jnp.stack([s_f, s_b], axis=1)

def linear_scan(a, bx, h0):
    bx = bx.at[:, 0].add(a[:, 0] * h0)

    def comb(l, r):
        return l[0] * r[0], r[0] * l[1] + r[1]

    _, h = lax.associative_scan(comb, (a, bx), axis=1)
    return h

def rglru_branch(x, gate, conv_w, conv_b, w_r, b_r, w_i, b_i, lam, h0):
    bsz, t, _ = x.shape
    xf = (short_conv(x, conv_w) + conv_b).astype(jnp.float32)
    xb = xf.reshape(bsz, t, N_RG_BLOCKS, RG_BLOCK)
    r = jax.nn.sigmoid(jnp.einsum('btnk,dnkj->btdnj', xb, w_r).reshape(bsz, t, N_DIR, D_RG) + b_r)
    i = jax.nn.sigmoid(jnp.einsum('btnk,dnkj->btdnj', xb, w_i).reshape(bsz, t, N_DIR, D_RG) + b_i)
    log_a = -RG_C * r * jax.nn.softplus(-lam)
    a = jnp.exp(log_a)
    bx = jnp.sqrt(-jnp.expm1(2.0 * log_a)) * (i * xf[:, :, None, :])
    h0 = h0.astype(jnp.float32)
    h_f = linear_scan(a[:, :, 0], bx[:, :, 0], h0[:, 0])
    h_b = jnp.flip(linear_scan(jnp.flip(a[:, :, 1], 1), jnp.flip(bx[:, :, 1], 1), h0[:, 1]), 1)
    y = (h_f + h_b) * jax.nn.silu(gate.astype(jnp.float32))
    return y, jnp.stack([h_f[:, -1], h_b[:, 0]], axis=1)

def mixer_layer(x, mod, s_dn0, s_rg0, pre_w, post_w, w_in, w_out, dn_conv_w, dn_a_log, dn_dt_bias,
                dn_norm_w, rg_conv_w, rg_conv_b, rg_w_r, rg_b_r, rg_w_i, rg_b_i, rg_lam):
    bsz, t, _ = x.shape
    shift, scale, gate = jnp.split(mod[:, None, :].astype(x.dtype), 3, axis=-1)
    h = rmsnorm(x, pre_w) * (1 + scale) + shift
    proj = h @ w_in
    o_dn, s_dn = delta_branch(
        proj[..., :OFF_Z], proj[..., OFF_Z:OFF_B],
        proj[..., OFF_B:OFF_A].reshape(bsz, t, N_DIR, N_DN_HEADS),
        proj[..., OFF_A:OFF_RX].reshape(bsz, t, N_DIR, N_DN_HEADS),
        dn_conv_w, dn_a_log, dn_dt_bias, dn_norm_w, s_dn0)
    o_rg, s_rg = rglru_branch(proj[..., OFF_RX:OFF_RG], proj[..., OFF_RG:], rg_conv_w, rg_conv_b,
                              rg_w_r, rg_b_r, rg_w_i, rg_b_i, rg_lam, s_rg0)
    y = jnp.concatenate([o_dn, o_rg], axis=-1).astype(x.dtype) @ w_out
    return x + gate * rmsnorm(y, post_w), s_dn, s_rg

def setup_inputs(seed: int = 0) -> dict:
    key = jax.random.key(seed)
    ks = jax.random.split(key, 23)
    f32 = jnp.float32
    nrm = lambda k, shape, s: s * jax.random.normal(k, shape, f32)
    L = DEPTH
    dt = jnp.exp(jax.random.uniform(ks[14], (L, N_DIR, N_DN_HEADS), f32, math.log(1e-3), math.log(1e-1)))
    u = jax.random.uniform(ks[22], (L, N_DIR, D_RG), f32, 0.9, 0.999)
    log_sig = jnp.log(u) / RG_C
    return {
        'x_prompt': nrm(ks[0], (BATCH, SEQ, D_MODEL), 1.0),
        'x_sample': nrm(ks[1], (DEC_BATCH, DEC_SEQ, D_MODEL), 1.0),
        'state_delta': nrm(ks[2], (DEC_BATCH, L, N_DIR, N_DN_HEADS, DN_HEAD_DIM, DN_HEAD_DIM), 0.3),
        'state_rglru': nrm(ks[3], (DEC_BATCH, L, N_DIR, D_RG), 0.5),
        'c': nrm(ks[4], (DEC_BATCH, D_MODEL), 1.0),
        'c_ctx': nrm(ks[5], (D_MODEL,), 1.0),
        'ada_w': nrm(ks[6], (L, D_MODEL, 3 * D_MODEL), D_MODEL ** -0.5),
        'ada_b': nrm(ks[7], (L, 3 * D_MODEL), 0.02),
        'pre_norm_w': 1.0 + nrm(ks[8], (L, D_MODEL), 0.02),
        'post_norm_w': 1.0 + nrm(ks[9], (L, D_MODEL), 0.02),
        'w_in': nrm(ks[10], (L, D_MODEL, D_IN), D_MODEL ** -0.5),
        'w_out': nrm(ks[11], (L, D_MIX, D_MODEL), D_MIX ** -0.5),
        'dn_conv_w': nrm(ks[12], (L, CONV_W, 3 * D_DN), CONV_W ** -0.5),
        'dn_a_log': jnp.log(jax.random.uniform(ks[13], (L, N_DIR, N_DN_HEADS), f32, 1.0, 16.0)),
        'dn_dt_bias': dt + jnp.log(-jnp.expm1(-dt)),
        'dn_norm_w': 1.0 + nrm(ks[15], (L, DN_HEAD_DIM), 0.02),
        'rg_conv_w': nrm(ks[16], (L, CONV_W, D_RG), CONV_W ** -0.5),
        'rg_conv_b': nrm(ks[17], (L, D_RG), 0.01),
        'rg_w_r': nrm(ks[18], (L, N_DIR, N_RG_BLOCKS, RG_BLOCK, RG_BLOCK), RG_BLOCK ** -0.5),
        'rg_b_r': nrm(ks[19], (L, N_DIR, D_RG), 0.01),
        'rg_w_i': nrm(ks[20], (L, N_DIR, N_RG_BLOCKS, RG_BLOCK, RG_BLOCK), RG_BLOCK ** -0.5),
        'rg_b_i': nrm(ks[21], (L, N_DIR, D_RG), 0.01),
        'rg_lam': log_sig - jnp.log(-jnp.expm1(log_sig)),
    }

def reference(x_prompt, x_sample, state_delta, state_rglru, c, c_ctx, ada_w, ada_b, pre_norm_w,
              post_norm_w, w_in, w_out, dn_conv_w, dn_a_log, dn_dt_bias, dn_norm_w, rg_conv_w,
              rg_conv_b, rg_w_r, rg_b_r, rg_w_i, rg_b_i, rg_lam):
    xp = x_prompt
    xs = x_sample + grid_pos_embed(x_sample.shape[1], x_sample.dtype)[None]
    bp = x_prompt.shape[0]
    new_dn, new_rg = [], []
    for l in range(DEPTH):
        params = (pre_norm_w[l], post_norm_w[l], w_in[l], w_out[l], dn_conv_w[l], dn_a_log[l],
                  dn_dt_bias[l], dn_norm_w[l], rg_conv_w[l], rg_conv_b[l], rg_w_r[l], rg_b_r[l],
                  rg_w_i[l], rg_b_i[l], rg_lam[l])
        mod_ctx = jax.nn.silu(c_ctx[None]) @ ada_w[l] + ada_b[l]
        mod_lat = jax.nn.silu(c) @ ada_w[l] + ada_b[l]
        zero_dn = jnp.zeros((bp, N_DIR, N_DN_HEADS, DN_HEAD_DIM, DN_HEAD_DIM), jnp.float32)
        zero_rg = jnp.zeros((bp, N_DIR, D_RG), jnp.float32)
        xp, s_dn, s_rg = mixer_layer(xp, mod_ctx, zero_dn, zero_rg, *params)
        xs, _, _ = mixer_layer(xs, mod_lat, state_delta[:, l], state_rglru[:, l], *params)
        new_dn.append(s_dn.astype(x_prompt.dtype))
        new_rg.append(s_rg.astype(x_prompt.dtype))
    new_state_delta = jnp.stack(new_dn, axis=1)
    new_state_rglru = jnp.stack(new_rg, axis=1)
    return (xp, xs, new_state_delta, new_state_rglru)


_drawn_inputs = setup_inputs


def setup_inputs(seed=0):
    import zlib

    import numpy as np

    out = dict(_drawn_inputs(seed))
    spreads = {}
    factors = {'state_delta': 4.599,
     'state_rglru': 5.957,
     'post_norm_w': 15.892,
     'dn_norm_w': 27.297,
     'rg_conv_b': 3.656,
     'rg_b_r': 44.057,
     'rg_b_i': 8.0}
    for name, (base, spread) in spreads.items():
        noise = np.random.default_rng([zlib.crc32(name.encode()), seed]).standard_normal(out[name].shape)
        drawn = base * np.exp(spread * noise) if base else spread * noise
        out[name] = __import__('jax').numpy.asarray(drawn.astype(out[name].dtype))
    for name, factor in factors.items():
        out[name] = (out[name] * factor).astype(out[name].dtype)
    return out
```

```python
import math
from contextlib import ExitStack

import numpy as np

import concourse.bass as bass
from concourse import mybir

ALU = mybir.AluOpType
ACT = mybir.ActivationFunctionType
AX = mybir.AxisListType
F32 = mybir.dt.float32

P = 128
D = 1024
KT = D // P
HEADS = 8
NCH = 9
TOK = NCH * P
GAP = 2
TW = TOK + GAP
RAW = 2 + TW + 1
GROUPS = [(0, 386), (386, 384), (770, 384)]
DIRS = 2
INST = DIRS * NCH
OFF_B = 4 * D
OFF_RX = OFF_B + 4 * HEADS
OFF_RG = OFF_RX + D
EPS = 1e-6
MASKED = -1e30
BLK = 32
SQ = BLK * BLK


def col(c):
    return 0 if c == 0 else GAP + P * c


class Count:

    def __init__(self, sem, before, per_head):
        self.sem, self.before, self.per_head = sem, before, per_head

    def at(self, head, n):
        return head * self.per_head + (self.before + n)


class Chain:

    def __init__(self, engine, sem):
        self.engine, self.sem, self.n = engine, sem, 0

    def __call__(self, instruction):
        self.later(instruction)
        self.settle()

    def later(self, instruction):
        instruction.then_inc(self.sem, 1)
        self.n += 1

    def settle(self):
        self.engine.wait_ge(self.sem, self.n)

    def clear(self):
        self.settle()
        self.engine.sem_clear(self.sem)
        self.n = 0


def hybrid_layer(nc, x_prompt, x_sample, state_delta, state_rglru, c, c_ctx, ada_w, ada_b, pre_norm_w,
                 post_norm_w, w_in, w_out, dn_conv_w, dn_a_log, dn_dt_bias, dn_norm_w, rg_conv_w, rg_conv_b,
                 rg_w_r, rg_b_r, rg_w_i, rg_b_i, rg_lam, pos_row, pos_col,
                 y_prompt, y_sample, new_delta, new_rglru):
    ctx = ExitStack()
    with ctx:
        def sem(name):
            return ctx.enter_context(nc.semaphore(name))

        sizes = {
            "hT": KT * TW, "w": 3 * KT * P, "raw": 4 * RAW, "kq": 2 * TW, "vT": TW, "xf": TW, "decay": 2 * TOK,
            "nmat": 2 * TOK, "ktok": TOK, "vtok": TOK, "sub": 3 * SQ, "sub_tmp": 256, "Z": INST * P, "Zt": INST * P,
            "Q": 2 * 3 * P, "qd": 2 * TOK, "sz": TW, "sg": TW, "rg": 4 * TW,
            "scan_tmp": 6 * P, "S": 2 * P, "S_new": 2 * P, "wg": 4 * P, "ident": P, "tri": 2 * P, "ones": P,
            "mask32": 2 * P, "colsA": P, "colsB": P, "ba": NCH * 32, "cum": NCH * 16, "tot": NCH * 16,
            "beta": NCH * 16, "eG": NCH * 16, "edec": NCH * 16, "gl": NCH * 16, "head_cols": 16 * 20,
            "small": 96,
        }
        total = sum(sizes.values())
        arena = ctx.enter_context(nc.sbuf_tensor("arena", [P, total], F32))
        at, off = {}, 0
        for name, n in sizes.items():
            at[name] = off
            off += n

        def view(name, start=0, n=None):
            n = sizes[name] - start if n is None else n
            return arena[:, at[name] + start:at[name] + start + n]

        hT = view("hT").rearrange("p (k t) -> p k t", k=KT)
        w_ring = view("w").rearrange("p (s k n) -> p s k n", s=3, k=KT)
        raw = view("raw").rearrange("p (j t) -> p j t", j=4)
        kq = view("kq").rearrange("p (j t) -> p j t", j=2)
        kT, qT = kq[:, 0], kq[:, 1]
        vT = view("vT")
        xf = view("xf")
        decay = view("decay").rearrange("p (m i) -> p m i", i=P)
        nmat = view("nmat").rearrange("p (m i) -> p m i", i=P)
        ktok = view("ktok").rearrange("p (c d) -> p c d", d=P)
        vtok = view("vtok").rearrange("p (c d) -> p c d", d=P)
        sub = [view("sub", i * SQ, SQ) for i in range(3)]
        block_in, block_T = (s.rearrange("p (m c) -> p m c", c=BLK) for s in (sub[0], sub[2]))
        Z = view("Z").rearrange("p (m i) -> p m i", i=P)
        Zt = view("Zt").rearrange("p (m i) -> p m i", i=P)
        Qb = view("Q").rearrange("p (b m i) -> p b m i", b=2, i=P)
        qd = view("qd").rearrange("p (d t) -> p d t", d=2)
        sz, sg = view("sz"), view("sg")
        RA, RB, RC, RH = (view("rg", i * TW, TW) for i in range(4))
        rhs_v = view("scan_tmp", 0, 2 * P).rearrange("p (d v) -> p d v", d=2)
        vt = view("scan_tmp", 2 * P, 2 * P).rearrange("p (d v) -> p d v", d=2)
        vd = view("scan_tmp", 4 * P, 2 * P).rearrange("p (d v) -> p d v", d=2)
        S = view("S").rearrange("p (d v) -> p d v", d=2)
        S_new = view("S_new").rearrange("p (d v) -> p d v", d=2)
        wg = view("wg").rearrange("p (n j) -> p n j", n=4)
        ident, ones = view("ident"), view("ones")
        tri = view("tri").rearrange("p (d i) -> p d i", d=2)
        mask32 = view("mask32").rearrange("p (d i) -> p d i", d=2)
        colsA, colsB = view("colsA"), view("colsB")
        ba = view("ba").rearrange("p (c n) -> p c n", n=32)
        cols = {n: view(n).rearrange("p (c n) -> p c n", n=16) for n in ("cum", "tot", "beta", "eG", "edec", "gl")}
        o_tok = vT[:, 0:TOK].rearrange("p (c d) -> p c d", d=P)
        hc = view("head_cols")
        small = view("small")
        hcv = {n: hc[:, i * 20:i * 20 + INST].rearrange("p (d c) -> p d c", d=2)
               for i, n in enumerate(("cum", "negeG", "Pk", "Pdec", "gl"))}
        hcc = {n: hc[:, 100 + i * 10:100 + i * 10 + NCH]
               for i, n in enumerate(("ssk", "ssq", "rk2", "rkinv", "sso", "rstd", "epsq"))}
        half_b = hc[:, 180:212].rearrange("p (n b) -> p n b", b=8)
        c8 = hc[:, 212:228].rearrange("p (d b) -> p d b", b=8)
        nc8 = hc[:, 228:244].rearrange("p (d b) -> p d b", b=8)
        st_rg = hc[:, 244:260].rearrange("p (d b) -> p d b", b=8)
        rg_tab = hc[:, 180:244].rearrange("p (n b) -> p n b", b=8)
        rg_cols = hc[:, 262:270]
        br_h, bi_h, c8_h, nc8_h = (rg_cols[:, 2 * i:2 * i + 2] for i in range(4))
        pf, pb = hc[:, 260:261], hc[:, 261:262]
        convw = colsA[:, 0:96].rearrange("p (j t) -> p j t", j=4)
        rconvw = colsA[:, 96:128].rearrange("p (j t) -> p j t", j=4)
        B_C, B_PRE, B_CB, B_BR, B_BI, B_LAM, B_ST, B_NW, B_ROWS = 0, 16, 24, 32, 48, 64, 80, 96, 97

        base = [at["raw"]]

        def early(n):
            base[0] += n
            return arena[:, base[0] - n:base[0]]

        adaw = early(KT * 3 * D).rearrange("p (k n) -> p k n", k=KT)
        mod_row, ada_brow = early(3 * D), early(3 * D)
        x_in = early(2 * D).rearrange("p (b n) -> p b n", b=2)
        pos = early(2 * D).rearrange("p (b n) -> p b n", b=2)
        rowsA, rowsB = early(P), early(P)
        assert base[0] <= at["wg"]
        square_out = view("w", KT * P, KT * P)
        base[0] = at["kq"]
        baT, G_rows = early(TW), early(2 * TOK).rearrange("p (d t) -> p d t", d=2)
        N_SP = NCH * 16 + 16
        sp_y, sp_e, sp_z, sp_z2, sp_p, sp_r = (early(N_SP) for _ in range(6))
        dt_bias, a_log = small[:, 56:72], small[:, 72:88]
        mod_ab = small[:, 0:32].rearrange("p (s k) -> p s k", s=4)
        silu_c = small[:, 32:48].rearrange("p (s k) -> p s k", s=2)
        x_ss = small[:, 48:50]

        banks = [ctx.enter_context(nc.psum_tensor(f"bank{i}", [P, 512], F32)) for i in range(8)]
        scr_G = nc.dram_tensor("scr_G", (DIRS, HEADS, TOK), F32, kind="Internal").ap()
        scr_o = nc.dram_tensor("scr_o", (2 * HEADS, P, TOK), F32, kind="Internal").ap()
        scr_gate = nc.dram_tensor("scr_gate", (2, D), F32, kind="Internal").ap()

        rows_in, consts_in, ba_w_in = sem("rows_in"), sem("consts_in"), sem("ba_w_in")
        ada_in = [sem(f"ada_in{k}") for k in range(KT)]
        ident_made, consts_made = sem("ident_made"), sem("consts_made")
        cols_turned, cols_made, silu_c_made = sem("cols_turned"), sem("cols_made"), sem("silu_c_made")
        ada_done, mod_row_made, mod_turned, mod_made = sem("ada_done"), sem("mod_row_made"), sem("mod_turned"), sem("mod_made")
        gate_stored = sem("gate_stored")
        x_loaded = [sem("x_loaded0"), sem("x_loaded1")]
        x_added, x_squared, x_meaned, x_rooted = sem("x_added"), sem("x_squared"), sem("x_meaned"), sem("x_rooted")
        x_normed, x_turned, h_made_v, h_made_a = sem("x_normed"), sem("x_turned"), sem("h_made_v"), sem("h_made_a")
        ba_done, baT_made, ba_turned, ba_made = sem("ba_done"), sem("baT_made"), sem("ba_turned"), sem("ba_made")
        sp_ready, sp_exped, g_made, G_summed, G_taken = sem("sp_ready"), sem("sp_exped"), sem("g_made"), sem("G_summed"), sem("G_taken")
        G_exp_in, G_exped, Grow_done, Grow_made, G_stored = sem("G_exp_in"), sem("G_exped"), sem("Grow_done"), sem("Grow_made"), sem("G_stored")
        grounds_made, c_tanh, cols_ready = sem("grounds_made"), sem("c_tanh"), sem("cols_ready")
        Zt_cleared = Count(sem("Zt_cleared"), 1, 1)
        v_own, a_own, g_own = sem("v_own"), sem("a_own"), sem("g_own")

        w_in_slot = [Count(sem("w_slot0"), 1, 2), Count(sem("w_slot1"), 1, 2), Count(sem("w_slot2"), 2, 2)]
        projected = Count(sem("projected"), 12, 18)
        proj_taken = Count(sem("proj_taken"), 12, 18)
        conv_done = Count(sem("conv_done"), 0, 4)
        tanh_done = Count(sem("tanh_done"), 0, 5)
        silu_done = Count(sem("silu_done"), 0, 5)
        turned = Count(sem("turned"), 0, 9)
        turn_taken_a = Count(sem("turn_taken_a"), 0, 6)
        turn_taken_v = Count(sem("turn_taken_v"), 0, 3)
        sq_k_done = Count(sem("sq_k_done"), 0, 1)
        ss_done = Count(sem("ss_done"), 0, 2)
        rk_root = Count(sem("rk_root"), 0, 1)
        v_scaled = Count(sem("v_scaled"), 0, 1)
        decay_in = Count(sem("decay_in"), 2, 2)
        S_in = Count(sem("S_in"), 2, 2)
        wg_in = Count(sem("wg_in"), 4, 4)
        eG_row = Count(sem("eG_row"), 0, 1)
        head_cols_made = Count(sem("head_cols_made"), 0, 4)
        masked = Count(sem("masked"), 0, 2)
        decay_exped = Count(sem("decay_exped"), 0, 1)
        qd_made = Count(sem("qd_made"), 0, 4)
        n_scaled = Count(sem("n_scaled"), 0, 2)
        gated = Count(sem("gated"), 0, 12)
        gate_tanh = Count(sem("gate_tanh"), 0, 12)
        rg_t_made = Count(sem("rg_t_made"), 0, 6)
        rg_u_made = Count(sem("rg_u_made"), 0, 2)
        rg_root = Count(sem("rg_root"), 0, 2)
        rg_ix_made = Count(sem("rg_ix_made"), 0, 2)
        rg_bx_made = Count(sem("rg_bx_made"), 0, 2)
        rg_scanned = Count(sem("rg_scanned"), 0, 6)
        rg_stored = Count(sem("rg_stored"), 0, 2)
        scored = Count(sem("scored"), 0, 5)
        scores_taken = Count(sem("scores_taken"), 0, 20)
        unblocked = Count(sem("unblocked"), 0, 2)
        Z_placed = Count(sem("Z_placed"), 0, 8)
        Zt_placed = Count(sem("Zt_placed"), 0, 8)
        Q_done = Count(sem("Q_done"), 0, 12)
        Q_taken = Count(sem("Q_taken"), 0, 12)
        dZ_done = Count(sem("dZ_done"), 0, 12)
        dZ_taken = Count(sem("dZ_taken"), 0, 30)
        KS_done = Count(sem("KS_done"), 0, 16)
        rhs_made = Count(sem("rhs_made"), 0, 16)
        solved = Count(sem("solved"), 0, 18)
        vnew_made = Count(sem("vnew_made"), 0, 36)
        stepped = Count(sem("stepped"), 0, 18)
        S_made = Count(sem("S_made"), 0, 16)
        o_made = Count(sem("o_made"), 0, 17)
        prompt_S_stored = Count(sem("prompt_S_stored"), 0, 1)
        o_squared = Count(sem("o_squared"), 0, 1)
        o_meaned = Count(sem("o_meaned"), 0, 1)
        o_rooted = Count(sem("o_rooted"), 0, 1)
        o_normed = Count(sem("o_normed"), 0, 1)
        o_turned = Count(sem("o_turned"), 0, 3)
        oz_made = Count(sem("oz_made"), 0, 4)
        oz_stored = Count(sem("oz_stored"), 0, 1)
        w_out_in = [sem(f"w_out_in{i}") for i in range(4)]
        post_in, gate_post_made, states_stored = sem("post_in"), sem("gate_post_made"), sem("states_stored")
        states_turned, states_taken = sem("states_turned"), sem("states_taken")
        ot_in = [sem("ot_in0"), sem("ot_in1")]
        xr_in = [sem("xr_in0"), sem("xr_in1")]
        xr_added, y_done, y_squared, y_meaned, y_rooted, y_made, raw_cleared = (
            sem(n) for n in ("xr_added", "y_done", "y_squared", "y_meaned", "y_rooted", "y_made", "raw_cleared"))
        y_stored = [sem("y_stored0"), sem("y_stored1")]

        wo = arena[:, 0:2 * HEADS * D].rearrange("p (k n) -> p k n", n=D)
        assert 2 * HEADS * D <= at["kq"]
        ot = arena[:, at["decay"]:at["decay"] + 2 * 16 * P].rearrange("p (b k t) -> p b k t", b=2, k=16)
        base[0] = at["ktok"]
        x_res = early(2 * D).rearrange("p (b n) -> p b n", b=2)
        pos_res = early(2 * D).rearrange("p (b n) -> p b n", b=2)
        y_out = early(2 * D).rearrange("p (b n) -> p b n", b=2)
        gate_post = early(2 * D).rearrange("p (b n) -> p b n", b=2)
        post_b = early(D)
        y_junk = early(D)
        assert base[0] <= at["qd"]
        y_ss = small[:, 0:8]

        SECTION = {"z": 3 * D, "gate": OFF_RG, "k": D, "q": 0, "v": 2 * D, "rx": OFF_RX}
        TILES = ["z", "gate", "k", "q", "v", "rx"]
        w_in2, w_out2 = w_in[0], w_out[0]
        bd = bass.ds

        def w_tile(name, head):
            return w_in2[:, bd(P * (head + SECTION[name] // P) + SECTION[name] % P, P)].rearrange("(k p) n -> p k n", p=P)

        block = ctx.enter_context(nc.Block())

        @block.sync
        def _(sp):
            sp.dma_start(rowsA[0:96, :], dn_conv_w[0].rearrange("j (t p) -> (j t) p", p=P)).then_inc(rows_in, 16)
            sp.dma_start(rowsA[96:128, :], rg_conv_w[0].rearrange("j (t p) -> (j t) p", p=P)).then_inc(rows_in, 16)
            for first, src in ((B_C, c_ctx.rearrange("(k p) -> k p", p=P)), (B_C + 8, c[0].rearrange("(k p) -> k p", p=P)),
                               (B_PRE, pre_norm_w[0].rearrange("(k p) -> k p", p=P)),
                               (B_CB, rg_conv_b[0].rearrange("(k p) -> k p", p=P)),
                               (B_BR, rg_b_r[0].rearrange("d (k p) -> (d k) p", p=P)),
                               (B_BI, rg_b_i[0].rearrange("d (k p) -> (d k) p", p=P)),
                               (B_LAM, rg_lam[0].rearrange("d (k p) -> (d k) p", p=P)),
                               (B_ST, state_rglru[0, 0].rearrange("d (k p) -> (d k) p", p=P)),
                               (B_NW, dn_norm_w)):
                sp.dma_start(rowsB[first:first + src.shape[0], :], src).then_inc(rows_in, 16)
            for k in range(KT):
                sp.dma_start(adaw[:, k, :], ada_w[0, k * P:(k + 1) * P, :]).then_inc(ada_in[k], 16)
            sp.dma_start(ada_brow[0:2, :], ada_b.to_broadcast([2, 3 * D]))\
              .then_inc(consts_in, 16)
            sp.dma_start(dt_bias, dn_dt_bias.rearrange("l d h -> l (d h)").to_broadcast([P, 16])).then_inc(consts_in, 16)
            sp.dma_start(a_log, dn_a_log.rearrange("l d h -> l (d h)").to_broadcast([P, 16])).then_inc(consts_in, 16)
            for b in range(2):
                for half in range(2):
                    sp.dma_start(pos[64 * half:64 * half + 64, b, 512:], pos_col).then_inc(consts_in, 16)
            sp.dma_start(x_in[:, 0], x_prompt[0]).then_inc(x_loaded[0], 16)

            def load_x(buf, xs, ps, tile, s):
                sp.dma_start(xs[:, buf], x_sample[0, bd(P * tile, P), :]).then_inc(s[buf], 16)
                for half in range(2):
                    sp.dma_start(ps[64 * half:64 * half + 64, buf, 0:512],
                                 pos_row[bd(2 * tile + half, 1), :].to_broadcast([64, 512])).then_inc(s[buf], 16)

            load_x(1, x_in, pos, 0, x_loaded)
            with sp.Fori(0, 3) as i:
                sp.wait_ge(x_turned, 4 * i + 2)
                load_x(0, x_in, pos, 2 * i + 1, x_loaded)
                sp.wait_ge(x_turned, 4 * i + 4)
                load_x(1, x_in, pos, 2 * i + 2, x_loaded)
            sp.wait_ge(x_turned, 14)
            load_x(0, x_in, pos, 7, x_loaded)
            sp.dma_start(w_ring[:, 0, :, 0:32], w_in2[:, OFF_B:OFF_RX].rearrange("(k p) n -> p k n", p=P)).then_inc(ba_w_in, 16)
            sp.wait_ge(mod_row_made, 6)
            sp.dma_start(scr_gate, mod_row[0:2, 2 * D:]).then_inc(gate_stored, 16)

            def load_w(slot, name, head):
                sp.dma_start(w_ring[:, slot], w_tile(name, head)).then_inc(w_in_slot[slot].sem, 16)

            load_w(2, "k", 0)
            sp.wait_ge(x_squared, NCH)
            load_w(1, "v", 0)
            sp.wait_ge(ba_done, 1)
            load_w(0, "q", 0)
            sp.wait_ge(projected.sem, 3)
            load_w(2, "rx", 0)
            sp.wait_ge(projected.sem, 6)
            load_w(0, "z", 0)
            sp.wait_ge(projected.sem, 9)
            load_w(1, "gate", 0)

            def load_head(head):
                for d in range(DIRS):
                    sp.dma_start(decay.rearrange("p (d c) i -> p d (c i)", d=2)[:, d],
                                 scr_G[d, bd(head, 1), :].to_broadcast([P, TOK])).then_inc(decay_in.sem, 16)
                for d in range(DIRS):
                    sp.dma_start(S[:, d], state_delta[0, 0, d, bd(head, 1)].rearrange("a k v -> (a k) v"))\
                      .then_inc(S_in.sem, 16)

            def load_gates(head):
                for n, src in enumerate((rg_w_r[0, 0], rg_w_r[0, 1], rg_w_i[0, 0], rg_w_i[0, 1])):
                    sp.dma_start(wg[:, n], src[bd(head, 1)].rearrange("a k j -> (a k) j")).then_inc(wg_in.sem, 16)

            load_gates(0)
            for d in range(DIRS):
                sp.wait_ge(G_taken, 5 + 3 * d)
                sp.dma_start(scr_G[d], G_rows[0:HEADS, d]).then_inc(G_stored, 16)
            sp.wait_ge(G_stored, 32)
            load_head(0)

            def head_loads(h):
                for j in range(2, 6):
                    sp.wait_ge(projected.sem, projected.at(h, 3 * j - 6))
                    load_w(j % 3, TILES[j], h + 1)
                sp.wait_ge(gated.sem, gated.at(h, 12))
                load_gates(h + 1)
                for j in range(2):
                    sp.wait_ge(projected.sem, projected.at(h, 3 * j + 12))
                    load_w(j, TILES[j], h + 1)
                sp.wait_ge(stepped.sem, stepped.at(h, 18))
                load_head(h + 1)

            with sp.Fori(0, HEADS - 1) as h:
                head_loads(h)
            h = HEADS - 1
            sp.wait_ge(projected.sem, projected.at(h, 6))
            sp.wait_ge(conv_done.sem, conv_done.at(h, 4))
            for q in range(4):
                sp.dma_start(wo[:, 4 * q:4 * q + 4, :],
                             w_out2[512 * q:512 * q + 512, :].rearrange("(k p) n -> p k n", p=P)).then_inc(w_out_in[q], 16)
            sp.wait_ge(stepped.sem, stepped.at(h, 18))
            sp.wait_ge(o_made.sem, o_made.at(h, 17))
            sp.wait_ge(gate_stored, 16)
            for s in range(2):
                sp.dma_start(gate_post[:, s], scr_gate[s:s + 1, :].to_broadcast([P, D])).then_inc(post_in, 16)
            sp.dma_start(post_b, post_norm_w.to_broadcast([P, D])).then_inc(post_in, 16)
            for b in range(2):
                for half in range(2):
                    sp.dma_start(pos_res[64 * half:64 * half + 64, b, 512:], pos_col).then_inc(post_in, 16)
            sp.dma_start(x_res[:, 0], x_prompt[0]).then_inc(xr_in[0], 16)
            load_x(1, x_res, pos_res, 0, xr_in)
            sp.wait_ge(oz_stored.sem, 16 * oz_stored.at(h, 1))
            sp.wait_ge(rg_stored.sem, 16 * rg_stored.at(h, 2))

            def load_o(buf, tile):
                sp.dma_start(ot[:, buf], scr_o[:, :, bd(P * tile, P)].rearrange("k p t -> p k t")).then_inc(ot_in[buf], 16)

            load_o(0, 0)
            load_o(1, 1)
            sp.wait_ge(states_taken, 1)
            sp.dma_start(new_rglru[0, 0].rearrange("d (b p) -> (d b) p", p=P), hc[0:16, 0:P]).then_inc(states_stored, 16)
            sp.wait_ge(y_made, 1)
            sp.dma_start(y_prompt[0], y_out[:, 0]).then_inc(y_stored[0], 16)
            load_o(0, 2)
            load_x(0, x_res, pos_res, 1, xr_in)

            def store_y(buf, tile):
                sp.dma_start(y_sample[0, bd(P * tile, P), :], y_out[:, buf]).then_inc(y_stored[buf], 16)

            with sp.Fori(0, 3) as i:
                sp.wait_ge(y_made, 2 * i + 2)
                store_y(1, 2 * i)
                load_o(1, 2 * i + 3)
                load_x(1, x_res, pos_res, 2 * i + 2, xr_in)
                sp.wait_ge(y_made, 2 * i + 3)
                store_y(0, 2 * i + 1)
                load_o(0, 2 * i + 4)
                load_x(0, x_res, pos_res, 2 * i + 3, xr_in)
            sp.wait_ge(y_made, 8)
            store_y(1, 6)
            sp.wait_ge(y_made, 9)
            store_y(0, 7)
            sp.wait_ge(y_stored[0], 16 * 5)
            sp.wait_ge(y_stored[1], 16 * 4)
            sp.wait_ge(states_stored, 16)
            sp.wait_ge(prompt_S_stored.sem, 16 * HEADS)

        @block.gpsimd
        def _(gp):
            own = Chain(gp, g_own)
            own(gp.memset(ident, 0.0))
            own(gp.affine_select(out=ident, in_=ident, compare_op=ALU.not_equal, fill=1.0, base=0,
                                 pattern=[[-1, P]], channel_multiplier=1))
            own(gp.memset(tri, 1.0))
            own(gp.affine_select(out=tri[:, 0], in_=tri[:, 0], compare_op=ALU.is_ge, fill=0.0, base=0,
                                 pattern=[[1, P]], channel_multiplier=-1))
            own(gp.affine_select(out=tri[:, 1], in_=tri[:, 1], compare_op=ALU.is_ge, fill=0.0, base=0,
                                 pattern=[[-1, P]], channel_multiplier=1))
            own(gp.memset(ones, 1.0))
            own(gp.memset(mask32, 0.0))
            for d in range(DIRS):
                for b in (0, 2):
                    r, cc = (b + 1, b) if d == 0 else (b, b + 1)
                    own(gp.memset(mask32[BLK * r:BLK * r + BLK, d, BLK * cc:BLK * cc + BLK], -1.0))
            gp.memset(hT[:, :, P:P + GAP], 0.0).then_inc(consts_made, 1)

            gp.wait_ge(ada_done, 6)
            gp.memset(raw, 0.0).then_inc(raw_cleared, 1)
            own(gp.memset(sub[0], 0.0))
            gp.memset(Z, 0.0).then_inc(grounds_made, 1)
            gp.memset(Zt, 0.0).then_inc(Zt_cleared.sem, 1)
            gp.wait_ge(cols_ready, 1)
            gp.wait_ge(gate_stored, 16)

            dview = decay.rearrange("p (d c) i -> p d c i", d=2)
            nview = nmat.rearrange("p (d c) i -> p d c i", d=2)
            chv = {n: cols[n].rearrange("p c (d h) -> p h d c", d=2) for n in ("cum", "eG", "gl")}
            runs = [(0, 0, P), (P, P + GAP, TOK - P)]

            def head(h, last=False):
                own.n = 0
                for n, to in (("cum", "cum"), ("eG", "negeG"), ("gl", "gl")):
                    gp.tensor_copy(hcv[to], chv[n][:, bd(h, 1)].rearrange("p a d c -> p (a d) c")).then_inc(head_cols_made.sem, 1)
                gp.tensor_copy(rg_cols, rg_tab[:, :, bd(h, 1)].rearrange("p n a -> p (n a)")).then_inc(head_cols_made.sem, 1)
                gp.wait_ge(head_cols_made.sem, head_cols_made.at(h, 4))
                gp.wait_ge(eG_row.sem, eG_row.at(h, 1))
                for d in range(DIRS):
                    own(gp.tensor_tensor(dview[:, d], dview[:, d],
                                         hcv["cum"][:, d].unsqueeze(2).to_broadcast([P, NCH, P]), ALU.subtract))
                    s = 1 if d == 0 else -1
                    gp.affine_select(out=dview[:, d], in_=dview[:, d], compare_op=ALU.is_ge, fill=MASKED, base=0,
                                     pattern=[[0, NCH], [s, P]], channel_multiplier=-s).then_inc(masked.sem, 1)
                gp.wait_ge(silu_done.sem, silu_done.at(h, 2))
                for d in range(DIRS):
                    for a, b, n in runs:
                        gp.tensor_tensor(qd[:, d, a:a + n], qd[:, d, a:a + n], qT[:, b:b + n], ALU.mult)\
                          .then_inc(qd_made.sem, 1)
                gp.wait_ge(rk_root.sem, rk_root.at(h, 1))
                gp.wait_ge(turn_taken_v.sem, turn_taken_v.at(h, 3))
                gp.tensor_tensor(vtok, vtok, hcc["rkinv"].unsqueeze(2).to_broadcast([P, NCH, P]), ALU.mult)\
                  .then_inc(v_scaled.sem, 1)
                gp.wait_ge(decay_exped.sem, decay_exped.at(h, 1))
                gp.wait_ge(ss_done.sem, ss_done.at(h, 1))
                for d in range(DIRS):
                    gp.tensor_tensor(nview[:, d], dview[:, d], hcv["Pk"][:, d].unsqueeze(2).to_broadcast([P, NCH, P]),
                                     ALU.mult).then_inc(n_scaled.sem, 1)
                for d in range(DIRS):
                    gp.wait_ge(rg_root.sem, rg_root.at(h, d + 1))
                    gp.wait_ge(rg_ix_made.sem, rg_ix_made.at(h, d + 1))
                    gp.tensor_tensor(RB, RB, RC, ALU.mult).then_inc(rg_bx_made.sem, 1)
                gp.wait_ge(Q_done.sem, Q_done.at(h, 12))
                gp.wait_ge(rg_scanned.sem, rg_scanned.at(h, 6))
                own(gp.tensor_tensor(RH, RH, RC, ALU.add))
                if not last:
                    gp.memset(Zt, 0.0).then_inc(Zt_cleared.sem, 1)
                own(gp.tensor_tensor(RH, RH, sg, ALU.mult))
                for a, b, n in runs:
                    gp.dma_start(scr_o[bd(h + HEADS, 1), :, a:a + n].rearrange("a p t -> (a p) t"), RH[:, b:b + n])\
                      .then_inc(rg_stored.sem, 16)
                gp.wait_ge(S_made.sem, S_made.at(h, 2))
                gp.dma_start(new_delta[0, 0, :, bd(h, 1)].rearrange("d a k v -> k (d a) v"), S_new)\
                  .then_inc(prompt_S_stored.sem, 16)
                gp.wait_ge(oz_made.sem, oz_made.at(h, 4))
                gp.dma_start(scr_o[bd(h, 1)].rearrange("a p t -> (a p) t"), qd[:, 0]).then_inc(oz_stored.sem, 16)
                own.clear()

            own.clear()
            with gp.Fori(0, HEADS - 1) as h:
                head(h)
            head(HEADS - 1, last=True)
            gp.wait_ge(post_in, 16 * 7)
            for s in range(2):
                gp.tensor_tensor(gate_post[:, s], gate_post[:, s], post_b, ALU.mult).then_inc(gate_post_made, 1)

            def residual(buf, n):
                gp.wait_ge(xr_in[buf], n)
                gp.tensor_tensor(x_res[:, buf], x_res[:, buf], pos_res[:, buf], ALU.add).then_inc(xr_added, 1)

            with gp.Fori(0, 4) as i:
                residual(1, i * 48 + 48)
                residual(0, i * 48 + 64)

        @block.tensor
        def _(pe):
            pe.wait_ge(consts_made, 1)
            pe.wait_ge(rows_in, 16 * 11)
            pe.transpose(banks[6][:, 0:P], rowsA, ident).then_inc(cols_turned, 1)
            pe.transpose(banks[7][:, 0:B_ROWS], rowsB[0:B_ROWS, :], ident[0:B_ROWS, 0:B_ROWS]).then_inc(cols_turned, 1)
            pe.wait_ge(silu_c_made, 1)
            for k in range(KT):
                pe.wait_ge(ada_in[k], 16)
                for n in range(6):
                    mm = pe.matmul(banks[n][0:2, :], silu_c[:, :, k], adaw[:, k, 512 * n:512 * n + 512],
                                   start=(k == 0), stop=(k == KT - 1))
                    if k == KT - 1:
                        mm.then_inc(ada_done, 1)
            for m in range(16):
                pe.wait_ge(mod_row_made, m // 4 + 1)
                mm = pe.transpose(banks[6][:, 2 * m:2 * m + 2], mod_row[0:2, P * m:P * m + P], ident[0:2, 0:2])
            mm.then_inc(mod_turned, 1)
            pe.wait_ge(mod_row_made, 6)

            def turn_x(buf, n):
                pe.wait_ge(x_normed, n + 1)
                for half in range(2):
                    if not isinstance(n, int) or n > 1:
                        pe.wait_ge((h_made_v, h_made_a)[half], 4 * n - 4)
                    for k in range(4):
                        mm = pe.transpose(banks[2 * buf + half][:, P * k:P * k + P],
                                          x_in[:, buf, P * (4 * half + k):P * (4 * half + k) + P], ident)
                    mm.then_inc(x_turned, 1)

            turn_x(0, 0)
            turn_x(1, 1)
            with pe.Fori(0, 3) as i:
                turn_x(0, 2 * i + 2)
                turn_x(1, 2 * i + 3)
            turn_x(0, 8)
            pe.wait_ge(ba_w_in, 16)
            pe.wait_ge(h_made_v, 36)
            pe.wait_ge(h_made_a, 36)
            for g, (o, n) in enumerate(GROUPS):
                for k in range(KT):
                    mm = pe.matmul(banks[5 + g][0:32, 0:n], w_ring[:, 0, k, 0:32], hT[:, k, o:o + n],
                                   start=(k == 0), stop=(k == KT - 1))
                if g == 2:
                    mm.then_inc(ba_done, 1)

            def project(first, count, h=None):
                for u in range(first, first + count):
                    j, g, k = u // 24, u % 24 // 8, u % 8
                    n = u // 8
                    if u % 24 == 0:
                        slot = w_in_slot[j % 3]
                        if h is None:
                            pe.wait_ge(slot.sem, 16 if j < 5 else 32)
                        else:
                            pe.wait_ge(slot.sem, slot.at(h, j // 3 + 1) * 16)
                    if k == 0:
                        if h is not None:
                            pe.wait_ge(proj_taken.sem, proj_taken.at(h, n - 1))
                        elif n >= 8:
                            pe.wait_ge(proj_taken.sem, n - 7)
                    o, w = GROUPS[g]
                    mm = pe.matmul(banks[n % 2][:, 0:w], w_ring[:, j % 3, k], hT[:, k, o:o + w],
                                   start=(k == 0), stop=(k == KT - 1))
                    if k == KT - 1:
                        mm.then_inc(projected.sem, 1)

            project(48, 24)
            pe.wait_ge(baT_made, 3)
            for ch in range(NCH):
                mm = pe.transpose(banks[2][:, 32 * ch:32 * ch + 32], baT[0:32, col(ch):col(ch) + P], ident[0:32, 0:32])
            mm.then_inc(ba_turned, 1)
            project(72, 24)
            pe.wait_ge(g_made, 1)
            g = sp_e[:, 0:NCH * 16].rearrange("p (c n) -> p c n", n=16)
            G_ps = banks[3][:, 0:NCH * 16].rearrange("p (c n) -> p c n", n=16)
            for d in range(DIRS):
                pe.matmul(G_ps[:, :, 8 * d:8 * d + 8], tri[:, d], g[:, :, 8 * d:8 * d + 8], start=True, stop=True)\
                  .then_inc(G_summed, 1)
            pe.matmul(banks[4][:, 0:NCH * 16], ones, sp_e[:, 0:NCH * 16], start=True, stop=True).then_inc(G_summed, 1)
            row_banks = [[5, 6, 7], [2, 3, 4]]
            for d in range(DIRS):
                if d == 1:
                    pe.wait_ge(G_taken, 2)
                for ch in range(NCH):
                    mm = pe.matmul(banks[row_banks[d][ch // 4]][0:8, P * (ch % 4):P * (ch % 4) + P],
                                   g[:, ch, 8 * d:8 * d + 8], tri[:, d], start=True, stop=True)
                    if ch % 4 == 3 or ch == NCH - 1:
                        mm.then_inc(Grow_done, 1)
            project(96, 48)

            def head(h, last=False):
                def fill(first, count):
                    if not last or first < 48:
                        project(first, count, h)

                fill(0, 40)
                for j, (src, b0) in enumerate(((kT, 2), (qT, 5))):
                    pe.wait_ge(silu_done.sem, silu_done.at(h, j + 1))
                    for b in range(3):
                        for i in range(3):
                            ch = 3 * b + i
                            mm = pe.transpose(banks[b0 + b][:, P * i:P * i + P], src[:, col(ch):col(ch) + P], ident)
                        mm.then_inc(turned.sem, 1)
                fill(40, 8)
                pe.wait_ge(silu_done.sem, silu_done.at(h, 3))
                for b in range(3):
                    pe.wait_ge(turn_taken_a.sem, turn_taken_a.at(h, b + 1))
                    for i in range(3):
                        ch = 3 * b + i
                        mm = pe.transpose(banks[2 + b][:, P * i:P * i + P], vT[:, col(ch):col(ch) + P], ident)
                    mm.then_inc(turned.sem, 1)
                pe.wait_ge(wg_in.sem, wg_in.at(h, 0) * 16)
                pe.wait_ge(conv_done.sem, conv_done.at(h, 4))
                for d in range(DIRS):
                    for gate in range(2):
                        for b, (o, n) in enumerate(GROUPS):
                            if d == 0 and gate == 0:
                                pe.wait_ge(turn_taken_a.sem, turn_taken_a.at(h, 4 + b))
                            elif d == 0:
                                pe.wait_ge(turn_taken_v.sem, turn_taken_v.at(h, b + 1))
                            else:
                                pe.wait_ge(gate_tanh.sem, gate_tanh.at(h, 3 * gate + b + 1))
                            pe.matmul(banks[(2 if gate else 5) + b][:, 0:n], wg[:, 2 * gate + d], xf[:, o:o + n],
                                      start=True, stop=True).then_inc(gated.sem, 1)
                    fill(48 + 8 * d, 8)
                for f in range(5):
                    b = (5, 6, 7, 2, 3)[f]
                    pe.wait_ge(gate_tanh.sem, gate_tanh.at(h, 6 + (b - 5 if b >= 5 else b + 1) + 1))
                    for i in range(2 if f < 4 else 1):
                        ch = 2 * f + i
                        mm = pe.matmul(banks[b][:, 2 * P * i:2 * P * i + 2 * P].rearrange("p (j t) -> p j t", j=2),
                                       kT[:, col(ch):col(ch) + P], kq[:, :, col(ch):col(ch) + P], start=True, stop=True)
                    mm.then_inc(scored.sem, 1)
                fill(64, 32)
                pe.wait_ge(Z_placed.sem, Z_placed.at(h, 8))
                pe.wait_ge(Zt_placed.sem, Zt_placed.at(h, 8))
                pe.wait_ge(scores_taken.sem, scores_taken.at(h, 20))

                def q_products(level, g):
                    b = banks[2 if g % 2 == 0 else 5]
                    if g >= 2:
                        pe.wait_ge(Q_taken.sem, Q_taken.at(h, 6 * level + g - 1))
                    elif level:
                        pe.wait_ge(Q_taken.sem, Q_taken.at(h, 6))
                    if level:
                        pe.wait_ge(dZ_taken.sem, dZ_taken.at(h, 4 * g + 4))
                    for i in range(3):
                        m = 3 * g + i
                        mm = pe.matmul(b[:, P * i:P * i + P], nmat[:, m], Zt[:, m], start=True, stop=True)
                    mm.then_inc(Q_done.sem, 1)

                def join32(g):
                    b = 3 if g % 2 == 0 else 6
                    pe.wait_ge(Q_taken.sem, Q_taken.at(h, g + 1))
                    if g >= 2:
                        pe.wait_ge(dZ_taken.sem, dZ_taken.at(h, 4 * (g - 1)))
                    for i in range(3):
                        pe.matmul(banks[b][:, P * i:P * i + P], Z[:, 3 * g + i], Qb[:, g % 2, i], start=True, stop=True)
                    for i in range(3):
                        mm = pe.matmul(banks[b + 1][:, P * i:P * i + P], Qb[:, g % 2, i], Z[:, 3 * g + i],
                                       start=True, stop=True)
                    mm.then_inc(dZ_done.sem, 1)

                def join64(g):
                    b = banks[3 if g % 2 == 0 else 6]
                    pe.wait_ge(Q_taken.sem, Q_taken.at(h, 6 + g + 1))
                    pe.wait_ge(dZ_taken.sem, dZ_taken.at(h, 24 + g - 1 if g >= 2 else 24))
                    r = slice(64, P) if g < 3 else slice(0, 64)
                    for i in range(3):
                        mm = pe.matmul(b[:, P * i:P * i + P], Qb[r, g % 2, i], Z[r, 3 * g + i], start=True, stop=True)
                    mm.then_inc(dZ_done.sem, 1)

                for level, join in ((0, join32), (1, join64)):
                    for g in range(7):
                        if g < 6:
                            q_products(level, g)
                            fill(96 + 6 * level + g, 1)
                        if g > 0:
                            join(g - 1)
                pe.wait_ge(dZ_taken.sem, dZ_taken.at(h, 30))
                pe.wait_ge(v_scaled.sem, v_scaled.at(h, 1))
                pe.wait_ge(qd_made.sem, qd_made.at(h, 4))
                for step in range(NCH):
                    chunk = (step, step if step == 0 else NCH - step)
                    u = 108 + 4 * step
                    if step:
                        for d in range(DIRS):
                            if step == 1:
                                pe.wait_ge(S_in.sem, S_in.at(h, 0) * 16)
                            else:
                                pe.wait_ge(S_made.sem, S_made.at(h, 2 * step - 2 + d + 1))
                            pe.matmul(banks[2 + d][:, 0:P], kT[:, col(chunk[d]):col(chunk[d]) + P], S[:, d],
                                      start=True, stop=True).then_inc(KS_done.sem, 1)
                        fill(u, 2)
                    for d in range(DIRS):
                        if step:
                            pe.wait_ge(rhs_made.sem, rhs_made.at(h, 2 * step - 2 + d + 1))
                        rhs = rhs_v[:, d] if step else vtok[:, 0]
                        pe.matmul(banks[2 + d][:, P:2 * P], Z[:, d * NCH + chunk[d]], rhs, start=True, stop=True)\
                          .then_inc(solved.sem, 1)
                    fill(u + 2 if step else u, 2 if step else 4)
                    for d in range(DIRS):
                        ch, m = chunk[d], d * NCH + chunk[d]
                        bank = banks[4 + d]
                        pe.wait_ge(vnew_made.sem, vnew_made.at(h, 4 * step + 2 * d + 2))
                        if step:
                            pe.wait_ge(o_made.sem, o_made.at(h, 1 if step == 1 else 2 * step - 2 + d))
                            if step == 1:
                                pe.wait_ge(S_made.sem, S_made.at(h, 2))
                        if step < NCH - 1:
                            pe.matmul(bank[:, 0:P], ktok[:, ch], vd[:, d], start=True, stop=True)
                        if step == 0:
                            if d == 1:
                                pe.matmul(bank[:, P:2 * P], decay[:, 0], vt[:, 0], start=True, stop=False)
                                mm = pe.matmul(bank[:, P:2 * P], decay[:, NCH], vt[:, 1], start=False, stop=True)
                                mm.then_inc(stepped.sem, 2)
                        else:
                            pe.matmul(bank[:, P:2 * P], qd[:, d, P * ch:P * ch + P], S[:, d], start=True, stop=False)
                            pe.matmul(bank[:, P:2 * P], decay[:, m], vt[:, d], start=False, stop=True)\
                              .then_inc(stepped.sem, 1)
                pe.wait_ge(o_normed.sem, o_normed.at(h, 1))
                for b in range(3):
                    for i in range(3):
                        mm = pe.transpose(banks[(6, 7, 2)[b]][:, P * i:P * i + P], o_tok[:, 3 * b + i], ident)
                    mm.then_inc(o_turned.sem, 1)

            with pe.Fori(0, HEADS - 1) as h:
                head(h)
            head(HEADS - 1, last=True)

            pe.wait_ge(oz_made.sem, oz_made.at(HEADS - 1, 4))
            pe.wait_ge(rg_scanned.sem, rg_scanned.at(HEADS - 1, 6))
            pe.transpose(banks[7][0:16, 0:P], hc[:, 244:260], ident).then_inc(states_turned, 1)

            def out_tile(buf, n, loaded):
                pe.wait_ge(ot_in[buf], loaded)
                if not isinstance(n, int) or n >= 2:
                    pe.wait_ge(y_made, n - 1)
                for half in range(2):
                    for k in range(16):
                        mm = pe.matmul(banks[2 * buf + half][:, :], ot[:, buf, k], wo[:, k, 512 * half:512 * half + 512],
                                       start=(k == 0), stop=(k == 15))
                mm.then_inc(y_done, 1)

            for q in range(4):
                pe.wait_ge(w_out_in[q], 16)
            out_tile(0, 0, 16)
            out_tile(1, 1, 16)
            with pe.Fori(0, 3) as i:
                out_tile(0, 2 * i + 2, 16 * i + 32)
                out_tile(1, 2 * i + 3, 16 * i + 32)
            out_tile(0, 8, 80)

        @block.scalar
        def _(act):
            own = Chain(act, a_own)
            act.wait_ge(cols_made, 2)
            act.activation(silu_c, colsB[:, 0:16].rearrange("p (s k) -> p s k", s=2), ACT.Tanh, scale=0.5).then_inc(c_tanh, 1)

            def x_tile(buf, n):
                if isinstance(n, int) and n == 0:
                    act.wait_ge(x_loaded[0], 16)
                else:
                    act.wait_ge(x_added, n)
                    act.wait_ge(x_squared, n)
                act.activation(square_out, x_in[:, buf], ACT.Square, accum_out=x_ss[:, buf:buf + 1]).then_inc(x_squared, 1)
                act.wait_ge(x_meaned, n + 1)
                act.activation(x_ss[:, buf:buf + 1], x_ss[:, buf:buf + 1], ACT.Sqrt).then_inc(x_rooted, 1)
                act.wait_ge(mod_made, 3)
                act.wait_ge(x_turned, 2 * n + 2)
                s = 0 if isinstance(n, int) and n == 0 else 1
                first = 0 if s == 0 else GAP + P * n
                for k in range(4):
                    act.activation(hT[:, 4 + k, bd(first, P)], banks[2 * buf + 1][:, P * k:P * k + P], ACT.Identity,
                                   bias=mod_ab[:, 2 + s, 4 + k:5 + k], scale=mod_ab[:, s, 4 + k:5 + k]).then_inc(h_made_a, 1)

            x_tile(0, 0)
            x_tile(1, 1)
            with act.Fori(0, 3) as i:
                x_tile(0, 2 * i + 2)
                x_tile(1, 2 * i + 3)
            x_tile(0, 8)
            act.wait_ge(consts_in, 112)
            act.activation(a_log, a_log, ACT.Exp).then_inc(sp_exped, 1)

            def take_projection(n, h=None):
                j, g = n // 3, n % 3
                o, w = GROUPS[g]
                if h is None:
                    act.wait_ge(projected.sem, n - 5)
                else:
                    act.wait_ge(projected.sem, projected.at(h, n + 1))
                    if j >= 2 and g == 0:
                        act.wait_ge(conv_done.sem, conv_done.at(h, j - 1))
                if j < 2:
                    act.activation((sz, sg)[j][:, o:o + w], banks[n % 2][:, 0:w], ACT.Copy, scale=0.5)\
                       .then_inc(proj_taken.sem, 1)
                else:
                    act.activation(raw[:, j - 2, 2 + o:2 + o + w], banks[n % 2][:, 0:w], ACT.Copy)\
                       .then_inc(proj_taken.sem, 1)

            act.wait_ge(raw_cleared, 1)
            for n in range(6, 9):
                take_projection(n)
            act.wait_ge(ba_made, 1)
            act.activation(cols["beta"], ba[:, :, 0:16], ACT.Exp, scale=-1.0).then_inc(sp_exped, 1)
            act.wait_ge(sp_ready, 2)
            own(act.activation(sp_e, sp_y, ACT.Abs))
            act.activation(sp_e, sp_e, ACT.Exp, scale=-1.0).then_inc(sp_exped, 1)
            for n in range(9, 12):
                take_projection(n)
            act.wait_ge(G_exp_in, 1)
            act.activation(cols["eG"], cols["cum"], ACT.Exp).then_inc(G_exped, 1)
            act.activation(cols["gl"], cols["tot"], ACT.Exp).then_inc(G_exped, 1)
            act.activation(cols["edec"], cols["edec"], ACT.Exp).then_inc(G_exped, 1)
            for n in range(12, 18):
                take_projection(n)
            act.wait_ge(gate_stored, 16)

            def head(h, last=False):
                act.wait_ge(decay_in.sem, decay_in.at(h, 0) * 16)
                act.activation(view("qd"), view("decay"), ACT.Exp).then_inc(eG_row.sem, 1)
                for n in range(3):
                    take_projection(n, h)
                for n, (src, to) in enumerate(((kT, RA), (qT, RB))):
                    act.wait_ge(conv_done.sem, conv_done.at(h, n + 1))
                    act.activation(to, src, ACT.Tanh).then_inc(tanh_done.sem, 1)
                take_projection(3, h)
                act.wait_ge(conv_done.sem, conv_done.at(h, 3))
                act.activation(RC, vT, ACT.Tanh).then_inc(tanh_done.sem, 1)
                act.wait_ge(proj_taken.sem, proj_taken.at(h, 3))
                act.activation(RH, sz, ACT.Tanh).then_inc(tanh_done.sem, 1)
                take_projection(4, h)
                for b in range(3):
                    act.wait_ge(turned.sem, turned.at(h, b + 1))
                    act.activation(ktok[:, 3 * b:3 * b + 3], banks[2 + b][:, 0:3 * P].rearrange("p (c d) -> p c d", d=P),
                                   ACT.Copy).then_inc(turn_taken_a.sem, 1)
                take_projection(5, h)
                act.wait_ge(silu_done.sem, silu_done.at(h, 1))
                act.wait_ge(proj_taken.sem, proj_taken.at(h, 6))
                act.activation(RA, sg, ACT.Tanh).then_inc(tanh_done.sem, 1)
                act.wait_ge(silu_done.sem, silu_done.at(h, 2))
                act.wait_ge(turn_taken_a.sem, turn_taken_a.at(h, 3))
                act.activation(RB[:, 0:TOK], view("ktok"), ACT.Square).then_inc(sq_k_done.sem, 1)
                act.wait_ge(silu_done.sem, silu_done.at(h, 3))
                for b in range(3):
                    act.wait_ge(turned.sem, turned.at(h, 3 + b + 1))
                    act.activation(RC[:, 3 * P * b:3 * P * b + 3 * P], banks[5 + b][:, 0:3 * P], ACT.Square)\
                       .then_inc(turn_taken_a.sem, 1)
                act.wait_ge(masked.sem, masked.at(h, 2))
                act.activation(view("decay"), view("decay"), ACT.Exp).then_inc(decay_exped.sem, 1)
                act.wait_ge(ss_done.sem, ss_done.at(h, 1))
                act.activation(hcc["rkinv"], hcc["ssk"], ACT.Sqrt).then_inc(rk_root.sem, 1)
                act.wait_ge(head_cols_made.sem, head_cols_made.at(h, 4))
                for d in range(DIRS):
                    if d == 0:
                        act.wait_ge(silu_done.sem, silu_done.at(h, 5))
                    else:
                        act.wait_ge(rg_scanned.sem, rg_scanned.at(h, 3))
                    for b, (o, n) in enumerate(GROUPS):
                        act.wait_ge(gated.sem, gated.at(h, 6 * d + b + 1))
                        act.activation(RA[:, o:o + n], banks[5 + b][:, 0:n], ACT.Tanh, scale=0.5,
                                       bias=br_h[:, d:d + 1]).then_inc(gate_tanh.sem, 1)
                    act.wait_ge(gate_tanh.sem, gate_tanh.at(h, 6 * d + 3))
                    act.activation(RB, RA, ACT.Tanh, scale=nc8_h[:, d:d + 1], bias=nc8_h[:, d:d + 1])\
                       .then_inc(rg_t_made.sem, 1)
                    act.wait_ge(rg_t_made.sem, rg_t_made.at(h, 3 * d + 1))
                    act.activation(RA, RA, ACT.Exp, scale=c8_h[:, d:d + 1], bias=c8_h[:, d:d + 1])\
                       .then_inc(rg_t_made.sem, 1)
                    if d == 0:
                        act.wait_ge(ss_done.sem, ss_done.at(h, 2))
                    act.wait_ge(rg_t_made.sem, rg_t_made.at(h, 3 * d + 2))
                    act.activation(RC, RA, ACT.Square).then_inc(rg_t_made.sem, 1)
                    if not last:
                        take_projection(6 + d, h)
                    act.wait_ge(rg_u_made.sem, rg_u_made.at(h, d + 1))
                    for b, (o, n) in enumerate(GROUPS):
                        act.wait_ge(gated.sem, gated.at(h, 6 * d + 3 + b + 1))
                        act.activation(RC[:, o:o + n], banks[2 + b][:, 0:n], ACT.Tanh, scale=0.5,
                                       bias=bi_h[:, d:d + 1]).then_inc(gate_tanh.sem, 1)
                    act.activation(RB, RB, ACT.Sqrt, scale=0.25).then_inc(rg_root.sem, 1)
                if not last:
                    for n in range(8, 12):
                        take_projection(n, h)
                act.wait_ge(Zt_cleared.sem, Zt_cleared.at(h, 0))
                for d in range(DIRS):
                    src = block_T if d else block_in
                    act.wait_ge(unblocked.sem, unblocked.at(h, 2))
                    for q in range(4):
                        r = slice(BLK * q, BLK * q + BLK)
                        act.activation(Zt[r, NCH * d:NCH * d + NCH, r], src[r, NCH * d:NCH * d + NCH, :], ACT.Copy)\
                           .then_inc(Zt_placed.sem, 1)
                for g in range(6):
                    act.wait_ge(dZ_done.sem, dZ_done.at(h, g + 1))
                    m = slice(3 * g, 3 * g + 3)
                    for to, bank, below in ((Zt, 3, g < 3), (Z, 4, g >= 3)):
                        ps = banks[bank + 3 * (g % 2)][:, 0:3 * P].rearrange("p (m i) -> p m i", i=P)
                        for b in (0, 2):
                            r, cc = (b + 1, b) if below else (b, b + 1)
                            r, cc = slice(BLK * r, BLK * r + BLK), slice(BLK * cc, BLK * cc + BLK)
                            act.activation(to[r, m, cc], ps[r, :, cc], ACT.Copy).then_inc(dZ_taken.sem, 1)
                for g in range(6):
                    act.wait_ge(dZ_done.sem, dZ_done.at(h, 6 + g + 1))
                    ps = banks[3 + 3 * (g % 2)][:, 0:3 * P].rearrange("p (m i) -> p m i", i=P)
                    r, cc = (slice(0, 64), slice(64, P)) if g < 3 else (slice(64, P), slice(0, 64))
                    act.activation(Z[r, 3 * g:3 * g + 3, cc], ps[r, :, cc], ACT.Copy).then_inc(dZ_taken.sem, 1)
                if not last:
                    take_projection(12, h)
                for step in range(NCH):
                    chunk = (step, step if step == 0 else NCH - step)
                    for d in range(DIRS):
                        act.wait_ge(solved.sem, solved.at(h, 2 * step + d + 1))
                        c1 = slice(chunk[d], chunk[d] + 1)
                        for to, scale in ((vd, "Pdec"), (vt, "Pk")):
                            act.activation(to[:, d], banks[2 + d][:, P:2 * P], ACT.Copy, scale=hcv[scale][:, d, c1])\
                               .then_inc(vnew_made.sem, 1)
                    if step % 2 == 0 and not last:
                        take_projection(13 + step // 2, h)
                act.wait_ge(o_made.sem, o_made.at(h, 17))
                act.wait_ge(rg_scanned.sem, rg_scanned.at(h, 6))
                act.activation(RA[:, 0:TOK], vT[:, 0:TOK], ACT.Square).then_inc(o_squared.sem, 1)
                act.wait_ge(o_meaned.sem, o_meaned.at(h, 1))
                act.activation(hcc["rstd"], hcc["rstd"], ACT.Sqrt).then_inc(o_rooted.sem, 1)
                act.wait_ge(oz_made.sem, oz_made.at(h, 4))
                act.wait_ge(oz_stored.sem, oz_stored.at(h, 1) * 16)
                act.wait_ge(rg_stored.sem, rg_stored.at(h, 2) * 16)

            with act.Fori(0, HEADS - 1) as h:
                head(h)
            head(HEADS - 1, last=True)

            def y_tile(buf, n):
                act.wait_ge(y_done, n + 1)
                for half in range(2):
                    if not (isinstance(n, int) and n == 0 and half == 0):
                        act.wait_ge(y_squared, 2 * n + half)
                    act.activation(y_junk[:, 512 * half:512 * half + 512], banks[2 * buf + half][:, :], ACT.Square,
                                   accum_out=y_ss[:, 4 * buf + half:4 * buf + half + 1]).then_inc(y_squared, 1)
                act.wait_ge(y_meaned, n + 1)
                act.activation(y_ss[:, 4 * buf + 2:4 * buf + 3], y_ss[:, 4 * buf + 2:4 * buf + 3], ACT.Sqrt)\
                   .then_inc(y_rooted, 1)

            y_tile(0, 0)
            y_tile(1, 1)
            with act.Fori(0, 3) as i:
                y_tile(0, 2 * i + 2)
                y_tile(1, 2 * i + 3)
            y_tile(0, 8)

        @block.vector
        def _(dve):
            own = Chain(dve, v_own)
            dve.wait_ge(cols_turned, 2)
            dve.tensor_copy(colsA, banks[6][:, 0:P]).then_inc(cols_made, 1)
            dve.tensor_copy(colsB[:, 0:B_ROWS], banks[7][:, 0:B_ROWS]).then_inc(cols_made, 1)
            dve.wait_ge(c_tanh, 1)
            c_cols = colsB[:, 0:16].rearrange("p (s k) -> p s k", s=2)
            own(dve.scalar_tensor_tensor(silu_c, silu_c, 1.0, c_cols, ALU.add, ALU.mult))
            dve.tensor_scalar(silu_c, silu_c, 0.5, None, ALU.mult).then_inc(silu_c_made, 1)
            own(dve.tensor_scalar(colsA[:, 0:96], colsA[:, 0:96], 0.5, None, ALU.mult))
            own(dve.tensor_scalar(hc[:, 180:212], colsB[:, B_BR:B_BR + 32], 0.5, None, ALU.mult))
            id4 = ident.rearrange("p (q m) -> p q m", q=4)
            for to, first in ((pf, 0), (pb, NCH)):
                own(dve.tensor_reduce(to, id4[:, :, first:first + NCH], AX.XY, ALU.add))
                own(dve.tensor_scalar(to, to, -1.0, None, ALU.mult))
            dve.wait_ge(consts_in, 112)
            dve.wait_ge(ada_done, 6)
            for n in range(6):
                dve.tensor_tensor(mod_row[0:2, 512 * n:512 * n + 512], banks[n][0:2, :],
                                  ada_brow[0:2, 512 * n:512 * n + 512], ALU.add).then_inc(mod_row_made, 1)
            dve.wait_ge(mod_turned, 1)
            m_ps = banks[6][:, 0:32].rearrange("p (m s) -> p s m", s=2)
            for s in range(2):
                dve.scalar_tensor_tensor(mod_ab[:, s], m_ps[:, s, 8:16], 1.0, colsB[:, B_PRE:B_PRE + 8],
                                         ALU.add, ALU.mult).then_inc(mod_made, 1)
            dve.tensor_copy(mod_ab[:, 2:4], m_ps[:, :, 0:8]).then_inc(mod_made, 1)
            dve.wait_ge(mod_made, 3)

            def x_tile(buf, n, loaded):
                prompt = isinstance(n, int) and n == 0
                dve.wait_ge(x_loaded[buf], loaded)
                if not prompt:
                    dve.tensor_tensor(x_in[:, buf], x_in[:, buf], pos[:, buf], ALU.add).then_inc(x_added, 1)
                dve.wait_ge(x_squared, n + 1)
                dve.tensor_scalar(x_ss[:, buf:buf + 1], x_ss[:, buf:buf + 1], 1.0 / D, EPS, ALU.mult, ALU.add)\
                   .then_inc(x_meaned, 1)
                dve.wait_ge(x_rooted, n + 1)
                own(dve.reciprocal(x_ss[:, buf:buf + 1], x_ss[:, buf:buf + 1]))
                dve.tensor_scalar(x_in[:, buf], x_in[:, buf], x_ss[:, buf:buf + 1], None, ALU.mult).then_inc(x_normed, 1)
                dve.wait_ge(x_turned, 2 * n + 1)
                s = 0 if prompt else 1
                first = 0 if prompt else GAP + P * n
                for k in range(4):
                    dve.tensor_scalar(hT[:, k, bd(first, P)], banks[2 * buf][:, P * k:P * k + P], mod_ab[:, s, k:k + 1],
                                      mod_ab[:, 2 + s, k:k + 1], ALU.mult, ALU.add).then_inc(h_made_v, 1)

            x_tile(0, 0, 16)
            x_tile(1, 1, 48)
            own.clear()
            with dve.Fori(0, 3) as i:
                x_tile(0, 2 * i + 2, 48 * i + 64)
                x_tile(1, 2 * i + 3, 48 * i + 96)
                own.clear()
            x_tile(0, 8, 16 + 48 * 4)
            dve.wait_ge(ba_done, 1)
            for g, (o, n) in enumerate(GROUPS):
                dve.tensor_copy(baT[0:32, o:o + n], banks[5 + g][0:32, 0:n]).then_inc(baT_made, 1)
            dve.tensor_scalar(sp_y[:, NCH * 16:], colsB[:, B_LAM:B_LAM + 16], -1.0, None, ALU.mult).then_inc(sp_ready, 1)
            dve.wait_ge(ba_turned, 1)
            dve.tensor_copy(ba, banks[2][:, 0:NCH * 32].rearrange("p (c n) -> p c n", n=32)).then_inc(ba_made, 1)
            dve.wait_ge(ba_made, 1)
            by_tok = lambda a: a[:, 0:NCH * 16].rearrange("p (c n) -> p c n", n=16)
            dve.tensor_tensor(by_tok(sp_y), ba[:, :, 16:32], dt_bias.unsqueeze(1).to_broadcast([P, NCH, 16]), ALU.add)\
               .then_inc(sp_ready, 1)
            dve.wait_ge(sp_exped, 3)
            own(dve.tensor_scalar(sp_z, sp_e, 2.0, None, ALU.add))
            own(dve.reciprocal(sp_z, sp_z))
            own(dve.tensor_tensor(sp_z, sp_z, sp_e, ALU.mult))
            own(dve.tensor_tensor(sp_z2, sp_z, sp_z, ALU.mult))
            own(dve.tensor_scalar(sp_p, sp_z2, 1.0 / 15, None, ALU.mult))
            for n in (13, 11, 9, 7, 5, 3):
                own(dve.scalar_tensor_tensor(sp_p, sp_p, 1.0 / n, sp_z2, ALU.add, ALU.mult))
            own(dve.scalar_tensor_tensor(sp_p, sp_p, 1.0, sp_z, ALU.add, ALU.mult))
            own(dve.tensor_scalar(sp_r, sp_y, 0.0, None, ALU.max))
            own(dve.scalar_tensor_tensor(sp_r, sp_p, 2.0, sp_r, ALU.mult, ALU.add))
            dve.scalar_tensor_tensor(by_tok(sp_e), by_tok(sp_r), -1.0, a_log.unsqueeze(1).to_broadcast([P, NCH, 16]),
                                     ALU.mult, ALU.mult).then_inc(g_made, 1)
            own(dve.tensor_scalar(hc[:, 212:228], sp_r[:, NCH * 16:], -4.0, None, ALU.mult))
            own(dve.tensor_scalar(hc[:, 228:244], sp_r[:, NCH * 16:], 4.0, None, ALU.mult))
            own(dve.tensor_scalar(cols["beta"], cols["beta"], 1.0, None, ALU.add))
            own(dve.reciprocal(cols["beta"], cols["beta"]))
            dve.wait_ge(G_summed, 3)
            dve.tensor_copy(cols["cum"], by_tok(banks[3])).then_inc(G_taken, 1)
            dve.tensor_copy(cols["tot"], by_tok(banks[4])).then_inc(G_taken, 1)
            dve.wait_ge(G_taken, 2)
            dve.tensor_tensor(cols["edec"], cols["tot"], cols["cum"], ALU.subtract).then_inc(G_exp_in, 1)
            for d in range(DIRS):
                for b in range(3):
                    dve.wait_ge(Grow_done, 3 * d + b + 1)
                    n = min(4 * P, TOK - 4 * P * b)
                    dve.tensor_copy(G_rows[0:HEADS, d, 4 * P * b:4 * P * b + n], banks[(5, 2)[d] + b][0:HEADS, 0:n])\
                       .then_inc(G_taken, 1)
            dve.wait_ge(G_exped, 3)
            dve.tensor_scalar(cols["eG"], cols["eG"], -1.0, None, ALU.mult).then_inc(cols_ready, 1)
            dve.wait_ge(grounds_made, 1)
            dve.wait_ge(G_stored, 32)
            dve.wait_ge(gate_stored, 16)
            dve.wait_ge(cols_ready, 1)
            own.clear()

            chv = {n: cols[n].rearrange("p c (d h) -> p h d c", d=2) for n in ("beta", "edec")}
            dview = decay.rearrange("p (d c) i -> p d c i", d=2)
            nview = nmat.rearrange("p (d c) i -> p d c i", d=2)
            X = sub[1].rearrange("p (a b) -> p a b", b=BLK)
            by_d = lambda a: a[:, 0:TOK].rearrange("p (c d) -> p c d", d=P)
            prompt, sample = slice(0, P), slice(P + GAP, TW)
            runs = [(0, 0, P), (P, P + GAP, TOK - P)]

            def head(h, last=False):
                def conv(j, dest):
                    dve.wait_ge(proj_taken.sem, proj_taken.at(h, 3 * (j + 1) - 12))
                    tap = lambda t: (rconvw[:, t, bd(h, 1)] if j == 3 else convw[:, t, bd(h + (8, 0, 16)[j], 1)])
                    if j == 3:
                        own(dve.tensor_scalar(dest, raw[:, j, 0:TW], tap(0), colsB[:, bd(B_CB + h, 1)], ALU.mult, ALU.add))
                    else:
                        own(dve.tensor_scalar(dest, raw[:, j, 0:TW], tap(0), None, ALU.mult))
                    for t in range(1, 4):
                        step = dve.scalar_tensor_tensor(dest, raw[:, j, t:t + TW], tap(t), dest, ALU.mult, ALU.add)
                        if t < 3:
                            own(step)
                    step.then_inc(conv_done.sem, 1)

                def silu(n, t, x):
                    dve.wait_ge(tanh_done.sem, tanh_done.at(h, n))
                    dve.scalar_tensor_tensor(x, t, 1.0, x, ALU.add, ALU.mult).then_inc(silu_done.sem, 1)

                conv(0, kT)
                conv(1, qT)
                silu(1, RA, kT)
                conv(2, vT)
                silu(2, RB, qT)
                conv(3, xf)
                silu(3, RC, vT)
                silu(4, RH, sz)
                silu(5, RA, sg)
                dve.wait_ge(sq_k_done.sem, sq_k_done.at(h, 1))
                dve.wait_ge(head_cols_made.sem, head_cols_made.at(h, 4))
                own(dve.tensor_reduce(hcc["ssk"], by_d(RB), AX.X, ALU.add))
                own(dve.tensor_scalar(hcc["ssk"], hcc["ssk"], EPS, None, ALU.add))
                own(dve.reciprocal(hcc["rk2"], hcc["ssk"]))
                own(dve.tensor_tensor(hcv["Pk"], chv["beta"][:, bd(h, 1)].rearrange("p a d c -> p (a d) c"),
                                      hcc["rk2"].unsqueeze(1).to_broadcast([P, DIRS, NCH]), ALU.mult))
                dve.tensor_tensor(hcv["Pdec"], hcv["Pk"], chv["edec"][:, bd(h, 1)].rearrange("p a d c -> p (a d) c"),
                                  ALU.mult).then_inc(ss_done.sem, 1)
                dve.wait_ge(turn_taken_a.sem, turn_taken_a.at(h, 6))
                own(dve.tensor_reduce(hcc["ssq"], by_d(RC), AX.X, ALU.add))
                dve.tensor_scalar(hcc["epsq"], hcc["ssq"], P * EPS, P * EPS * EPS, ALU.mult, ALU.add)\
                   .then_inc(ss_done.sem, 1)
                for b in range(3):
                    dve.wait_ge(turned.sem, turned.at(h, 6 + b + 1))
                    dve.tensor_copy(vtok[:, 3 * b:3 * b + 3], banks[2 + b][:, 0:3 * P].rearrange("p (c d) -> p c d", d=P))\
                       .then_inc(turn_taken_v.sem, 1)
                for d in range(DIRS):
                    dve.wait_ge(rg_t_made.sem, rg_t_made.at(h, 3 * d + 3))
                    dve.scalar_tensor_tensor(RB, RC, 1.0, RB, ALU.add, ALU.mult).then_inc(rg_u_made.sem, 1)
                    dve.wait_ge(gate_tanh.sem, gate_tanh.at(h, 6 * d + 6))
                    dve.scalar_tensor_tensor(RC, RC, 1.0, xf, ALU.add, ALU.mult).then_inc(rg_ix_made.sem, 1)
                    dve.wait_ge(rg_bx_made.sem, rg_bx_made.at(h, d + 1))
                    out = RC if d else RH
                    way = (lambda a: a[:, P - 1::-1], lambda a: a[:, TW - 1:P + GAP - 1:-1]) if d else \
                        (lambda a: a[:, prompt], lambda a: a[:, sample])
                    for run, first in zip(way, (0.0, colsB[:, bd(B_ST + 8 * d + h, 1)])):
                        dve.tensor_tensor_scan(run(out), run(RA), run(RB), first, ALU.mult, ALU.add)\
                           .then_inc(rg_scanned.sem, 1)
                    dve.wait_ge(rg_scanned.sem, rg_scanned.at(h, 3 * d + 1))
                    end = 0 if d else P - 1
                    dve.tensor_copy(st_rg[:, d, bd(h, 1)], out[:, end:end + 1]).then_inc(rg_scanned.sem, 1)
                dve.wait_ge(n_scaled.sem, n_scaled.at(h, 2))
                for f in range(5):
                    dve.wait_ge(scored.sem, scored.at(h, f + 1))
                    n = 2 if f < 4 else 1
                    ps = banks[(5, 6, 7, 2, 3)[f]][:, 0:2 * P * n].rearrange("p (c j t) -> p c j t", j=2, t=P)
                    cs = slice(2 * f, 2 * f + n)
                    for d in range(DIRS):
                        dve.tensor_tensor(nview[:, d, cs], ps[:, :, 0], nview[:, d, cs], ALU.mult).then_inc(scores_taken.sem, 1)
                    for d in range(DIRS):
                        dve.tensor_tensor(dview[:, d, cs], ps[:, :, 1], dview[:, d, cs], ALU.mult).then_inc(scores_taken.sem, 1)
                dve.wait_ge(scores_taken.sem, scores_taken.at(h, 20))
                for q in range(4):
                    r = slice(BLK * q, BLK * q + BLK)
                    own.later(dve.tensor_copy(block_in[r, 0:INST, :], nmat[r, :, r]))
                own.settle()
                own(dve.transpose(sub[1].rearrange("p (c r) -> p c r", c=BLK), sub[0].rearrange("p (m c) -> p c m", c=BLK)))
                own(dve.transpose(sub[2].rearrange("p (r c) -> p c r", c=BLK), sub[0].rearrange("p (m c) -> p c m", c=BLK)))
                own(dve.tensor_scalar(sub[2], sub[2], pb, None, ALU.mult))
                own(dve.scalar_tensor_tensor(sub[1], sub[1], pf, sub[2], ALU.mult, ALU.add))
                own(dve.memset(sub[1][:, 0:SQ:BLK + 1], 1.0))
                for k in range(1, BLK - 1):
                    rows = BLK - 1 - k
                    tmp = view("sub_tmp", 0, rows * k).rearrange("p (a b) -> p a b", b=k)
                    own(dve.tensor_tensor(tmp, X[:, k + 1:, k:k + 1].to_broadcast([P, rows, k]),
                                          X[:, k:k + 1, 0:k].to_broadcast([P, rows, k]), ALU.mult))
                    own(dve.tensor_tensor(X[:, k + 1:, 0:k], X[:, k + 1:, 0:k], tmp, ALU.add))
                dve.transpose(sub[2].rearrange("p (m a) -> p a m", a=BLK), X).then_inc(unblocked.sem, 1)
                dve.transpose(sub[0].rearrange("p (m b) -> p b m", b=BLK), X.rearrange("p a b -> p b a"))\
                   .then_inc(unblocked.sem, 1)
                dve.wait_ge(unblocked.sem, unblocked.at(h, 2))
                for d in range(DIRS):
                    for q in range(4):
                        r = slice(BLK * q, BLK * q + BLK)
                        dve.tensor_copy(Z[r, NCH * d:NCH * d + NCH, r], (block_in if d else block_T)[r, NCH * d:NCH * d + NCH, :])\
                           .then_inc(Z_placed.sem, 1)
                for g in range(6):
                    dve.wait_ge(Q_done.sem, Q_done.at(h, g + 1))
                    if g >= 2:
                        dve.wait_ge(dZ_done.sem, dZ_done.at(h, g - 1))
                    ps = banks[2 + 3 * (g % 2)][:, 0:3 * P].rearrange("p (m i) -> p m i", i=P)
                    dve.tensor_tensor(Qb[:, g % 2], ps, mask32[:, g // 3].unsqueeze(1).to_broadcast([P, 3, P]), ALU.mult)\
                       .then_inc(Q_taken.sem, 1)
                for g in range(6):
                    dve.wait_ge(Q_done.sem, Q_done.at(h, 6 + g + 1))
                    dve.wait_ge(dZ_done.sem, dZ_done.at(h, 6 + g - 1))
                    ps = banks[2 + 3 * (g % 2)][:, 0:3 * P].rearrange("p (m i) -> p m i", i=P)
                    r = slice(64, P) if g < 3 else slice(0, 64)
                    dve.tensor_scalar(Qb[r, g % 2], ps[r], -1.0, None, ALU.mult).then_inc(Q_taken.sem, 1)
                dve.wait_ge(v_scaled.sem, v_scaled.at(h, 1))
                for step in range(NCH):
                    chunk = (step, step if step == 0 else NCH - step)
                    if step:
                        for d in range(DIRS):
                            dve.wait_ge(KS_done.sem, KS_done.at(h, 2 * step - 2 + d + 1))
                            c1 = slice(chunk[d], chunk[d] + 1)
                            dve.scalar_tensor_tensor(rhs_v[:, d], banks[2 + d][:, 0:P], hcv["negeG"][:, d, c1],
                                                     vtok[:, chunk[d]], ALU.mult, ALU.add).then_inc(rhs_made.sem, 1)
                    if step == 0:
                        dve.wait_ge(stepped.sem, stepped.at(h, 2))
                        for d in range(DIRS):
                            dve.tensor_copy(S_new[:, d], banks[4 + d][:, 0:P]).then_inc(S_made.sem, 1)
                        dve.tensor_copy(o_tok[:, 0], banks[5][:, P:2 * P]).then_inc(o_made.sem, 1)
                        continue
                    for d in range(DIRS):
                        ch = chunk[d]
                        dve.wait_ge(stepped.sem, stepped.at(h, 2 * step + d + 1))
                        if step < NCH - 1:
                            if step == 1:
                                dve.wait_ge(S_in.sem, S_in.at(h, 0) * 16)
                            else:
                                dve.wait_ge(S_made.sem, S_made.at(h, 2 * step - 2 + d + 1))
                            dve.scalar_tensor_tensor(S[:, d], S[:, d], hcv["gl"][:, d, ch:ch + 1], banks[4 + d][:, 0:P],
                                                     ALU.mult, ALU.add).then_inc(S_made.sem, 1)
                        if step <= 4:
                            dve.tensor_copy(o_tok[:, ch], banks[4 + d][:, P:2 * P]).then_inc(o_made.sem, 1)
                        else:
                            dve.wait_ge(o_made.sem, o_made.at(h, 2 * step - 1))
                            dve.tensor_tensor(o_tok[:, ch], banks[4 + d][:, P:2 * P], o_tok[:, ch], ALU.add)\
                               .then_inc(o_made.sem, 1)
                dve.wait_ge(o_squared.sem, o_squared.at(h, 1))
                own(dve.tensor_reduce(hcc["sso"], by_d(RA), AX.X, ALU.add))
                dve.scalar_tensor_tensor(hcc["rstd"], hcc["sso"], 1.0 / P, hcc["epsq"], ALU.mult, ALU.add)\
                   .then_inc(o_meaned.sem, 1)
                dve.wait_ge(o_rooted.sem, o_rooted.at(h, 1))
                own(dve.reciprocal(hcc["rstd"], hcc["rstd"]))
                dve.tensor_tensor(o_tok, o_tok, hcc["rstd"].unsqueeze(2).to_broadcast([P, NCH, P]), ALU.mult)\
                   .then_inc(o_normed.sem, 1)
                for b, bank, a, to, z0, n in ((0, 6, 0, 0, 0, P), (0, 6, P, P, P + GAP, 2 * P),
                                              (1, 7, 0, 3 * P, 3 * P + GAP, 3 * P), (2, 2, 0, 6 * P, 6 * P + GAP, 3 * P)):
                    dve.wait_ge(o_turned.sem, o_turned.at(h, b + 1))
                    dve.scalar_tensor_tensor(qd[:, 0, to:to + n], banks[bank][:, a:a + n], colsB[:, B_NW:B_NW + 1],
                                             sz[:, z0:z0 + n], ALU.mult, ALU.mult).then_inc(oz_made.sem, 1)
                own.clear()
                dve.wait_ge(prompt_S_stored.sem, prompt_S_stored.at(h, 1) * 16)

            with dve.Fori(0, HEADS - 1) as h:
                head(h)
            head(HEADS - 1, last=True)
            dve.wait_ge(states_turned, 1)
            dve.tensor_copy(hc[0:16, 0:P], banks[7][0:16, 0:P]).then_inc(states_taken, 1)

            def y_tile(buf, n, s):
                first = isinstance(n, int) and n < 2
                ss = lambda i: y_ss[:, 4 * buf + i:4 * buf + i + 1]
                dve.wait_ge(y_squared, 2 * n + 2)
                own(dve.tensor_tensor(ss(2), ss(0), ss(1), ALU.add))
                dve.tensor_scalar(ss(2), ss(2), 1.0 / D, EPS, ALU.mult, ALU.add).then_inc(y_meaned, 1)
                dve.wait_ge(y_rooted, n + 1)
                own(dve.reciprocal(ss(3), ss(2)))
                if not first:
                    dve.wait_ge(y_stored[buf], 8 * n if buf == 0 else 8 * n - 8)
                for half in range(2):
                    cc = slice(512 * half, 512 * half + 512)
                    own.later(dve.scalar_tensor_tensor(y_out[:, buf, cc], banks[2 * buf + half][:, :], ss(3),
                                                       gate_post[:, s, cc], ALU.mult, ALU.mult))
                own.settle()
                if isinstance(n, int) and n == 0:
                    dve.wait_ge(xr_in[0], 16)
                else:
                    dve.wait_ge(xr_added, n)
                dve.tensor_tensor(y_out[:, buf], y_out[:, buf], x_res[:, buf], ALU.add).then_inc(y_made, 1)

            dve.wait_ge(gate_post_made, 2)
            y_tile(0, 0, 0)
            y_tile(1, 1, 1)
            own.clear()
            with dve.Fori(0, 3) as i:
                y_tile(0, 2 * i + 2, 1)
                y_tile(1, 2 * i + 3, 1)
                own.clear()
            y_tile(0, 8, 1)


_INS = ["x_prompt", "x_sample", "state_delta", "state_rglru", "c", "c_ctx", "ada_w", "ada_b", "pre_norm_w",
        "post_norm_w", "w_in", "w_out", "dn_conv_w", "dn_a_log", "dn_dt_bias", "dn_norm_w", "rg_conv_w", "rg_conv_b",
        "rg_w_r", "rg_b_r", "rg_w_i", "rg_b_i", "rg_lam"]
_OUTS = [("y_prompt", (1, P, D)), ("y_sample", (1, TOK - P, D)), ("new_delta", (1, 1, DIRS, HEADS, P, P)),
         ("new_rglru", (1, 1, DIRS, D))]


def positions():
    quarter, width = D // 4, 64
    freqs = np.exp(np.float32(-math.log(10000.0)) * np.arange(quarter, dtype=np.float32) / np.float32(quarter))
    table = []
    for n in ((TOK - P) // width, width):
        angle = np.arange(n, dtype=np.float32)[:, None] * freqs[None]
        table.append(np.concatenate([np.sin(angle), np.cos(angle)], axis=1).astype(np.float32))
    return table


def build(nc):
    shapes = {
        "x_prompt": (1, P, D), "x_sample": (1, TOK - P, D), "state_delta": (1, 1, DIRS, HEADS, P, P),
        "state_rglru": (1, 1, DIRS, D), "c": (1, D), "c_ctx": (D,), "ada_w": (1, D, 3 * D), "ada_b": (1, 3 * D),
        "pre_norm_w": (1, D), "post_norm_w": (1, D), "w_in": (1, D, OFF_RG + D), "w_out": (1, 2 * D, D),
        "dn_conv_w": (1, 4, 3 * D), "dn_a_log": (1, DIRS, HEADS), "dn_dt_bias": (1, DIRS, HEADS), "dn_norm_w": (1, P),
        "rg_conv_w": (1, 4, D), "rg_conv_b": (1, D), "rg_w_r": (1, DIRS, HEADS, P, P), "rg_b_r": (1, DIRS, D),
        "rg_w_i": (1, DIRS, HEADS, P, P), "rg_b_i": (1, DIRS, D), "rg_lam": (1, DIRS, D)}
    args = [nc.dram_tensor(n, shapes[n], F32, kind="ExternalInput").ap() for n in _INS]
    args += [nc.dram_tensor(n, s, F32, kind="ExternalInput").ap() for n, s in (("pos_row", (16, 512)), ("pos_col", (64, 512)))]
    args += [nc.dram_tensor(n, s, F32, kind="ExternalOutput").ap() for n, s in _OUTS]
    hybrid_layer(nc, *args)


def kernel(**inputs):
    import concourse.bacc as bacc
    from concourse.bass_utils import run_bass_kernel_spmd

    nc = bacc.Bacc("TRN2", target_bir_lowering=False, num_devices=1)
    arrays = {n: np.ascontiguousarray(inputs[n]) for n in _INS}
    arrays["pos_row"], arrays["pos_col"] = positions()
    build(nc)
    got = run_bass_kernel_spmd(nc, [arrays], core_ids=[0]).results[0]
    return tuple(got[n] for n, _ in _OUTS)
```

```python
import math
from contextlib import ExitStack

import numpy as np

import concourse.bass as bass
from concourse import mybir

ALU = mybir.AluOpType
ACT = mybir.ActivationFunctionType
AX = mybir.AxisListType
F32 = mybir.dt.float32

P = 128
D = 1024
KT = D // P
HEADS = 8
NCH = 9
TOK = NCH * P
GAP = 2
TW = TOK + GAP
RAW = 2 + TW + 1
GROUPS = [(0, 386), (386, 384), (770, 384)]
DIRS = 2
INST = DIRS * NCH
OFF_B = 4 * D
OFF_RX = OFF_B + 4 * HEADS
OFF_RG = OFF_RX + D
EPS = 1e-6
MASKED = -1e30
BLK = 32
SQ = BLK * BLK


LEVEL_FILLS = [3] * 6 + [3, 3, 2, 2, 2, 2]
SCAN_FILLS = [4, 4, 4, 5, 4, 4, 4, 5, 4]
assert 64 + sum(LEVEL_FILLS) + sum(SCAN_FILLS) + 10 == 6 * 3 * KT


def col(c):
    return 0 if c == 0 else GAP + P * c


class Count:

    def __init__(self, sem, before, per_head):
        self.sem, self.before, self.per_head = sem, before, per_head

    def at(self, head, n):
        return head * self.per_head + (self.before + n)


class Chain:

    def __init__(self, engine, sem):
        self.engine, self.sem, self.n = engine, sem, 0

    def __call__(self, instruction):
        self.later(instruction)
        self.settle()

    def later(self, instruction):
        instruction.then_inc(self.sem, 1)
        self.n += 1

    def settle(self):
        self.engine.wait_ge(self.sem, self.n)

    def clear(self):
        self.settle()
        self.engine.sem_clear(self.sem)
        self.n = 0


def hybrid_layer(nc, x_prompt, x_sample, state_delta, state_rglru, c, c_ctx, ada_w, ada_b, pre_norm_w,
                 post_norm_w, w_in, w_out, dn_conv_w, dn_a_log, dn_dt_bias, dn_norm_w, rg_conv_w, rg_conv_b,
                 rg_w_r, rg_b_r, rg_w_i, rg_b_i, rg_lam, pos_row, pos_col,
                 y_prompt, y_sample, new_delta, new_rglru):
    ctx = ExitStack()
    with ctx:
        def sem(name):
            return ctx.enter_context(nc.semaphore(name))

        sizes = {
            "hT": KT * TW, "w": 3 * KT * P, "raw": 4 * RAW, "kq": 2 * TW, "vT": TW, "xf": TW, "decay": 2 * TOK,
            "nmat": 2 * TOK, "ktok": TOK, "vtok": TW, "sub": 3 * SQ, "sub_tmp": 256, "Z": INST * P,
            "Q": 2 * 3 * P, "qd": 2 * TOK, "Zt": INST * P, "sz": TW, "sg": TW, "rg": 4 * TW,
            "scan_tmp": 6 * P, "S": 2 * P, "S_new": 2 * P, "wg": 4 * P, "ident": P, "tri": 2 * P, "ones": P,
            "mask32": 2 * P, "colsA": P, "colsB": P, "ba": NCH * 32, "cum": NCH * 16, "tot": NCH * 16,
            "beta": NCH * 16, "eG": NCH * 16, "edec": NCH * 16, "gl": NCH * 16, "head_cols": 16 * 20,
            "small": 96,
        }
        total = sum(sizes.values())
        arena = ctx.enter_context(nc.sbuf_tensor("arena", [P, total], F32))
        at, off = {}, 0
        for name, n in sizes.items():
            at[name] = off
            off += n

        def view(name, start=0, n=None):
            n = sizes[name] - start if n is None else n
            return arena[:, at[name] + start:at[name] + start + n]

        hT = view("hT").rearrange("p (k t) -> p k t", k=KT)
        w_ring = view("w").rearrange("p (s k n) -> p s k n", s=3, k=KT)
        raw = view("raw").rearrange("p (j t) -> p j t", j=4)
        kq = view("kq").rearrange("p (j t) -> p j t", j=2)
        kT, qT = kq[:, 0], kq[:, 1]
        vT = view("vT")
        xf = view("xf")
        decay = view("decay").rearrange("p (m i) -> p m i", i=P)
        nmat = view("nmat").rearrange("p (m i) -> p m i", i=P)
        ktok = view("ktok").rearrange("p (c d) -> p c d", d=P)
        vtok = view("vtok", 0, TOK).rearrange("p (c d) -> p c d", d=P)
        sub = [view("sub", i * SQ, SQ) for i in range(3)]
        block_in, block_T = (s.rearrange("p (m c) -> p m c", c=BLK) for s in (sub[0], sub[2]))
        Z = view("Z").rearrange("p (m i) -> p m i", i=P)
        Zt = view("Zt").rearrange("p (m i) -> p m i", i=P)
        Qb = view("Q").rearrange("p (b m i) -> p b m i", b=2, i=P)
        qd = view("qd").rearrange("p (d t) -> p d t", d=2)
        sz, sg = view("sz"), view("sg")
        eG_rows = view("sub", 0, 2 * TOK).rearrange("p (d t) -> p d t", d=2)
        tanh_v = view("vtok")
        tanh_z, tanh_g = view("sub", 0, TW), view("sub", TW, TW)
        RA, RB, RC, RH = (view("rg", i * TW, TW) for i in range(4))
        rhs_v = view("scan_tmp", 0, 2 * P).rearrange("p (d v) -> p d v", d=2)
        vt = view("scan_tmp", 2 * P, 2 * P).rearrange("p (d v) -> p d v", d=2)
        vd = view("scan_tmp", 4 * P, 2 * P).rearrange("p (d v) -> p d v", d=2)
        S = view("S").rearrange("p (d v) -> p d v", d=2)
        S_new = view("S_new").rearrange("p (d v) -> p d v", d=2)
        wg = view("wg").rearrange("p (n j) -> p n j", n=4)
        ident, ones = view("ident"), view("ones")
        tri = view("tri").rearrange("p (d i) -> p d i", d=2)
        mask32 = view("mask32").rearrange("p (d i) -> p d i", d=2)
        colsA, colsB = view("colsA"), view("colsB")
        ba = view("ba").rearrange("p (c n) -> p c n", n=32)
        cols = {n: view(n).rearrange("p (c n) -> p c n", n=16) for n in ("cum", "tot", "beta", "eG", "edec", "gl")}
        o_tok = vT[:, 0:TOK].rearrange("p (c d) -> p c d", d=P)
        hc = view("head_cols")
        small = view("small")
        oz = view("Zt", 0, TOK)
        hcv = {n: hc[:, i * 20:i * 20 + INST].rearrange("p (d c) -> p d c", d=2)
               for i, n in enumerate(("ncum", "negeG", "Pk", "Pdec", "gl"))}
        hcc = {n: hc[:, 100 + i * 10:100 + i * 10 + NCH]
               for i, n in enumerate(("ssk", "ssq", "rk2", "rkinv", "sso", "rstd", "epsq"))}
        half_b = hc[:, 180:212].rearrange("p (n b) -> p n b", b=8)
        c8 = hc[:, 212:228].rearrange("p (d b) -> p d b", b=8)
        nc8 = hc[:, 228:244].rearrange("p (d b) -> p d b", b=8)
        st_rg = hc[:, 244:260].rearrange("p (d b) -> p d b", b=8)
        rg_tab = hc[:, 180:244].rearrange("p (n b) -> p n b", b=8)
        rg_cols = hc[:, 262:270]
        clear_mark = hc[:, 270:271]
        br_h, bi_h, c8_h, nc8_h = (rg_cols[:, 2 * i:2 * i + 2] for i in range(4))
        pf, pb = hc[:, 260:261], hc[:, 261:262]
        convw = colsA[:, 0:96].rearrange("p (j t) -> p j t", j=4)
        rconvw = colsA[:, 96:128].rearrange("p (j t) -> p j t", j=4)
        B_C, B_PRE, B_CB, B_BR, B_BI, B_LAM, B_ST, B_NW, B_ROWS = 0, 16, 24, 32, 48, 64, 80, 96, 97

        base = [at["raw"]]

        def early(n):
            base[0] += n
            return arena[:, base[0] - n:base[0]]

        adaw = early(KT * 3 * D).rearrange("p (k n) -> p k n", k=KT)
        mod_row, ada_brow = early(3 * D), early(3 * D)
        x_in = early(2 * D).rearrange("p (b n) -> p b n", b=2)
        pos = early(2 * D).rearrange("p (b n) -> p b n", b=2)
        rowsA, rowsB = early(P), early(P)
        assert base[0] <= at["wg"]
        square_out = view("w", KT * P, KT * P)
        base[0] = at["kq"]
        baT, G_rows = early(TW), early(2 * TOK).rearrange("p (d t) -> p d t", d=2)
        N_SP = NCH * 16 + 16
        sp_y, sp_e, sp_z, sp_z2, sp_p, sp_r = (early(N_SP) for _ in range(6))
        dt_bias, a_log = small[:, 56:72], small[:, 72:88]
        mod_ab = small[:, 0:32].rearrange("p (s k) -> p s k", s=4)
        silu_c = small[:, 32:48].rearrange("p (s k) -> p s k", s=2)
        x_ss = small[:, 48:50]

        banks = [ctx.enter_context(nc.psum_tensor(f"bank{i}", [P, 512], F32)) for i in range(8)]
        scr_G = nc.dram_tensor("scr_G", (DIRS, HEADS, TOK), F32, kind="Internal").ap()
        scr_o = nc.dram_tensor("scr_o", (2 * HEADS, P, TOK), F32, kind="Internal").ap()
        scr_gate = nc.dram_tensor("scr_gate", (2, D), F32, kind="Internal").ap()

        rows_in, consts_in, ba_w_in = sem("rows_in"), sem("consts_in"), sem("ba_w_in")
        ada_in = [sem(f"ada_in{k}") for k in range(KT)]
        ident_made, consts_made = sem("ident_made"), sem("consts_made")
        cols_turned, cols_made, silu_c_made = sem("cols_turned"), sem("cols_made"), sem("silu_c_made")
        ada_done, mod_row_made, mod_turned, mod_made = sem("ada_done"), sem("mod_row_made"), sem("mod_turned"), sem("mod_made")
        gate_stored = sem("gate_stored")
        x_loaded = [sem("x_loaded0"), sem("x_loaded1")]
        x_added, x_squared, x_meaned, x_rooted = sem("x_added"), sem("x_squared"), sem("x_meaned"), sem("x_rooted")
        x_normed, x_turned, h_made_v, h_made_a = sem("x_normed"), sem("x_turned"), sem("h_made_v"), sem("h_made_a")
        ba_done, baT_made, ba_turned, ba_made = sem("ba_done"), sem("baT_made"), sem("ba_turned"), sem("ba_made")
        sp_ready, sp_exped, g_made, G_summed, G_taken = sem("sp_ready"), sem("sp_exped"), sem("g_made"), sem("G_summed"), sem("G_taken")
        G_exp_in, G_exped, Grow_done, Grow_made, G_stored = sem("G_exp_in"), sem("G_exped"), sem("Grow_done"), sem("Grow_made"), sem("G_stored")
        grounds_made, c_tanh, cols_ready = sem("grounds_made"), sem("c_tanh"), sem("cols_ready")
        Zt_cleared = Count(sem("Zt_cleared"), 1, 1)
        v_own, a_own, g_own = sem("v_own"), sem("a_own"), sem("g_own")

        w_in_slot = [Count(sem("w_slot0"), 1, 2), Count(sem("w_slot1"), 1, 2), Count(sem("w_slot2"), 2, 2)]
        projected = Count(sem("projected"), 12, 18)
        proj_taken = Count(sem("proj_taken"), 12, 18)
        conv_done = Count(sem("conv_done"), 3, 4)
        tanh_done = Count(sem("tanh_done"), 2, 5)
        silu_done = Count(sem("silu_done"), 2, 5)
        turned = Count(sem("turned"), 3, 9)
        turn_taken_a = Count(sem("turn_taken_a"), 0, 21)
        turn_taken_v = Count(sem("turn_taken_v"), 0, 3)
        ss_done = Count(sem("ss_done"), 0, 2)
        rk_root = Count(sem("rk_root"), 0, 1)
        v_scaled = Count(sem("v_scaled"), 0, 1)
        decay_in = Count(sem("decay_in"), 2, 2)
        S_in = Count(sem("S_in"), 2, 2)
        wg_in = Count(sem("wg_in"), 4, 4)
        eG_row = Count(sem("eG_row"), 1, 1)
        head_cols_made = Count(sem("head_cols_made"), 4, 4)
        masked = Count(sem("masked"), 2, 2)
        decay_exped = Count(sem("decay_exped"), 0, INST)
        qd_made = Count(sem("qd_made"), 0, 4)
        gated = Count(sem("gated"), 0, 12)
        gate_tanh = Count(sem("gate_tanh"), 0, 12)
        rg_t_made = Count(sem("rg_t_made"), 0, 6)
        rg_u_made = Count(sem("rg_u_made"), 0, 2)
        rg_root = Count(sem("rg_root"), 0, 2)
        rg_ix_made = Count(sem("rg_ix_made"), 0, 2)
        rg_bx_made = Count(sem("rg_bx_made"), 0, 2)
        rg_scanned = Count(sem("rg_scanned"), 0, 6)
        rg_stored = Count(sem("rg_stored"), 0, 2)
        scored = Count(sem("scored"), 0, 5)
        scores_taken = Count(sem("scores_taken"), 0, 28)
        unblocked = Count(sem("unblocked"), 0, 2)
        Z_placed = Count(sem("Z_placed"), 0, 8)
        Zt_placed = Count(sem("Zt_placed"), 0, 8)
        Q_done = Count(sem("Q_done"), 0, 12)
        Q_taken = Count(sem("Q_taken"), 0, 12)
        dZ_done = Count(sem("dZ_done"), 0, 12)
        dZ_taken = Count(sem("dZ_taken"), 0, 30)
        KS_done = Count(sem("KS_done"), 0, 16)
        rhs_made = Count(sem("rhs_made"), 0, 16)
        solved = Count(sem("solved"), 0, 18)
        vnew_made = Count(sem("vnew_made"), 0, 36)
        stepped = Count(sem("stepped"), 0, 18)
        S_made = Count(sem("S_made"), 0, 16)
        o_made = Count(sem("o_made"), 0, 17)
        prompt_S_stored = Count(sem("prompt_S_stored"), 0, 1)
        o_squared = Count(sem("o_squared"), 0, NCH)
        o_meaned = Count(sem("o_meaned"), 0, 1)
        o_rooted = Count(sem("o_rooted"), 0, 1)
        o_normed = Count(sem("o_normed"), 0, 1)
        o_turned = Count(sem("o_turned"), 0, 3)
        oz_made = Count(sem("oz_made"), 1, 4)
        oz_stored = Count(sem("oz_stored"), 0, 1)
        w_out_in = [sem(f"w_out_in{i}") for i in range(4)]
        post_in, gate_post_made, states_stored = sem("post_in"), sem("gate_post_made"), sem("states_stored")
        states_turned, states_taken = sem("states_turned"), sem("states_taken")
        ot_in = [sem("ot_in0"), sem("ot_in1")]
        xr_in = [sem("xr_in0"), sem("xr_in1")]
        xr_added, y_done, y_squared, y_meaned, y_rooted, y_made, raw_cleared = (
            sem(n) for n in ("xr_added", "y_done", "y_squared", "y_meaned", "y_rooted", "y_made", "raw_cleared"))
        y_stored = [sem("y_stored0"), sem("y_stored1")]

        wo = arena[:, 0:2 * HEADS * D].rearrange("p (k n) -> p k n", n=D)
        assert 2 * HEADS * D <= at["kq"]
        ot = arena[:, at["decay"]:at["decay"] + 2 * 16 * P].rearrange("p (b k t) -> p b k t", b=2, k=16)
        base[0] = at["ktok"]
        x_res = early(2 * D).rearrange("p (b n) -> p b n", b=2)
        pos_res = early(2 * D).rearrange("p (b n) -> p b n", b=2)
        y_out = early(2 * D).rearrange("p (b n) -> p b n", b=2)
        gate_post = early(2 * D).rearrange("p (b n) -> p b n", b=2)
        post_b = early(D)
        y_junk = early(D)
        assert base[0] <= at["Zt"]
        y_ss = small[:, 0:8]

        SECTION = {"z": 3 * D, "gate": OFF_RG, "k": D, "q": 0, "v": 2 * D, "rx": OFF_RX}
        TILES = ["z", "gate", "k", "q", "rx", "v"]
        w_in2, w_out2 = w_in[0], w_out[0]
        bd = bass.ds

        def w_tile(name, head):
            return w_in2[:, bd(P * (head + SECTION[name] // P) + SECTION[name] % P, P)].rearrange("(k p) n -> p k n", p=P)

        block = ctx.enter_context(nc.Block())

        @block.sync
        def _(sp):
            sp.dma_start(rowsA[0:96, :], dn_conv_w[0].rearrange("j (t p) -> (j t) p", p=P)).then_inc(rows_in, 16)
            sp.dma_start(rowsA[96:128, :], rg_conv_w[0].rearrange("j (t p) -> (j t) p", p=P)).then_inc(rows_in, 16)
            for first, src in ((B_C, c_ctx.rearrange("(k p) -> k p", p=P)), (B_C + 8, c[0].rearrange("(k p) -> k p", p=P)),
                               (B_PRE, pre_norm_w[0].rearrange("(k p) -> k p", p=P)),
                               (B_CB, rg_conv_b[0].rearrange("(k p) -> k p", p=P)),
                               (B_BR, rg_b_r[0].rearrange("d (k p) -> (d k) p", p=P)),
                               (B_BI, rg_b_i[0].rearrange("d (k p) -> (d k) p", p=P)),
                               (B_LAM, rg_lam[0].rearrange("d (k p) -> (d k) p", p=P)),
                               (B_ST, state_rglru[0, 0].rearrange("d (k p) -> (d k) p", p=P)),
                               (B_NW, dn_norm_w)):
                sp.dma_start(rowsB[first:first + src.shape[0], :], src).then_inc(rows_in, 16)
            for k in range(KT):
                sp.dma_start(adaw[:, k, :], ada_w[0, k * P:(k + 1) * P, :]).then_inc(ada_in[k], 16)
            sp.dma_start(ada_brow[0:2, :], ada_b.to_broadcast([2, 3 * D]))\
              .then_inc(consts_in, 16)
            sp.dma_start(dt_bias, dn_dt_bias.rearrange("l d h -> l (d h)").to_broadcast([P, 16])).then_inc(consts_in, 16)
            sp.dma_start(a_log, dn_a_log.rearrange("l d h -> l (d h)").to_broadcast([P, 16])).then_inc(consts_in, 16)
            for b in range(2):
                for half in range(2):
                    sp.dma_start(pos[64 * half:64 * half + 64, b, 512:], pos_col).then_inc(consts_in, 16)
            sp.dma_start(x_in[:, 0], x_prompt[0]).then_inc(x_loaded[0], 16)

            def load_x(buf, xs, ps, tile, s):
                sp.dma_start(xs[:, buf], x_sample[0, bd(P * tile, P), :]).then_inc(s[buf], 16)
                for half in range(2):
                    sp.dma_start(ps[64 * half:64 * half + 64, buf, 0:512],
                                 pos_row[bd(2 * tile + half, 1), :].to_broadcast([64, 512])).then_inc(s[buf], 16)

            load_x(1, x_in, pos, 0, x_loaded)
            with sp.Fori(0, 3) as i:
                sp.wait_ge(x_turned, 4 * i + 2)
                load_x(0, x_in, pos, 2 * i + 1, x_loaded)
                sp.wait_ge(x_turned, 4 * i + 4)
                load_x(1, x_in, pos, 2 * i + 2, x_loaded)
            sp.wait_ge(x_turned, 14)
            load_x(0, x_in, pos, 7, x_loaded)
            sp.dma_start(w_ring[:, 0, :, 0:32], w_in2[:, OFF_B:OFF_RX].rearrange("(k p) n -> p k n", p=P)).then_inc(ba_w_in, 16)
            sp.wait_ge(mod_row_made, 6)
            sp.dma_start(scr_gate, mod_row[0:2, 2 * D:]).then_inc(gate_stored, 16)

            def load_w(slot, name, head):
                sp.dma_start(w_ring[:, slot], w_tile(name, head)).then_inc(w_in_slot[slot].sem, 16)

            load_w(2, "k", 0)
            sp.wait_ge(x_squared, NCH)
            load_w(1, "rx", 0)
            sp.wait_ge(ba_done, 1)
            load_w(0, "q", 0)
            sp.wait_ge(projected.sem, 3)
            load_w(2, "v", 0)
            sp.wait_ge(projected.sem, 6)
            load_w(0, "z", 0)
            sp.wait_ge(projected.sem, 9)
            load_w(1, "gate", 0)

            g_rows = nmat.rearrange("p (d c) i -> p d (c i)", d=2)

            def load_rows(head):
                for d in range(DIRS):
                    sp.dma_start(g_rows[:, d], scr_G[d, bd(head, 1), :].to_broadcast([P, TOK])).then_inc(decay_in.sem, 16)

            def load_states(head):
                for d in range(DIRS):
                    sp.dma_start(S[:, d], state_delta[0, 0, d, bd(head, 1)].rearrange("a k v -> (a k) v"))\
                      .then_inc(S_in.sem, 16)

            def load_gates(head):
                for n, src in enumerate((rg_w_r[0, 0], rg_w_r[0, 1], rg_w_i[0, 0], rg_w_i[0, 1])):
                    sp.dma_start(wg[:, n], src[bd(head, 1)].rearrange("a k j -> (a k) j")).then_inc(wg_in.sem, 16)

            load_gates(0)
            for d in range(DIRS):
                sp.wait_ge(G_taken, 5 + 3 * d)
                sp.dma_start(scr_G[d], G_rows[0:HEADS, d]).then_inc(G_stored, 16)
            sp.wait_ge(G_stored, 32)
            load_rows(0)
            load_states(0)

            def head_loads(h):
                def load_tile(j):
                    sp.wait_ge(projected.sem, projected.at(h, 3 * (j if j > 1 else j + 6) - 6))
                    load_w(j % 3, TILES[j], h + 1)

                load_tile(2)
                load_tile(3)
                sp.wait_ge(gated.sem, gated.at(h, 12))
                load_gates(h + 1)
                load_tile(4)
                load_tile(5)
                sp.wait_ge(Q_done.sem, Q_done.at(h, 12))
                load_rows(h + 1)
                load_tile(0)
                load_tile(1)
                sp.wait_ge(stepped.sem, stepped.at(h, 18))
                load_states(h + 1)

            with sp.Fori(0, HEADS - 1) as h:
                head_loads(h)
            h = HEADS - 1
            sp.wait_ge(projected.sem, projected.at(h, 6))
            sp.wait_ge(conv_done.sem, conv_done.at(h, 1))
            for q in range(4):
                sp.dma_start(wo[:, 4 * q:4 * q + 4, :],
                             w_out2[512 * q:512 * q + 512, :].rearrange("(k p) n -> p k n", p=P)).then_inc(w_out_in[q], 16)
            sp.wait_ge(stepped.sem, stepped.at(h, 18))
            sp.wait_ge(o_made.sem, o_made.at(h, 17))
            sp.wait_ge(gate_stored, 16)
            for s in range(2):
                sp.dma_start(gate_post[:, s], scr_gate[s:s + 1, :].to_broadcast([P, D])).then_inc(post_in, 16)
            sp.dma_start(post_b, post_norm_w.to_broadcast([P, D])).then_inc(post_in, 16)
            for b in range(2):
                for half in range(2):
                    sp.dma_start(pos_res[64 * half:64 * half + 64, b, 512:], pos_col).then_inc(post_in, 16)
            sp.dma_start(x_res[:, 0], x_prompt[0]).then_inc(xr_in[0], 16)
            load_x(1, x_res, pos_res, 0, xr_in)
            sp.wait_ge(oz_stored.sem, 16 * oz_stored.at(h, 1))
            sp.wait_ge(rg_stored.sem, 16 * rg_stored.at(h, 2))

            def load_o(buf, tile):
                sp.dma_start(ot[:, buf], scr_o[:, :, bd(P * tile, P)].rearrange("k p t -> p k t")).then_inc(ot_in[buf], 16)

            load_o(0, 0)
            load_o(1, 1)
            sp.wait_ge(states_taken, 1)
            sp.dma_start(new_rglru[0, 0].rearrange("d (b p) -> (d b) p", p=P), hc[0:16, 0:P]).then_inc(states_stored, 16)
            sp.wait_ge(y_made, 1)
            sp.dma_start(y_prompt[0], y_out[:, 0]).then_inc(y_stored[0], 16)
            load_o(0, 2)
            load_x(0, x_res, pos_res, 1, xr_in)

            def store_y(buf, tile):
                sp.dma_start(y_sample[0, bd(P * tile, P), :], y_out[:, buf]).then_inc(y_stored[buf], 16)

            with sp.Fori(0, 3) as i:
                sp.wait_ge(y_made, 2 * i + 2)
                store_y(1, 2 * i)
                load_o(1, 2 * i + 3)
                load_x(1, x_res, pos_res, 2 * i + 2, xr_in)
                sp.wait_ge(y_made, 2 * i + 3)
                store_y(0, 2 * i + 1)
                load_o(0, 2 * i + 4)
                load_x(0, x_res, pos_res, 2 * i + 3, xr_in)
            sp.wait_ge(y_made, 8)
            store_y(1, 6)
            sp.wait_ge(y_made, 9)
            store_y(0, 7)
            sp.wait_ge(y_stored[0], 16 * 5)
            sp.wait_ge(y_stored[1], 16 * 4)
            sp.wait_ge(states_stored, 16)
            sp.wait_ge(prompt_S_stored.sem, 16 * HEADS)

        @block.gpsimd
        def _(gp):
            own = Chain(gp, g_own)
            own(gp.memset(ident, 0.0))
            own(gp.affine_select(out=ident, in_=ident, compare_op=ALU.not_equal, fill=1.0, base=0,
                                 pattern=[[-1, P]], channel_multiplier=1))
            own(gp.memset(tri, 1.0))
            own(gp.affine_select(out=tri[:, 0], in_=tri[:, 0], compare_op=ALU.is_ge, fill=0.0, base=0,
                                 pattern=[[1, P]], channel_multiplier=-1))
            own(gp.affine_select(out=tri[:, 1], in_=tri[:, 1], compare_op=ALU.is_ge, fill=0.0, base=0,
                                 pattern=[[-1, P]], channel_multiplier=1))
            own(gp.memset(ones, 1.0))
            own(gp.memset(mask32, 0.0))
            for d in range(DIRS):
                for b in (0, 2):
                    r, cc = (b + 1, b) if d == 0 else (b, b + 1)
                    own(gp.memset(mask32[BLK * r:BLK * r + BLK, d, BLK * cc:BLK * cc + BLK], -1.0))
            gp.memset(hT[:, :, P:P + GAP], 0.0).then_inc(consts_made, 1)

            gp.wait_ge(ada_done, 6)
            gp.memset(raw, 0.0).then_inc(raw_cleared, 1)
            own(gp.memset(sub[0], 0.0))
            gp.memset(Z, 0.0).then_inc(grounds_made, 1)
            gp.wait_ge(mod_turned, 1)
            gp.wait_ge(gate_stored, 16)
            gp.memset(Zt, 0.0).then_inc(Zt_cleared.sem, 1)
            gp.wait_ge(cols_ready, 1)

            dview = decay.rearrange("p (d c) i -> p d c i", d=2)
            nview = nmat.rearrange("p (d c) i -> p d c i", d=2)
            chv = {n: cols[n].rearrange("p c (d h) -> p h d c", d=2) for n in ("cum", "eG", "gl")}
            runs = [(0, 0, P), (P, P + GAP, TOK - P)]

            def prepare(h):
                for n, to in (("cum", "ncum"), ("eG", "negeG"), ("gl", "gl")):
                    gp.tensor_copy(hcv[to], chv[n][:, bd(h, 1)].rearrange("p a d c -> p (a d) c"))\
                      .then_inc(head_cols_made.sem, 1)
                gp.tensor_copy(rg_cols, rg_tab[:, :, bd(h, 1)].rearrange("p n a -> p (n a)")).then_inc(head_cols_made.sem, 1)

            def mask(d):
                s = 1 if d == 0 else -1
                gp.affine_select(out=dview[:, d], in_=nview[:, d], compare_op=ALU.is_ge, fill=MASKED, base=0,
                                 pattern=[[0, NCH], [s, P]], channel_multiplier=-s).then_inc(masked.sem, 1)

            def head(h, last=False):
                gp.wait_ge(silu_done.sem, silu_done.at(h, -1))
                gp.wait_ge(eG_row.sem, eG_row.at(h, 0))
                for d in range(DIRS):
                    for a, b, n in runs:
                        gp.tensor_tensor(qd[:, d, a:a + n], eG_rows[:, d, a:a + n], qT[:, b:b + n], ALU.mult)\
                          .then_inc(qd_made.sem, 1)
                for d in range(DIRS):
                    gp.wait_ge(rg_root.sem, rg_root.at(h, d + 1))
                    gp.wait_ge(rg_ix_made.sem, rg_ix_made.at(h, d + 1))
                    gp.tensor_tensor(RB, RB, RC, ALU.mult).then_inc(rg_bx_made.sem, 1)
                    if d == 0:
                        gp.wait_ge(rk_root.sem, rk_root.at(h, 1))
                        gp.wait_ge(turn_taken_v.sem, turn_taken_v.at(h, 3))
                        gp.tensor_tensor(vtok, vtok, hcc["rkinv"].unsqueeze(2).to_broadcast([P, NCH, P]), ALU.mult)\
                          .then_inc(v_scaled.sem, 1)
                gp.wait_ge(rg_scanned.sem, rg_scanned.at(h, 6))
                own(gp.tensor_tensor(RH, RH, RC, ALU.add))
                gp.wait_ge(silu_done.sem, silu_done.at(h, 3))
                own(gp.tensor_tensor(RH, RH, sg, ALU.mult))
                for a, b, n in runs:
                    gp.dma_start(scr_o[bd(h + HEADS, 1), :, a:a + n].rearrange("a p t -> (a p) t"), RH[:, b:b + n])\
                      .then_inc(rg_stored.sem, 16)
                gp.wait_ge(S_made.sem, S_made.at(h, 2))
                gp.dma_start(new_delta[0, 0, :, bd(h, 1)].rearrange("d a k v -> k (d a) v"), S_new)\
                  .then_inc(prompt_S_stored.sem, 16)
                if not last:
                    gp.wait_ge(decay_in.sem, decay_in.at(h, 2) * 16)
                    gp.wait_ge(stepped.sem, stepped.at(h, 18))
                    gp.wait_ge(S_made.sem, S_made.at(h, 16))
                    gp.wait_ge(rhs_made.sem, rhs_made.at(h, 16))
                    gp.wait_ge(vnew_made.sem, vnew_made.at(h, 36))
                    prepare(h + 1)
                    for d in range(DIRS):
                        mask(d)
                gp.wait_ge(oz_made.sem, oz_made.at(h, 4))
                gp.dma_start(scr_o[bd(h, 1)].rearrange("a p t -> (a p) t"), oz).then_inc(oz_stored.sem, 16)
                own.settle()
                if not last:
                    gp.wait_ge(oz_stored.sem, oz_stored.at(h, 1) * 16)
                    own(gp.tensor_tensor(clear_mark, ident[:, 0:1], ident[:, 0:1], ALU.mult))
                    gp.memset(Zt, 0.0).then_inc(Zt_cleared.sem, 1)
                own.clear()

            gp.wait_ge(decay_in.sem, 32)
            prepare(0)
            for d in range(DIRS):
                mask(d)
            own.clear()
            with gp.Fori(0, HEADS - 1) as h:
                head(h)
            head(HEADS - 1, last=True)
            gp.wait_ge(post_in, 16 * 7)
            for s in range(2):
                gp.tensor_tensor(gate_post[:, s], gate_post[:, s], post_b, ALU.mult).then_inc(gate_post_made, 1)

            def residual(buf, n):
                gp.wait_ge(xr_in[buf], n)
                gp.tensor_tensor(x_res[:, buf], x_res[:, buf], pos_res[:, buf], ALU.add).then_inc(xr_added, 1)

            with gp.Fori(0, 4) as i:
                residual(1, i * 48 + 48)
                residual(0, i * 48 + 64)

        @block.tensor
        def _(pe):
            pe.wait_ge(consts_made, 1)
            pe.wait_ge(rows_in, 16 * 11)
            pe.transpose(banks[6][:, 0:P], rowsA, ident).then_inc(cols_turned, 1)
            pe.transpose(banks[7][:, 0:B_ROWS], rowsB[0:B_ROWS, :], ident[0:B_ROWS, 0:B_ROWS]).then_inc(cols_turned, 1)
            pe.wait_ge(silu_c_made, 1)
            for k in range(KT):
                pe.wait_ge(ada_in[k], 16)
                for n in range(6):
                    mm = pe.matmul(banks[n][0:2, :], silu_c[:, :, k], adaw[:, k, 512 * n:512 * n + 512],
                                   start=(k == 0), stop=(k == KT - 1))
                    if k == KT - 1:
                        mm.then_inc(ada_done, 1)
            for m in range(16):
                pe.wait_ge(mod_row_made, m // 4 + 1)
                mm = pe.transpose(banks[6][:, 2 * m:2 * m + 2], mod_row[0:2, P * m:P * m + P], ident[0:2, 0:2])
            mm.then_inc(mod_turned, 1)
            pe.wait_ge(mod_row_made, 6)

            def turn_x(buf, n):
                pe.wait_ge(x_normed, n + 1)
                for half in range(2):
                    if not isinstance(n, int) or n > 1:
                        pe.wait_ge((h_made_v, h_made_a)[half], 4 * n - 4)
                    for k in range(4):
                        mm = pe.transpose(banks[2 * buf + half][:, P * k:P * k + P],
                                          x_in[:, buf, P * (4 * half + k):P * (4 * half + k) + P], ident)
                    mm.then_inc(x_turned, 1)

            turn_x(0, 0)
            turn_x(1, 1)
            with pe.Fori(0, 3) as i:
                turn_x(0, 2 * i + 2)
                turn_x(1, 2 * i + 3)
            turn_x(0, 8)
            pe.wait_ge(ba_w_in, 16)
            pe.wait_ge(h_made_v, 36)
            pe.wait_ge(h_made_a, 36)
            for g, (o, n) in enumerate(GROUPS):
                for k in range(KT):
                    mm = pe.matmul(banks[5 + g][0:32, 0:n], w_ring[:, 0, k, 0:32], hT[:, k, o:o + n],
                                   start=(k == 0), stop=(k == KT - 1))
                if g == 2:
                    mm.then_inc(ba_done, 1)

            def project(first, count, h=None):
                for u in range(first, first + count):
                    j, g, k = u // 24, u % 24 // 8, u % 8
                    n = u // 8
                    if u % 24 == 0:
                        slot = w_in_slot[j % 3]
                        if h is None:
                            pe.wait_ge(slot.sem, 16 if j < 5 else 32)
                        else:
                            pe.wait_ge(slot.sem, slot.at(h, j // 3 + 1) * 16)
                    if k == 0:
                        if h is not None:
                            pe.wait_ge(proj_taken.sem, proj_taken.at(h, n - 1))
                        elif n >= 8:
                            pe.wait_ge(proj_taken.sem, n - 7)
                    o, w = GROUPS[g]
                    mm = pe.matmul(banks[n % 2][:, 0:w], w_ring[:, j % 3, k], hT[:, k, o:o + w],
                                   start=(k == 0), stop=(k == KT - 1))
                    if k == KT - 1:
                        mm.then_inc(projected.sem, 1)

            project(48, 24)
            pe.wait_ge(baT_made, 3)
            for ch in range(NCH):
                mm = pe.transpose(banks[2][:, 32 * ch:32 * ch + 32], baT[0:32, col(ch):col(ch) + P], ident[0:32, 0:32])
            mm.then_inc(ba_turned, 1)
            project(72, 24)
            pe.wait_ge(g_made, 1)
            g = sp_e[:, 0:NCH * 16].rearrange("p (c n) -> p c n", n=16)
            G_ps = banks[3][:, 0:NCH * 16].rearrange("p (c n) -> p c n", n=16)
            for d in range(DIRS):
                pe.matmul(G_ps[:, :, 8 * d:8 * d + 8], tri[:, d], g[:, :, 8 * d:8 * d + 8], start=True, stop=True)\
                  .then_inc(G_summed, 1)
            pe.matmul(banks[4][:, 0:NCH * 16], ones, sp_e[:, 0:NCH * 16], start=True, stop=True).then_inc(G_summed, 1)
            row_banks = [[5, 6, 7], [2, 3, 4]]
            for d in range(DIRS):
                if d == 1:
                    pe.wait_ge(G_taken, 2)
                for ch in range(NCH):
                    mm = pe.matmul(banks[row_banks[d][ch // 4]][0:8, P * (ch % 4):P * (ch % 4) + P],
                                   g[:, ch, 8 * d:8 * d + 8], tri[:, d], start=True, stop=True)
                    if ch % 4 == 3 or ch == NCH - 1:
                        mm.then_inc(Grow_done, 1)
            project(96, 48)

            def turn(src, first_bank):
                for b in range(3):
                    for i in range(3):
                        ch = 3 * b + i
                        mm = pe.transpose(banks[first_bank + b][:, P * i:P * i + P], src[:, col(ch):col(ch) + P], ident)
                    mm.then_inc(turned.sem, 1)

            def head(h, last=False):
                cursor = [0]

                def fill(count):
                    first, cursor[0] = cursor[0], cursor[0] + count
                    if last:
                        count = max(0, min(count, 48 - first))
                    project(first, count, h)

                fill(8)
                pe.wait_ge(oz_made.sem, oz_made.at(h, 0))
                pe.wait_ge(silu_done.sem, silu_done.at(h, -1))
                turn(qT, 5)
                for f in range(5):
                    pe.wait_ge(turn_taken_a.sem, turn_taken_a.at(h, (4, 8, 12, 15, 18)[f]))
                    for i in range(2 if f < 4 else 1):
                        ch = 2 * f + i
                        mm = pe.matmul(banks[2 + f][:, 2 * P * i:2 * P * i + 2 * P].rearrange("p (j t) -> p j t", j=2),
                                       kT[:, col(ch):col(ch) + P], kq[:, :, col(ch):col(ch) + P], start=True, stop=True)
                    mm.then_inc(scored.sem, 1)
                fill(16)
                pe.wait_ge(wg_in.sem, wg_in.at(h, 0) * 16)
                pe.wait_ge(conv_done.sem, conv_done.at(h, 0))
                pe.wait_ge(turn_taken_a.sem, turn_taken_a.at(h, 21))
                for d in range(DIRS):
                    for gate in range(2):
                        if d == 0 and gate == 1:
                            fill(8)
                            pe.wait_ge(silu_done.sem, silu_done.at(h, 1))
                            turn(vT, 2)
                        for b, (o, n) in enumerate(GROUPS):
                            if d == 0 and gate == 0:
                                pe.wait_ge(scores_taken.sem, scores_taken.at(h, 28))
                            elif d == 0:
                                pe.wait_ge(turn_taken_v.sem, turn_taken_v.at(h, b + 1))
                            else:
                                pe.wait_ge(gate_tanh.sem, gate_tanh.at(h, 3 * gate + b + 1))
                            pe.matmul(banks[(2 if gate else 5) + b][:, 0:n], wg[:, 2 * gate + d], xf[:, o:o + n],
                                      start=True, stop=True).then_inc(gated.sem, 1)
                    if d == 0:
                        fill(8)
                fill(24)
                pe.wait_ge(Z_placed.sem, Z_placed.at(h, 8))
                pe.wait_ge(Zt_placed.sem, Zt_placed.at(h, 8))
                pe.wait_ge(gate_tanh.sem, gate_tanh.at(h, 12))

                def q_products(level, g):
                    b = banks[2 if g % 2 == 0 else 5]
                    if g >= 2:
                        pe.wait_ge(Q_taken.sem, Q_taken.at(h, 6 * level + g - 1))
                    elif level:
                        pe.wait_ge(Q_taken.sem, Q_taken.at(h, 6))
                    if level:
                        pe.wait_ge(dZ_taken.sem, dZ_taken.at(h, 4 * g + 4))
                    for i in range(3):
                        m = 3 * g + i
                        mm = pe.matmul(b[:, P * i:P * i + P], nmat[:, m], Zt[:, m], start=True, stop=True)
                    mm.then_inc(Q_done.sem, 1)

                def join32(g):
                    b = 3 if g % 2 == 0 else 6
                    pe.wait_ge(Q_taken.sem, Q_taken.at(h, g + 1))
                    if g >= 2:
                        pe.wait_ge(dZ_taken.sem, dZ_taken.at(h, 4 * (g - 1)))
                    for i in range(3):
                        pe.matmul(banks[b][:, P * i:P * i + P], Z[:, 3 * g + i], Qb[:, g % 2, i], start=True, stop=True)
                    for i in range(3):
                        mm = pe.matmul(banks[b + 1][:, P * i:P * i + P], Qb[:, g % 2, i], Z[:, 3 * g + i],
                                       start=True, stop=True)
                    mm.then_inc(dZ_done.sem, 1)

                def join64(g):
                    b = banks[3 if g % 2 == 0 else 6]
                    pe.wait_ge(Q_taken.sem, Q_taken.at(h, 6 + g + 1))
                    pe.wait_ge(dZ_taken.sem, dZ_taken.at(h, 24 + g - 1 if g >= 2 else 24))
                    r = slice(64, P) if g < 3 else slice(0, 64)
                    for i in range(3):
                        mm = pe.matmul(b[:, P * i:P * i + P], Qb[r, g % 2, i], Z[r, 3 * g + i], start=True, stop=True)
                    mm.then_inc(dZ_done.sem, 1)

                for level, join in ((0, join32), (1, join64)):
                    for g in range(7):
                        if g < 6:
                            q_products(level, g)
                            fill(LEVEL_FILLS[6 * level + g])
                        if g > 0:
                            join(g - 1)
                pe.wait_ge(dZ_taken.sem, dZ_taken.at(h, 30))
                pe.wait_ge(v_scaled.sem, v_scaled.at(h, 1))
                pe.wait_ge(qd_made.sem, qd_made.at(h, 4))
                for step in range(NCH):
                    chunk = (step, step if step == 0 else NCH - step)
                    half = SCAN_FILLS[step] // 2
                    if step:
                        for d in range(DIRS):
                            if step == 1:
                                pe.wait_ge(S_in.sem, S_in.at(h, 0) * 16)
                            else:
                                pe.wait_ge(S_made.sem, S_made.at(h, 2 * step - 2 + d + 1))
                            pe.matmul(banks[2 + d][:, 0:P], kT[:, col(chunk[d]):col(chunk[d]) + P], S[:, d],
                                      start=True, stop=True).then_inc(KS_done.sem, 1)
                        fill(half)
                    for d in range(DIRS):
                        if step:
                            pe.wait_ge(rhs_made.sem, rhs_made.at(h, 2 * step - 2 + d + 1))
                        rhs = rhs_v[:, d] if step else vtok[:, 0]
                        pe.matmul(banks[2 + d][:, P:2 * P], Z[:, d * NCH + chunk[d]], rhs, start=True, stop=True)\
                          .then_inc(solved.sem, 1)
                    fill(SCAN_FILLS[step] - half if step else SCAN_FILLS[step])
                    for d in range(DIRS):
                        ch, m = chunk[d], d * NCH + chunk[d]
                        bank = banks[4 + d]
                        if step:
                            pe.wait_ge(o_made.sem, o_made.at(h, 1 if step == 1 else 2 * step - 2 + d))
                            if step == 1:
                                pe.wait_ge(S_made.sem, S_made.at(h, 2))
                        pe.wait_ge(vnew_made.sem, vnew_made.at(h, 4 * step + 2 * d + 2))
                        if step < NCH - 1:
                            pe.matmul(bank[:, 0:P], ktok[:, ch], vd[:, d], start=True, stop=True)
                        if step == 0:
                            if d == 1:
                                pe.matmul(bank[:, P:2 * P], decay[:, 0], vt[:, 0], start=True, stop=False)
                                mm = pe.matmul(bank[:, P:2 * P], decay[:, NCH], vt[:, 1], start=False, stop=True)
                                mm.then_inc(stepped.sem, 2)
                        else:
                            pe.matmul(bank[:, P:2 * P], qd[:, d, P * ch:P * ch + P], S[:, d], start=True, stop=False)
                            pe.matmul(bank[:, P:2 * P], decay[:, m], vt[:, d], start=False, stop=True)\
                              .then_inc(stepped.sem, 1)
                fill(5)
                if not last:
                    pe.wait_ge(silu_done.sem, silu_done.at(h, 5))
                    pe.wait_ge(o_made.sem, o_made.at(h, 17))
                    turn(kT, 2)
                fill(5)
                pe.wait_ge(o_normed.sem, o_normed.at(h, 1))
                for b in range(3):
                    for i in range(3):
                        mm = pe.transpose(banks[(6, 7, 5)[b]][:, P * i:P * i + P], o_tok[:, 3 * b + i], ident)
                    mm.then_inc(o_turned.sem, 1)

            pe.wait_ge(silu_done.sem, 2)
            pe.wait_ge(G_taken, 8)
            turn(kT, 2)

            with pe.Fori(0, HEADS - 1) as h:
                head(h)
            head(HEADS - 1, last=True)

            pe.wait_ge(oz_made.sem, oz_made.at(HEADS - 1, 4))
            pe.wait_ge(rg_scanned.sem, rg_scanned.at(HEADS - 1, 6))
            pe.transpose(banks[7][0:16, 0:P], hc[:, 244:260], ident).then_inc(states_turned, 1)

            def out_tile(buf, n, loaded):
                pe.wait_ge(ot_in[buf], loaded)
                if not isinstance(n, int) or n >= 2:
                    pe.wait_ge(y_made, n - 1)
                for half in range(2):
                    for k in range(16):
                        mm = pe.matmul(banks[2 * buf + half][:, :], ot[:, buf, k], wo[:, k, 512 * half:512 * half + 512],
                                       start=(k == 0), stop=(k == 15))
                mm.then_inc(y_done, 1)

            for q in range(4):
                pe.wait_ge(w_out_in[q], 16)
            out_tile(0, 0, 16)
            out_tile(1, 1, 16)
            with pe.Fori(0, 3) as i:
                out_tile(0, 2 * i + 2, 16 * i + 32)
                out_tile(1, 2 * i + 3, 16 * i + 32)
            out_tile(0, 8, 80)

        @block.scalar
        def _(act):
            own = Chain(act, a_own)
            act.wait_ge(cols_made, 2)
            act.activation(silu_c, colsB[:, 0:16].rearrange("p (s k) -> p s k", s=2), ACT.Tanh, scale=0.5).then_inc(c_tanh, 1)

            def x_tile(buf, n):
                if isinstance(n, int) and n == 0:
                    act.wait_ge(x_loaded[0], 16)
                else:
                    act.wait_ge(x_added, n)
                    act.wait_ge(x_squared, n)
                act.activation(square_out, x_in[:, buf], ACT.Square, accum_out=x_ss[:, buf:buf + 1]).then_inc(x_squared, 1)
                act.wait_ge(x_meaned, n + 1)
                act.activation(x_ss[:, buf:buf + 1], x_ss[:, buf:buf + 1], ACT.Sqrt).then_inc(x_rooted, 1)
                act.wait_ge(mod_made, 3)
                act.wait_ge(x_turned, 2 * n + 2)
                s = 0 if isinstance(n, int) and n == 0 else 1
                first = 0 if s == 0 else GAP + P * n
                for k in range(4):
                    act.activation(hT[:, 4 + k, bd(first, P)], banks[2 * buf + 1][:, P * k:P * k + P], ACT.Identity,
                                   bias=mod_ab[:, 2 + s, 4 + k:5 + k], scale=mod_ab[:, s, 4 + k:5 + k]).then_inc(h_made_a, 1)

            x_tile(0, 0)
            x_tile(1, 1)
            with act.Fori(0, 3) as i:
                x_tile(0, 2 * i + 2)
                x_tile(1, 2 * i + 3)
            x_tile(0, 8)
            act.wait_ge(consts_in, 112)
            act.activation(a_log, a_log, ACT.Exp).then_inc(sp_exped, 1)

            def take_projection(n, h=None):
                j, g = n // 3, n % 3
                o, w = GROUPS[g]
                if h is None:
                    act.wait_ge(projected.sem, n - 5)
                else:
                    act.wait_ge(projected.sem, projected.at(h, n + 1))
                    if j >= 2 and g == 0:
                        act.wait_ge(conv_done.sem, conv_done.at(h, j - 4))
                if j < 2:
                    act.activation((sz, sg)[j][:, o:o + w], banks[n % 2][:, 0:w], ACT.Copy, scale=0.5)\
                       .then_inc(proj_taken.sem, 1)
                else:
                    act.activation(raw[:, j - 2, 2 + o:2 + o + w], banks[n % 2][:, 0:w], ACT.Copy)\
                       .then_inc(proj_taken.sem, 1)

            act.wait_ge(raw_cleared, 1)
            for n in range(6, 9):
                take_projection(n)
            act.wait_ge(ba_made, 1)
            act.activation(cols["beta"], ba[:, :, 0:16], ACT.Exp, scale=-1.0).then_inc(sp_exped, 1)
            act.wait_ge(sp_ready, 2)
            own(act.activation(sp_e, sp_y, ACT.Abs))
            act.activation(sp_e, sp_e, ACT.Exp, scale=-1.0).then_inc(sp_exped, 1)
            for n in range(9, 12):
                take_projection(n)
            act.wait_ge(G_exp_in, 1)
            act.activation(cols["eG"], cols["cum"], ACT.Exp).then_inc(G_exped, 1)
            act.activation(cols["gl"], cols["tot"], ACT.Exp).then_inc(G_exped, 1)
            act.activation(cols["edec"], cols["edec"], ACT.Exp).then_inc(G_exped, 1)
            for n in range(12, 18):
                take_projection(n)
            act.wait_ge(gate_stored, 16)
            act.wait_ge(decay_in.sem, 32)
            act.wait_ge(grounds_made, 1)
            act.activation(view("sub", 0, 2 * TOK), view("nmat"), ACT.Exp).then_inc(eG_row.sem, 1)
            for n, (src, to) in enumerate(((RB, qT), (RA, kT))):
                act.wait_ge(conv_done.sem, 2 - n)
                act.activation(to, src, ACT.Tanh).then_inc(tanh_done.sem, 1)

            def head(h, last=False):
                act.wait_ge(head_cols_made.sem, head_cols_made.at(h, 0))
                for d in range(DIRS):
                    act.wait_ge(masked.sem, masked.at(h, d - 1))
                    for ch in range(NCH):
                        m = NCH * d + ch
                        act.activation(decay[:, m], decay[:, m], ACT.Exp, bias=hcv["ncum"][:, d, ch:ch + 1])\
                           .then_inc(decay_exped.sem, 1)
                for b in range(3):
                    act.wait_ge(turned.sem, turned.at(h, b - 2))
                    act.activation(ktok[:, 3 * b:3 * b + 3], banks[2 + b][:, 0:3 * P].rearrange("p (c d) -> p c d", d=P),
                                   ACT.Copy).then_inc(turn_taken_a.sem, 1)
                    for i in range(3):
                        c1 = 3 * b + i
                        act.activation(RC[:, P * c1:P * c1 + P], banks[2 + b][:, P * i:P * i + P], ACT.Square,
                                       accum_out=hcc["ssk"][:, c1:c1 + 1]).then_inc(turn_taken_a.sem, 1)
                act.wait_ge(oz_made.sem, oz_made.at(h, 0))
                take_projection(0, h)
                for b in range(3):
                    act.wait_ge(turned.sem, turned.at(h, b + 1))
                    for i in range(3):
                        c1 = 3 * b + i
                        act.activation(RH[:, P * c1:P * c1 + P], banks[5 + b][:, P * i:P * i + P], ACT.Square,
                                       accum_out=hcc["ssq"][:, c1:c1 + 1]).then_inc(turn_taken_a.sem, 1)
                take_projection(1, h)
                act.wait_ge(conv_done.sem, conv_done.at(h, 1))
                act.activation(tanh_v, vT, ACT.Tanh).then_inc(tanh_done.sem, 1)
                take_projection(2, h)
                act.wait_ge(silu_done.sem, silu_done.at(h, 0))
                for d in range(DIRS):
                    if d == 1:
                        act.wait_ge(rg_scanned.sem, rg_scanned.at(h, 3))
                    for b, (o, n) in enumerate(GROUPS):
                        act.wait_ge(gated.sem, gated.at(h, 6 * d + b + 1))
                        act.activation(RA[:, o:o + n], banks[5 + b][:, 0:n], ACT.Tanh, scale=0.5,
                                       bias=br_h[:, d:d + 1]).then_inc(gate_tanh.sem, 1)
                    act.wait_ge(gate_tanh.sem, gate_tanh.at(h, 6 * d + 3))
                    act.activation(RB, RA, ACT.Tanh, scale=nc8_h[:, d:d + 1], bias=nc8_h[:, d:d + 1])\
                       .then_inc(rg_t_made.sem, 1)
                    act.wait_ge(rg_t_made.sem, rg_t_made.at(h, 3 * d + 1))
                    act.activation(RA, RA, ACT.Exp, scale=c8_h[:, d:d + 1], bias=c8_h[:, d:d + 1])\
                       .then_inc(rg_t_made.sem, 1)
                    act.wait_ge(rg_t_made.sem, rg_t_made.at(h, 3 * d + 2))
                    act.activation(RC, RA, ACT.Square).then_inc(rg_t_made.sem, 1)
                    act.wait_ge(rg_u_made.sem, rg_u_made.at(h, d + 1))
                    for b, (o, n) in enumerate(GROUPS):
                        act.wait_ge(gated.sem, gated.at(h, 6 * d + 3 + b + 1))
                        act.activation(RC[:, o:o + n], banks[2 + b][:, 0:n], ACT.Tanh, scale=0.5,
                                       bias=bi_h[:, d:d + 1]).then_inc(gate_tanh.sem, 1)
                    act.activation(RB, RB, ACT.Sqrt, scale=0.25).then_inc(rg_root.sem, 1)
                    if d == 0:
                        act.wait_ge(ss_done.sem, ss_done.at(h, 1))
                        act.activation(hcc["rkinv"], hcc["ssk"], ACT.Sqrt).then_inc(rk_root.sem, 1)
                        for n in (3, 4):
                            take_projection(n, h)
                for n in range(5, 8 if not last else 6):
                    take_projection(n, h)
                act.wait_ge(Zt_cleared.sem, Zt_cleared.at(h, 0))
                for d in range(DIRS):
                    src = block_T if d else block_in
                    act.wait_ge(unblocked.sem, unblocked.at(h, 2))
                    for q in range(4):
                        r = slice(BLK * q, BLK * q + BLK)
                        act.activation(Zt[r, NCH * d:NCH * d + NCH, r], src[r, NCH * d:NCH * d + NCH, :], ACT.Copy)\
                           .then_inc(Zt_placed.sem, 1)
                done = [8, 64]

                def given(count):
                    done[1] += count
                    while 8 * (done[0] + 1) <= done[1]:
                        if not last:
                            take_projection(done[0], h)
                        done[0] += 1

                for g in range(6):
                    act.wait_ge(dZ_done.sem, dZ_done.at(h, g + 1))
                    m = slice(3 * g, 3 * g + 3)
                    for to, bank, below in ((Zt, 3, g < 3), (Z, 4, g >= 3)):
                        ps = banks[bank + 3 * (g % 2)][:, 0:3 * P].rearrange("p (m i) -> p m i", i=P)
                        for b in (0, 2):
                            r, cc = (b + 1, b) if below else (b, b + 1)
                            r, cc = slice(BLK * r, BLK * r + BLK), slice(BLK * cc, BLK * cc + BLK)
                            act.activation(to[r, m, cc], ps[r, :, cc], ACT.Copy).then_inc(dZ_taken.sem, 1)
                    given(LEVEL_FILLS[g])
                act.wait_ge(Z_placed.sem, Z_placed.at(h, 8))
                act.wait_ge(Zt_placed.sem, Zt_placed.at(h, 8))
                act.wait_ge(proj_taken.sem, proj_taken.at(h, 6))
                for to, src in ((tanh_z, sz), (tanh_g, sg)):
                    act.activation(to, src, ACT.Tanh).then_inc(tanh_done.sem, 1)
                for g in range(6):
                    act.wait_ge(dZ_done.sem, dZ_done.at(h, 6 + g + 1))
                    ps = banks[3 + 3 * (g % 2)][:, 0:3 * P].rearrange("p (m i) -> p m i", i=P)
                    r, cc = (slice(0, 64), slice(64, P)) if g < 3 else (slice(64, P), slice(0, 64))
                    act.activation(Z[r, 3 * g:3 * g + 3, cc], ps[r, :, cc], ACT.Copy).then_inc(dZ_taken.sem, 1)
                    given(LEVEL_FILLS[6 + g])

                def square_o(chunks):
                    for ch in chunks:
                        act.activation(RC[:, P * ch:P * ch + P], o_tok[:, ch], ACT.Square,
                                       accum_out=hcc["sso"][:, ch:ch + 1]).then_inc(o_squared.sem, 1)

                for step in range(NCH):
                    chunk = (step, step if step == 0 else NCH - step)
                    for d in range(DIRS):
                        act.wait_ge(solved.sem, solved.at(h, 2 * step + d + 1))
                        c1 = slice(chunk[d], chunk[d] + 1)
                        for to, scale in ((vd, "Pdec"), (vt, "Pk")):
                            act.activation(to[:, d], banks[2 + d][:, P:2 * P], ACT.Copy, scale=hcv[scale][:, d, c1])\
                               .then_inc(vnew_made.sem, 1)
                    given(SCAN_FILLS[step])
                    if step == 4 and not last:
                        act.wait_ge(conv_done.sem, conv_done.at(h, 3))
                        act.activation(qT, RB, ACT.Tanh).then_inc(tanh_done.sem, 1)
                        act.wait_ge(silu_done.sem, silu_done.at(h, 3))
                        act.wait_ge(decay_in.sem, decay_in.at(h, 2) * 16)
                        act.activation(view("sub", 0, 2 * TOK), view("nmat"), ACT.Exp).then_inc(eG_row.sem, 1)
                    if step == 7:
                        act.wait_ge(o_made.sem, o_made.at(h, 13))
                        act.wait_ge(rg_stored.sem, rg_stored.at(h, 2) * 16)
                        square_o((0, 3, 4, 5, 6))
                if not last:
                    act.wait_ge(conv_done.sem, conv_done.at(h, 2))
                    act.wait_ge(KS_done.sem, KS_done.at(h, 16))
                    act.activation(kT, RA, ACT.Tanh).then_inc(tanh_done.sem, 1)
                act.wait_ge(o_made.sem, o_made.at(h, 15))
                square_o((2, 7))
                act.wait_ge(o_made.sem, o_made.at(h, 17))
                square_o((1, 8))
                act.wait_ge(o_meaned.sem, o_meaned.at(h, 1))
                act.activation(hcc["rstd"], hcc["rstd"], ACT.Sqrt).then_inc(o_rooted.sem, 1)
                if not last:
                    for n in (16, 17):
                        if n >= done[0]:
                            take_projection(n, h)

            with act.Fori(0, HEADS - 1) as h:
                head(h)
            head(HEADS - 1, last=True)

            def y_tile(buf, n):
                act.wait_ge(y_done, n + 1)
                for half in range(2):
                    if not (isinstance(n, int) and n == 0 and half == 0):
                        act.wait_ge(y_squared, 2 * n + half)
                    act.activation(y_junk[:, 512 * half:512 * half + 512], banks[2 * buf + half][:, :], ACT.Square,
                                   accum_out=y_ss[:, 4 * buf + half:4 * buf + half + 1]).then_inc(y_squared, 1)
                act.wait_ge(y_meaned, n + 1)
                act.activation(y_ss[:, 4 * buf + 2:4 * buf + 3], y_ss[:, 4 * buf + 2:4 * buf + 3], ACT.Sqrt)\
                   .then_inc(y_rooted, 1)

            y_tile(0, 0)
            y_tile(1, 1)
            with act.Fori(0, 3) as i:
                y_tile(0, 2 * i + 2)
                y_tile(1, 2 * i + 3)
            y_tile(0, 8)

        @block.vector
        def _(dve):
            own = Chain(dve, v_own)
            dve.wait_ge(cols_turned, 2)
            dve.tensor_copy(colsA, banks[6][:, 0:P]).then_inc(cols_made, 1)
            dve.tensor_copy(colsB[:, 0:B_ROWS], banks[7][:, 0:B_ROWS]).then_inc(cols_made, 1)
            dve.wait_ge(c_tanh, 1)
            c_cols = colsB[:, 0:16].rearrange("p (s k) -> p s k", s=2)
            own(dve.scalar_tensor_tensor(silu_c, silu_c, 1.0, c_cols, ALU.add, ALU.mult))
            dve.tensor_scalar(silu_c, silu_c, 0.5, None, ALU.mult).then_inc(silu_c_made, 1)
            own(dve.tensor_scalar(colsA[:, 0:96], colsA[:, 0:96], 0.5, None, ALU.mult))
            own(dve.tensor_scalar(hc[:, 180:212], colsB[:, B_BR:B_BR + 32], 0.5, None, ALU.mult))
            id4 = ident.rearrange("p (q m) -> p q m", q=4)
            for to, first in ((pf, 0), (pb, NCH)):
                own(dve.tensor_reduce(to, id4[:, :, first:first + NCH], AX.XY, ALU.add))
                own(dve.tensor_scalar(to, to, -1.0, None, ALU.mult))
            dve.wait_ge(consts_in, 112)
            dve.wait_ge(ada_done, 6)
            for n in range(6):
                dve.tensor_tensor(mod_row[0:2, 512 * n:512 * n + 512], banks[n][0:2, :],
                                  ada_brow[0:2, 512 * n:512 * n + 512], ALU.add).then_inc(mod_row_made, 1)
            dve.wait_ge(mod_turned, 1)
            m_ps = banks[6][:, 0:32].rearrange("p (m s) -> p s m", s=2)
            for s in range(2):
                dve.scalar_tensor_tensor(mod_ab[:, s], m_ps[:, s, 8:16], 1.0, colsB[:, B_PRE:B_PRE + 8],
                                         ALU.add, ALU.mult).then_inc(mod_made, 1)
            dve.tensor_copy(mod_ab[:, 2:4], m_ps[:, :, 0:8]).then_inc(mod_made, 1)
            dve.wait_ge(mod_made, 3)

            def x_tile(buf, n, loaded):
                prompt = isinstance(n, int) and n == 0
                dve.wait_ge(x_loaded[buf], loaded)
                if not prompt:
                    dve.tensor_tensor(x_in[:, buf], x_in[:, buf], pos[:, buf], ALU.add).then_inc(x_added, 1)
                dve.wait_ge(x_squared, n + 1)
                dve.tensor_scalar(x_ss[:, buf:buf + 1], x_ss[:, buf:buf + 1], 1.0 / D, EPS, ALU.mult, ALU.add)\
                   .then_inc(x_meaned, 1)
                dve.wait_ge(x_rooted, n + 1)
                own(dve.reciprocal(x_ss[:, buf:buf + 1], x_ss[:, buf:buf + 1]))
                dve.tensor_scalar(x_in[:, buf], x_in[:, buf], x_ss[:, buf:buf + 1], None, ALU.mult).then_inc(x_normed, 1)
                dve.wait_ge(x_turned, 2 * n + 1)
                s = 0 if prompt else 1
                first = 0 if prompt else GAP + P * n
                for k in range(4):
                    dve.tensor_scalar(hT[:, k, bd(first, P)], banks[2 * buf][:, P * k:P * k + P], mod_ab[:, s, k:k + 1],
                                      mod_ab[:, 2 + s, k:k + 1], ALU.mult, ALU.add).then_inc(h_made_v, 1)

            x_tile(0, 0, 16)
            x_tile(1, 1, 48)
            own.clear()
            with dve.Fori(0, 3) as i:
                x_tile(0, 2 * i + 2, 48 * i + 64)
                x_tile(1, 2 * i + 3, 48 * i + 96)
                own.clear()
            x_tile(0, 8, 16 + 48 * 4)
            dve.wait_ge(ba_done, 1)
            for g, (o, n) in enumerate(GROUPS):
                dve.tensor_copy(baT[0:32, o:o + n], banks[5 + g][0:32, 0:n]).then_inc(baT_made, 1)
            dve.tensor_scalar(sp_y[:, NCH * 16:], colsB[:, B_LAM:B_LAM + 16], -1.0, None, ALU.mult).then_inc(sp_ready, 1)
            dve.wait_ge(ba_turned, 1)
            dve.tensor_copy(ba, banks[2][:, 0:NCH * 32].rearrange("p (c n) -> p c n", n=32)).then_inc(ba_made, 1)
            dve.wait_ge(ba_made, 1)
            by_tok = lambda a: a[:, 0:NCH * 16].rearrange("p (c n) -> p c n", n=16)
            dve.tensor_tensor(by_tok(sp_y), ba[:, :, 16:32], dt_bias.unsqueeze(1).to_broadcast([P, NCH, 16]), ALU.add)\
               .then_inc(sp_ready, 1)
            dve.wait_ge(sp_exped, 3)
            own(dve.tensor_scalar(sp_z, sp_e, 2.0, None, ALU.add))
            own(dve.reciprocal(sp_z, sp_z))
            own(dve.tensor_tensor(sp_z, sp_z, sp_e, ALU.mult))
            own(dve.tensor_tensor(sp_z2, sp_z, sp_z, ALU.mult))
            own(dve.tensor_scalar(sp_p, sp_z2, 1.0 / 15, None, ALU.mult))
            for n in (13, 11, 9, 7, 5, 3):
                own(dve.scalar_tensor_tensor(sp_p, sp_p, 1.0 / n, sp_z2, ALU.add, ALU.mult))
            own(dve.scalar_tensor_tensor(sp_p, sp_p, 1.0, sp_z, ALU.add, ALU.mult))
            own(dve.tensor_scalar(sp_r, sp_y, 0.0, None, ALU.max))
            own(dve.scalar_tensor_tensor(sp_r, sp_p, 2.0, sp_r, ALU.mult, ALU.add))
            dve.scalar_tensor_tensor(by_tok(sp_e), by_tok(sp_r), -1.0, a_log.unsqueeze(1).to_broadcast([P, NCH, 16]),
                                     ALU.mult, ALU.mult).then_inc(g_made, 1)
            own(dve.tensor_scalar(hc[:, 212:228], sp_r[:, NCH * 16:], -4.0, None, ALU.mult))
            own(dve.tensor_scalar(hc[:, 228:244], sp_r[:, NCH * 16:], 4.0, None, ALU.mult))
            own(dve.tensor_scalar(cols["beta"], cols["beta"], 1.0, None, ALU.add))
            own(dve.reciprocal(cols["beta"], cols["beta"]))
            dve.wait_ge(G_summed, 3)
            dve.tensor_copy(cols["cum"], by_tok(banks[3])).then_inc(G_taken, 1)
            dve.tensor_copy(cols["tot"], by_tok(banks[4])).then_inc(G_taken, 1)
            dve.wait_ge(G_taken, 2)
            dve.tensor_tensor(cols["edec"], cols["tot"], cols["cum"], ALU.subtract).then_inc(G_exp_in, 1)
            for d in range(DIRS):
                for b in range(3):
                    dve.wait_ge(Grow_done, 3 * d + b + 1)
                    n = min(4 * P, TOK - 4 * P * b)
                    dve.tensor_copy(G_rows[0:HEADS, d, 4 * P * b:4 * P * b + n], banks[(5, 2)[d] + b][0:HEADS, 0:n])\
                       .then_inc(G_taken, 1)
            dve.wait_ge(G_exped, 3)
            own(dve.tensor_scalar(cols["cum"], cols["cum"], -1.0, None, ALU.mult))
            dve.tensor_scalar(cols["eG"], cols["eG"], -1.0, None, ALU.mult).then_inc(cols_ready, 1)
            dve.wait_ge(grounds_made, 1)
            dve.wait_ge(G_stored, 32)
            dve.wait_ge(gate_stored, 16)
            dve.wait_ge(cols_ready, 1)
            own.clear()

            chv = {n: cols[n].rearrange("p c (d h) -> p h d c", d=2) for n in ("beta", "edec")}
            dview = decay.rearrange("p (d c) i -> p d c i", d=2)
            nview = nmat.rearrange("p (d c) i -> p d c i", d=2)
            X = sub[1].rearrange("p (a b) -> p a b", b=BLK)
            RG_AT = {1: ("silu_v", 0), 3: ("u", 0), 5: ("take_v", 0), 9: ("ix", 0), 14: ("scan", 0), 22: ("u", 1), 26: ("ix", 1)}
            RG_AFTER = (("scan", 1),)
            TAPS = [[(1, 0)], [(1, 1)], [(1, 2)], [(1, 3)], [], [(2, 0)], [(2, 1)], [(2, 2)], [(2, 3)]]
            prompt, sample = slice(0, P), slice(P + GAP, TW)
            runs = [(0, 0, P), (P, P + GAP, TOK - P)]

            def conv(j, dest, h, t):
                w = rconvw[:, t, bd(h, 1)] if j == 2 else convw[:, t, bd(h + (8, 0, 0, 16)[j], 1)]
                if t == 0 and j == 2:
                    own(dve.tensor_scalar(dest, raw[:, j, 0:TW], w, colsB[:, bd(B_CB + h, 1)], ALU.mult, ALU.add))
                elif t == 0:
                    own(dve.tensor_scalar(dest, raw[:, j, 0:TW], w, None, ALU.mult))
                else:
                    step = dve.scalar_tensor_tensor(dest, raw[:, j, t:t + TW], w, dest, ALU.mult, ALU.add)
                    if t == 3:
                        step.then_inc(conv_done.sem, 1)
                    else:
                        own(step)

            def silu(a, b, out):
                dve.scalar_tensor_tensor(out, a, 1.0, b, ALU.add, ALU.mult).then_inc(silu_done.sem, 1)

            for j, dest in enumerate((RA, RB, xf)):
                dve.wait_ge(proj_taken.sem, 3 * j + 3)
                for t in range(4):
                    conv(j, dest, 0, t)
            for n, (t, x) in enumerate(((qT, RB), (kT, RA))):
                dve.wait_ge(tanh_done.sem, n + 1)
                silu(t, x, t)
            dve.sem_inc(oz_made.sem, 1)
            own.clear()

            def head(h, last=False):
                dve.wait_ge(proj_taken.sem, proj_taken.at(h, 0))
                for t in range(4):
                    conv(3, vT, h, t)
                dve.wait_ge(turn_taken_a.sem, turn_taken_a.at(h, 12))
                dve.wait_ge(head_cols_made.sem, head_cols_made.at(h, 0))
                own(dve.tensor_scalar(hcc["ssk"], hcc["ssk"], EPS, None, ALU.add))
                own(dve.reciprocal(hcc["rk2"], hcc["ssk"]))
                own(dve.tensor_tensor(hcv["Pk"], chv["beta"][:, bd(h, 1)].rearrange("p a d c -> p (a d) c"),
                                      hcc["rk2"].unsqueeze(1).to_broadcast([P, DIRS, NCH]), ALU.mult))
                dve.tensor_tensor(hcv["Pdec"], hcv["Pk"], chv["edec"][:, bd(h, 1)].rearrange("p a d c -> p (a d) c"),
                                  ALU.mult).then_inc(ss_done.sem, 1)
                dve.wait_ge(turn_taken_a.sem, turn_taken_a.at(h, 21))
                dve.tensor_scalar(hcc["epsq"], hcc["ssq"], P * EPS, P * EPS * EPS, ALU.mult, ALU.add)\
                   .then_inc(ss_done.sem, 1)
                for f in range(5):
                    dve.wait_ge(scored.sem, scored.at(h, f + 1))
                    n = 2 if f < 4 else 1
                    ps = banks[2 + f][:, 0:2 * P * n].rearrange("p (c j t) -> p c j t", j=2, t=P)
                    cs = slice(2 * f, 2 * f + n)
                    for d in range(DIRS):
                        for i in range(n):
                            m = NCH * d + 2 * f + i
                            dve.wait_ge(decay_exped.sem, decay_exped.at(h, m + 1))
                            dve.scalar_tensor_tensor(nmat[:, m], ps[:, i, 0], hcv["Pk"][:, d, 2 * f + i:2 * f + i + 1],
                                                     decay[:, m], ALU.mult, ALU.mult).then_inc(scores_taken.sem, 1)
                    dve.wait_ge(scores_taken.sem, scores_taken.at(h, 6 * f + 2 * n))
                    for d in range(DIRS):
                        dve.tensor_tensor(dview[:, d, cs], ps[:, :, 1], dview[:, d, cs], ALU.mult).then_inc(scores_taken.sem, 1)
                def rg_piece(what, d):
                    if what == "silu_v":
                        dve.wait_ge(tanh_done.sem, tanh_done.at(h, 1))
                        silu(tanh_v, vT, vT)
                    elif what == "take_v":
                        for b in range(3):
                            dve.wait_ge(turned.sem, turned.at(h, 3 + b + 1))
                            dve.tensor_copy(vtok[:, 3 * b:3 * b + 3],
                                            banks[2 + b][:, 0:3 * P].rearrange("p (c d) -> p c d", d=P)).then_inc(turn_taken_v.sem, 1)
                    elif what == "u":
                        dve.wait_ge(rg_t_made.sem, rg_t_made.at(h, 3 * d + 3))
                        dve.scalar_tensor_tensor(RB, RC, 1.0, RB, ALU.add, ALU.mult).then_inc(rg_u_made.sem, 1)
                    elif what == "ix":
                        dve.wait_ge(gate_tanh.sem, gate_tanh.at(h, 6 * d + 6))
                        dve.scalar_tensor_tensor(RC, RC, 1.0, xf, ALU.add, ALU.mult).then_inc(rg_ix_made.sem, 1)
                    else:
                        dve.wait_ge(rg_bx_made.sem, rg_bx_made.at(h, d + 1))
                        out = RC if d else RH
                        way = (lambda a: a[:, P - 1::-1], lambda a: a[:, TW - 1:P + GAP - 1:-1]) if d else \
                            (lambda a: a[:, prompt], lambda a: a[:, sample])
                        for run, first in zip(way, (0.0, colsB[:, bd(B_ST + 8 * d + h, 1)])):
                            dve.tensor_tensor_scan(run(out), run(RA), run(RB), first, ALU.mult, ALU.add)\
                               .then_inc(rg_scanned.sem, 1)
                        dve.wait_ge(rg_scanned.sem, rg_scanned.at(h, 3 * d + 1))
                        end = 0 if d else P - 1
                        dve.tensor_copy(st_rg[:, d, bd(h, 1)], out[:, end:end + 1]).then_inc(rg_scanned.sem, 1)

                dve.wait_ge(scores_taken.sem, scores_taken.at(h, 28))
                dve.wait_ge(qd_made.sem, qd_made.at(h, 4))
                for q in range(4):
                    r = slice(BLK * q, BLK * q + BLK)
                    own.later(dve.tensor_copy(block_in[r, 0:INST, :], nmat[r, :, r]))
                own.settle()
                own(dve.transpose(sub[1].rearrange("p (c r) -> p c r", c=BLK), sub[0].rearrange("p (m c) -> p c m", c=BLK)))
                own(dve.transpose(sub[2].rearrange("p (r c) -> p c r", c=BLK), sub[0].rearrange("p (m c) -> p c m", c=BLK)))
                own(dve.tensor_scalar(sub[2], sub[2], pb, None, ALU.mult))
                own(dve.scalar_tensor_tensor(sub[1], sub[1], pf, sub[2], ALU.mult, ALU.add))
                own(dve.memset(sub[1][:, 0:SQ:BLK + 1], 1.0))
                for k in range(1, BLK - 1):
                    if k in RG_AT:
                        rg_piece(*RG_AT[k])
                    rows = BLK - 1 - k
                    tmp = view("sub_tmp", 0, rows * k).rearrange("p (a b) -> p a b", b=k)
                    own(dve.tensor_tensor(tmp, X[:, k + 1:, k:k + 1].to_broadcast([P, rows, k]),
                                          X[:, k:k + 1, 0:k].to_broadcast([P, rows, k]), ALU.mult))
                    own(dve.tensor_tensor(X[:, k + 1:, 0:k], X[:, k + 1:, 0:k], tmp, ALU.add))
                dve.transpose(sub[2].rearrange("p (m a) -> p a m", a=BLK), X).then_inc(unblocked.sem, 1)
                dve.transpose(sub[0].rearrange("p (m b) -> p b m", b=BLK), X.rearrange("p a b -> p b a"))\
                   .then_inc(unblocked.sem, 1)
                dve.wait_ge(unblocked.sem, unblocked.at(h, 2))
                for d in range(DIRS):
                    for q in range(4):
                        r = slice(BLK * q, BLK * q + BLK)
                        dve.tensor_copy(Z[r, NCH * d:NCH * d + NCH, r], (block_in if d else block_T)[r, NCH * d:NCH * d + NCH, :])\
                           .then_inc(Z_placed.sem, 1)
                for piece in RG_AFTER:
                    rg_piece(*piece)
                for g in range(6):
                    dve.wait_ge(Q_done.sem, Q_done.at(h, g + 1))
                    if g >= 2:
                        dve.wait_ge(dZ_done.sem, dZ_done.at(h, g - 1))
                    ps = banks[2 + 3 * (g % 2)][:, 0:3 * P].rearrange("p (m i) -> p m i", i=P)
                    dve.tensor_tensor(Qb[:, g % 2], ps, mask32[:, g // 3].unsqueeze(1).to_broadcast([P, 3, P]), ALU.mult)\
                       .then_inc(Q_taken.sem, 1)
                    if g >= 2 and not last:
                        if g == 2:
                            dve.wait_ge(proj_taken.sem, proj_taken.at(h, 9))
                        conv(0, RA, h + 1, g - 2)
                for g in range(6):
                    dve.wait_ge(Q_done.sem, Q_done.at(h, 6 + g + 1))
                    dve.wait_ge(dZ_done.sem, dZ_done.at(h, 6 + g - 1))
                    ps = banks[2 + 3 * (g % 2)][:, 0:3 * P].rearrange("p (m i) -> p m i", i=P)
                    r = slice(64, P) if g < 3 else slice(0, 64)
                    dve.tensor_scalar(Qb[r, g % 2], ps[r], -1.0, None, ALU.mult).then_inc(Q_taken.sem, 1)
                    if g >= 4:
                        t, x = (tanh_z, sz) if g == 4 else (tanh_g, sg)
                        dve.wait_ge(tanh_done.sem, tanh_done.at(h, g - 2))
                        silu(t, x, x)
                dve.wait_ge(v_scaled.sem, v_scaled.at(h, 1))
                def silu_k():
                    dve.wait_ge(tanh_done.sem, tanh_done.at(h, 5))
                    silu(kT, RA, kT)

                def next_taps(step):
                    if last:
                        return
                    for j, t in TAPS[step]:
                        if j == 2 and t == 3:
                            silu_k()
                        if t == 0:
                            dve.wait_ge(proj_taken.sem, proj_taken.at(h, 9 + 3 * j))
                        conv(j, (RA, RB, xf)[j], h + 1, t)
                    if step == 5:
                        dve.wait_ge(tanh_done.sem, tanh_done.at(h, 4))
                        silu(qT, RB, qT)

                for step in range(NCH):
                    chunk = (step, step if step == 0 else NCH - step)
                    if step:
                        for d in range(DIRS):
                            dve.wait_ge(KS_done.sem, KS_done.at(h, 2 * step - 2 + d + 1))
                            c1 = slice(chunk[d], chunk[d] + 1)
                            dve.scalar_tensor_tensor(rhs_v[:, d], banks[2 + d][:, 0:P], hcv["negeG"][:, d, c1],
                                                     vtok[:, chunk[d]], ALU.mult, ALU.add).then_inc(rhs_made.sem, 1)
                    if step == 0:
                        dve.wait_ge(stepped.sem, stepped.at(h, 2))
                        for d in range(DIRS):
                            dve.tensor_copy(S_new[:, d], banks[4 + d][:, 0:P]).then_inc(S_made.sem, 1)
                        dve.tensor_copy(o_tok[:, 0], banks[5][:, P:2 * P]).then_inc(o_made.sem, 1)
                        next_taps(step)
                        continue
                    for d in range(DIRS):
                        ch = chunk[d]
                        dve.wait_ge(stepped.sem, stepped.at(h, 2 * step + d + 1))
                        if step < NCH - 1:
                            if step == 1:
                                dve.wait_ge(S_in.sem, S_in.at(h, 0) * 16)
                            else:
                                dve.wait_ge(S_made.sem, S_made.at(h, 2 * step - 2 + d + 1))
                            dve.scalar_tensor_tensor(S[:, d], S[:, d], hcv["gl"][:, d, ch:ch + 1], banks[4 + d][:, 0:P],
                                                     ALU.mult, ALU.add).then_inc(S_made.sem, 1)
                        if step <= 4:
                            dve.tensor_copy(o_tok[:, ch], banks[4 + d][:, P:2 * P]).then_inc(o_made.sem, 1)
                        else:
                            dve.wait_ge(o_made.sem, o_made.at(h, 2 * step - 1))
                            dve.tensor_tensor(o_tok[:, ch], banks[4 + d][:, P:2 * P], o_tok[:, ch], ALU.add)\
                               .then_inc(o_made.sem, 1)
                    next_taps(step)
                dve.wait_ge(o_squared.sem, o_squared.at(h, NCH))
                dve.scalar_tensor_tensor(hcc["rstd"], hcc["sso"], 1.0 / P, hcc["epsq"], ALU.mult, ALU.add)\
                   .then_inc(o_meaned.sem, 1)
                dve.wait_ge(o_rooted.sem, o_rooted.at(h, 1))
                own(dve.reciprocal(hcc["rstd"], hcc["rstd"]))
                dve.tensor_tensor(o_tok, o_tok, hcc["rstd"].unsqueeze(2).to_broadcast([P, NCH, P]), ALU.mult)\
                   .then_inc(o_normed.sem, 1)
                for b, bank, a, to, z0, n in ((0, 6, 0, 0, 0, P), (0, 6, P, P, P + GAP, 2 * P),
                                              (1, 7, 0, 3 * P, 3 * P + GAP, 3 * P), (2, 5, 0, 6 * P, 6 * P + GAP, 3 * P)):
                    dve.wait_ge(o_turned.sem, o_turned.at(h, b + 1))
                    dve.scalar_tensor_tensor(oz[:, to:to + n], banks[bank][:, a:a + n], colsB[:, B_NW:B_NW + 1],
                                             sz[:, z0:z0 + n], ALU.mult, ALU.mult).then_inc(oz_made.sem, 1)
                own.clear()
                dve.wait_ge(prompt_S_stored.sem, prompt_S_stored.at(h, 1) * 16)

            with dve.Fori(0, HEADS - 1) as h:
                head(h)
            head(HEADS - 1, last=True)
            dve.wait_ge(states_turned, 1)
            dve.tensor_copy(hc[0:16, 0:P], banks[7][0:16, 0:P]).then_inc(states_taken, 1)

            def y_tile(buf, n, s):
                first = isinstance(n, int) and n < 2
                ss = lambda i: y_ss[:, 4 * buf + i:4 * buf + i + 1]
                dve.wait_ge(y_squared, 2 * n + 2)
                own(dve.tensor_tensor(ss(2), ss(0), ss(1), ALU.add))
                dve.tensor_scalar(ss(2), ss(2), 1.0 / D, EPS, ALU.mult, ALU.add).then_inc(y_meaned, 1)
                dve.wait_ge(y_rooted, n + 1)
                own(dve.reciprocal(ss(3), ss(2)))
                if not first:
                    dve.wait_ge(y_stored[buf], 8 * n if buf == 0 else 8 * n - 8)
                for half in range(2):
                    cc = slice(512 * half, 512 * half + 512)
                    own.later(dve.scalar_tensor_tensor(y_out[:, buf, cc], banks[2 * buf + half][:, :], ss(3),
                                                       gate_post[:, s, cc], ALU.mult, ALU.mult))
                own.settle()
                if isinstance(n, int) and n == 0:
                    dve.wait_ge(xr_in[0], 16)
                else:
                    dve.wait_ge(xr_added, n)
                dve.tensor_tensor(y_out[:, buf], y_out[:, buf], x_res[:, buf], ALU.add).then_inc(y_made, 1)

            dve.wait_ge(gate_post_made, 2)
            y_tile(0, 0, 0)
            y_tile(1, 1, 1)
            own.clear()
            with dve.Fori(0, 3) as i:
                y_tile(0, 2 * i + 2, 1)
                y_tile(1, 2 * i + 3, 1)
                own.clear()
            y_tile(0, 8, 1)


_INS = ["x_prompt", "x_sample", "state_delta", "state_rglru", "c", "c_ctx", "ada_w", "ada_b", "pre_norm_w",
        "post_norm_w", "w_in", "w_out", "dn_conv_w", "dn_a_log", "dn_dt_bias", "dn_norm_w", "rg_conv_w", "rg_conv_b",
        "rg_w_r", "rg_b_r", "rg_w_i", "rg_b_i", "rg_lam"]
_OUTS = [("y_prompt", (1, P, D)), ("y_sample", (1, TOK - P, D)), ("new_delta", (1, 1, DIRS, HEADS, P, P)),
         ("new_rglru", (1, 1, DIRS, D))]


def positions():
    quarter, width = D // 4, 64
    freqs = np.exp(np.float32(-math.log(10000.0)) * np.arange(quarter, dtype=np.float32) / np.float32(quarter))
    table = []
    for n in ((TOK - P) // width, width):
        angle = np.arange(n, dtype=np.float32)[:, None] * freqs[None]
        table.append(np.concatenate([np.sin(angle), np.cos(angle)], axis=1).astype(np.float32))
    return table


def build(nc):
    shapes = {
        "x_prompt": (1, P, D), "x_sample": (1, TOK - P, D), "state_delta": (1, 1, DIRS, HEADS, P, P),
        "state_rglru": (1, 1, DIRS, D), "c": (1, D), "c_ctx": (D,), "ada_w": (1, D, 3 * D), "ada_b": (1, 3 * D),
        "pre_norm_w": (1, D), "post_norm_w": (1, D), "w_in": (1, D, OFF_RG + D), "w_out": (1, 2 * D, D),
        "dn_conv_w": (1, 4, 3 * D), "dn_a_log": (1, DIRS, HEADS), "dn_dt_bias": (1, DIRS, HEADS), "dn_norm_w": (1, P),
        "rg_conv_w": (1, 4, D), "rg_conv_b": (1, D), "rg_w_r": (1, DIRS, HEADS, P, P), "rg_b_r": (1, DIRS, D),
        "rg_w_i": (1, DIRS, HEADS, P, P), "rg_b_i": (1, DIRS, D), "rg_lam": (1, DIRS, D)}
    args = [nc.dram_tensor(n, shapes[n], F32, kind="ExternalInput").ap() for n in _INS]
    args += [nc.dram_tensor(n, s, F32, kind="ExternalInput").ap() for n, s in (("pos_row", (16, 512)), ("pos_col", (64, 512)))]
    args += [nc.dram_tensor(n, s, F32, kind="ExternalOutput").ap() for n, s in _OUTS]
    hybrid_layer(nc, *args)


def kernel(**inputs):
    import concourse.bacc as bacc
    from concourse.bass_utils import run_bass_kernel_spmd

    nc = bacc.Bacc("TRN2", target_bir_lowering=False, num_devices=1)
    arrays = {n: np.ascontiguousarray(inputs[n]) for n in _INS}
    arrays["pos_row"], arrays["pos_col"] = positions()
    build(nc)
    got = run_bass_kernel_spmd(nc, [arrays], core_ids=[0]).results[0]
    return tuple(got[n] for n, _ in _OUTS)
```

```python
import math
from contextlib import ExitStack

import numpy as np

import concourse.bass as bass
from concourse import mybir

ALU = mybir.AluOpType
ACT = mybir.ActivationFunctionType
AX = mybir.AxisListType
F32 = mybir.dt.float32
F32R = mybir.dt.float32r

P = 128
D = 1024
KT = D // P
HEADS = 8
NCH = 9
TOK = NCH * P
GAP = 2
TW = TOK + GAP
RAW = 2 + TW + 1
GROUPS = [(0, 386), (386, 384), (770, 384)]
DIRS = 2
INST = DIRS * NCH
OFF_B = 4 * D
OFF_RX = OFF_B + 4 * HEADS
OFF_RG = OFF_RX + D
EPS = 1e-6
MASKED = -1e30
BLK = 32
SQ = BLK * BLK


LEVEL_FILLS = [3] * 6 + [2, 2, 2, 2, 1, 1]
SCAN_FILLS = [3, 3, 3, 3, 3, 3, 3, 3, 3]
BEFORE_JOINS = 79
assert BEFORE_JOINS + sum(LEVEL_FILLS) + sum(SCAN_FILLS) + 10 == 6 * 3 * KT


MOD_V = 5


def col(c):
    return 0 if c == 0 else GAP + P * c


class Count:

    def __init__(self, sem, before, per_head):
        self.sem, self.before, self.per_head = sem, before, per_head

    def at(self, head, n):
        return head * self.per_head + (self.before + n)


class Chain:

    def __init__(self, engine, sem):
        self.engine, self.sem, self.n = engine, sem, 0

    def __call__(self, instruction):
        self.later(instruction)
        self.settle()

    def later(self, instruction):
        instruction.then_inc(self.sem, 1)
        self.n += 1

    def settle(self):
        self.engine.wait_ge(self.sem, self.n)

    def clear(self):
        self.settle()
        self.engine.sem_clear(self.sem)
        self.n = 0


def hybrid_layer(nc, x_prompt, x_sample, state_delta, state_rglru, c, c_ctx, ada_w, ada_b, pre_norm_w,
                 post_norm_w, w_in, w_out, dn_conv_w, dn_a_log, dn_dt_bias, dn_norm_w, rg_conv_w, rg_conv_b,
                 rg_w_r, rg_b_r, rg_w_i, rg_b_i, rg_lam, pos_row, pos_col,
                 y_prompt, y_sample, new_delta, new_rglru):
    ctx = ExitStack()
    with ctx:
        def sem(name):
            return ctx.enter_context(nc.semaphore(name))

        sizes = {
            "hT": KT * TW, "w": 3 * KT * P, "raw": 4 * RAW, "kq": 2 * TW, "vT": TW, "xf": TW, "decay": 2 * TOK,
            "nmat": 2 * TOK, "ktok": TOK, "vtok": TW, "sub": 3 * SQ, "sub_tmp": 256, "Z": INST * P,
            "Q": 2 * 3 * P, "qd": 2 * TOK, "Zt": INST * P, "sz": TW, "sg": TW, "rg": 4 * TW,
            "scan_tmp": 6 * P, "S": 2 * P, "S_new": 2 * P, "wg": 4 * P, "tri": 2 * P, "ones": P,
            "mask32": 2 * P, "colsA": P, "colsB": P, "ba": NCH * 32, "cum": NCH * 16, "tot": NCH * 16,
            "beta": NCH * 16, "eG": NCH * 16, "edec": NCH * 16, "gl": NCH * 16,
            "ident": P, "head_cols": 16 * 20,
            "small": 96,
        }
        total = sum(sizes.values())
        W_WORDS, OT_WORDS = 2 * HEADS * D, 2 * 2 * HEADS * P
        with nc.sbuf_tensor("arena", [P, total], F32) as arena:
            pass
        with nc.sbuf_tensor("wo", [P, W_WORDS], F32) as wo:
            pass
        wo_lo, wo_hi = (ctx.enter_context(nc.sbuf_tensor(n, [P, W_WORDS], F32R)) for n in ("wo_lo", "wo_hi"))
        with nc.sbuf_tensor("ot", [P, OT_WORDS], F32) as ot:
            pass
        ot_lo, ot_hi = (ctx.enter_context(nc.sbuf_tensor(n, [P, OT_WORDS], F32R)) for n in ("ot_lo", "ot_hi"))
        at, off = {}, 0
        for name, n in sizes.items():
            at[name] = off
            off += n

        def view(name, start=0, n=None):
            n = sizes[name] - start if n is None else n
            return arena[:, at[name] + start:at[name] + start + n]

        hT = view("hT").rearrange("p (k t) -> p k t", k=KT)
        w_ring = view("w").rearrange("p (s k n) -> p s k n", s=3, k=KT)
        raw = view("raw").rearrange("p (j t) -> p j t", j=4)
        kq = view("kq").rearrange("p (j t) -> p j t", j=2)
        kT, qT = kq[:, 0], kq[:, 1]
        vT = view("vT")
        xf = view("xf")
        decay = view("decay").rearrange("p (m i) -> p m i", i=P)
        nmat = view("nmat").rearrange("p (m i) -> p m i", i=P)
        ktok = view("ktok").rearrange("p (c d) -> p c d", d=P)
        vtok = view("vtok", 0, TOK).rearrange("p (c d) -> p c d", d=P)
        sub = [view("sub", i * SQ, SQ) for i in range(3)]
        block_in, block_T = (s.rearrange("p (m c) -> p m c", c=BLK) for s in (sub[0], sub[2]))
        Z = view("Z").rearrange("p (m i) -> p m i", i=P)
        Zt = view("Zt").rearrange("p (m i) -> p m i", i=P)
        Qb = view("Q").rearrange("p (b m i) -> p b m i", b=2, i=P)
        qd = view("qd").rearrange("p (d t) -> p d t", d=2)
        sz, sg = view("sz"), view("sg")
        eG_rows = view("sub", 0, 2 * TOK).rearrange("p (d t) -> p d t", d=2)
        tanh_v = view("vtok")
        tanh_z, tanh_g = view("sub", 0, TW), view("sub", TW, TW)
        RA, RB, RC, RH = (view("rg", i * TW, TW) for i in range(4))
        rhs_v = view("scan_tmp", 0, 2 * P).rearrange("p (d v) -> p d v", d=2)
        vt = view("scan_tmp", 2 * P, 2 * P).rearrange("p (d v) -> p d v", d=2)
        vd = view("scan_tmp", 4 * P, 2 * P).rearrange("p (d v) -> p d v", d=2)
        S = view("S").rearrange("p (d v) -> p d v", d=2)
        S_new = view("S_new").rearrange("p (d v) -> p d v", d=2)
        wg = view("wg").rearrange("p (n j) -> p n j", n=4)
        ident, ones = view("ident"), view("ones")
        tri = view("tri").rearrange("p (d i) -> p d i", d=2)
        mask32 = view("mask32").rearrange("p (d i) -> p d i", d=2)
        colsA, colsB = view("colsA"), view("colsB")
        ba = view("ba").rearrange("p (c n) -> p c n", n=32)
        cols = {n: view(n).rearrange("p (c n) -> p c n", n=16) for n in ("cum", "tot", "beta", "eG", "edec", "gl")}
        o_tok = vT[:, 0:TOK].rearrange("p (c d) -> p c d", d=P)
        hc = view("head_cols")
        small = view("small")
        oz = view("Zt", 0, TOK)
        hcv = {n: hc[:, i * 20:i * 20 + INST].rearrange("p (d c) -> p d c", d=2)
               for i, n in enumerate(("ncum", "negeG", "Pk", "Pdec", "gl"))}
        hcc = {n: hc[:, 100 + i * 10:100 + i * 10 + NCH]
               for i, n in enumerate(("ssk", "ssq", "rk2", "rkinv", "sso", "rstd", "epsq"))}
        st_rg = hc[:, 244:260].rearrange("p (d b) -> p d b", b=8)
        rg_tab = hc[:, 180:244].rearrange("p (n b) -> p n b", b=8)
        rg_cols = hc[:, 262:270]
        clear_mark = hc[:, 270:271]
        br_h, bi_h, c8_h, nc8_h = (rg_cols[:, 2 * i:2 * i + 2] for i in range(4))
        pf, pb = hc[:, 260:261], hc[:, 261:262]
        convw = colsA[:, 0:96].rearrange("p (j t) -> p j t", j=4)
        rconvw = colsA[:, 96:128].rearrange("p (j t) -> p j t", j=4)
        B_C, B_PRE, B_CB, B_BR, B_BI, B_LAM, B_ST, B_NW, B_ROWS = 0, 16, 24, 32, 48, 64, 80, 96, 97

        base = [at["raw"]]

        def early(n):
            base[0] += n
            return arena[:, base[0] - n:base[0]]

        adaw = early(KT * 3 * D).rearrange("p (k n) -> p k n", k=KT)
        mod_row, ada_brow = early(3 * D), early(3 * D)
        x_in = early(2 * D).rearrange("p (b n) -> p b n", b=2)
        pos = early(2 * D).rearrange("p (b n) -> p b n", b=2)
        rowsA, rowsB = early(P), early(P)
        assert base[0] <= at["wg"]
        square_out = view("w", KT * P, KT * P)
        base[0] = at["kq"]
        baT, G_rows = early(TW), early(2 * TOK).rearrange("p (d t) -> p d t", d=2)
        N_SP = NCH * 16 + 16
        sp_y, sp_e, sp_z, sp_z2, sp_p, sp_r = (early(N_SP) for _ in range(6))
        dt_bias, a_log = small[:, 56:72], small[:, 72:88]
        mod_ab = small[:, 0:32].rearrange("p (s k) -> p s k", s=4)
        silu_c = small[:, 32:48].rearrange("p (s k) -> p s k", s=2)
        x_ss = small[:, 48:50]

        banks = [ctx.enter_context(nc.psum_tensor(f"bank{i}", [P, 512], F32)) for i in range(8)]
        scr_G = nc.dram_tensor("scr_G", (DIRS, HEADS, TOK), F32, kind="Internal").ap()
        scr_o = nc.dram_tensor("scr_o", (2 * HEADS, P, TOK), F32, kind="Internal").ap()
        scr_gate = nc.dram_tensor("scr_gate", (2, D), F32, kind="Internal").ap()

        rows_in, consts_in, pos_in, ba_w_in = sem("rows_in"), sem("consts_in"), sem("pos_in"), sem("ba_w_in")
        ada_in = [sem(f"ada_in{k}") for k in range(KT)]
        consts_made = sem("consts_made")
        cols_turned, cols_made, silu_c_made = sem("cols_turned"), sem("cols_made"), sem("silu_c_made")
        ada_done, mod_row_made, mod_turned, mod_made = sem("ada_done"), sem("mod_row_made"), sem("mod_turned"), sem("mod_made")
        gate_stored = sem("gate_stored")
        x_loaded = [sem("x_loaded0"), sem("x_loaded1")]
        x_added, x_squared, x_meaned, x_rooted = sem("x_added"), sem("x_squared"), sem("x_meaned"), sem("x_rooted")
        x_normed, x_turned, h_made_v, h_made_a = sem("x_normed"), sem("x_turned"), sem("h_made_v"), sem("h_made_a")
        h_modded_v, h_modded_a = sem("h_modded_v"), sem("h_modded_a")
        ba_done, baT_made, ba_turned, ba_made = sem("ba_done"), sem("baT_made"), sem("ba_turned"), sem("ba_made")
        sp_ready, sp_exped, g_made, G_summed, G_taken = sem("sp_ready"), sem("sp_exped"), sem("g_made"), sem("G_summed"), sem("G_taken")
        G_exp_in, G_exped, Grow_done, G_stored = sem("G_exp_in"), sem("G_exped"), sem("Grow_done"), sem("G_stored")
        grounds_made, c_tanh, cols_ready = sem("grounds_made"), sem("c_tanh"), sem("cols_ready")
        Zt_cleared = Count(sem("Zt_cleared"), 1, 1)
        v_own, a_own, g_own = sem("v_own"), sem("a_own"), sem("g_own")

        w_in_slot = [Count(sem("w_slot0"), 1, 2), Count(sem("w_slot1"), 1, 2), Count(sem("w_slot2"), 2, 2)]
        projected = Count(sem("projected"), 12, 18)
        proj_taken = Count(sem("proj_taken"), 12, 18)
        conv_done = Count(sem("conv_done"), 3, 4)
        tanh_done = Count(sem("tanh_done"), 2, 5)
        silu_done = Count(sem("silu_done"), 2, 5)
        turned = Count(sem("turned"), 3, 9)
        turn_taken_a = Count(sem("turn_taken_a"), 0, 21)
        turn_taken_v = Count(sem("turn_taken_v"), 0, 3)
        ss_done = Count(sem("ss_done"), 0, 2)
        rk_root = Count(sem("rk_root"), 0, 1)
        v_scaled = Count(sem("v_scaled"), 0, 1)
        decay_in = Count(sem("decay_in"), 2, 2)
        S_in = Count(sem("S_in"), 2, 2)
        wg_in = Count(sem("wg_in"), 4, 4)
        eG_row = Count(sem("eG_row"), 1, 1)
        head_cols_made = Count(sem("head_cols_made"), 4, 4)
        masked = Count(sem("masked"), 2, 2)
        decay_exped = Count(sem("decay_exped"), 0, INST)
        qd_made = Count(sem("qd_made"), 0, 4)
        gated = Count(sem("gated"), 0, 12)
        gate_tanh = Count(sem("gate_tanh"), 0, 12)
        rg_t_made = Count(sem("rg_t_made"), 0, 6)
        rg_u_made = Count(sem("rg_u_made"), 0, 2)
        rg_root = Count(sem("rg_root"), 0, 2)
        rg_ix_made = Count(sem("rg_ix_made"), 0, 2)
        rg_bx_made = Count(sem("rg_bx_made"), 0, 2)
        rg_scanned = Count(sem("rg_scanned"), 0, 6)
        rg_stored = Count(sem("rg_stored"), 0, 2)
        scored = Count(sem("scored"), 0, 5)
        scores_taken = Count(sem("scores_taken"), 0, 28)
        unblocked = Count(sem("unblocked"), 0, 2)
        Z_placed = Count(sem("Z_placed"), 0, 8)
        Zt_placed = Count(sem("Zt_placed"), 0, 8)
        Q_done = Count(sem("Q_done"), 0, 12)
        Q_taken = Count(sem("Q_taken"), 0, 12)
        dZ_done = Count(sem("dZ_done"), 0, 12)
        dZ_taken = Count(sem("dZ_taken"), 0, 30)
        KS_done = Count(sem("KS_done"), 0, 16)
        rhs_made = Count(sem("rhs_made"), 0, 16)
        solved = Count(sem("solved"), 0, 18)
        vnew_made = Count(sem("vnew_made"), 0, 36)
        S_done = Count(sem("S_done"), 0, 16)
        stepped = Count(sem("stepped"), 0, 18)
        S_made = Count(sem("S_made"), 0, 16)
        o_made = Count(sem("o_made"), 0, 17)
        prompt_S_stored = Count(sem("prompt_S_stored"), 0, 1)
        o_squared = Count(sem("o_squared"), 0, NCH)
        o_meaned = Count(sem("o_meaned"), 0, 1)
        o_rooted = Count(sem("o_rooted"), 0, 1)
        o_normed = Count(sem("o_normed"), 0, 1)
        o_turned = Count(sem("o_turned"), 0, 3)
        oz_made = Count(sem("oz_made"), 1, 4)
        oz_stored = Count(sem("oz_stored"), 0, 1)
        w_out_in = [sem(f"w_out_in{i}") for i in range(4)]
        wo_hi_made, wo_lo_made, ot_hi_made, ot_lo_made = (sem(n) for n in ("wo_hi_made", "wo_lo_made", "ot_hi_made", "ot_lo_made"))
        post_in, gate_post_made, states_stored = sem("post_in"), sem("gate_post_made"), sem("states_stored")
        states_turned, states_taken = sem("states_turned"), sem("states_taken")
        ot_in = [sem("ot_in0"), sem("ot_in1")]
        xr_in = [sem("xr_in0"), sem("xr_in1")]
        xr_added, y_done, y_squared, y_meaned, y_rooted, y_made, raw_cleared = (
            sem(n) for n in ("xr_added", "y_done", "y_squared", "y_meaned", "y_rooted", "y_made", "raw_cleared"))
        y_stored = [sem("y_stored0"), sem("y_stored1")]

        assert W_WORDS <= at["kq"]
        wo, wo_lo, wo_hi = (t[:, :].rearrange("p (k n) -> p k n", n=D) for t in (wo, wo_lo, wo_hi))
        ot, ot_lo, ot_hi = (t[:, :].rearrange("p (b n) -> p b n", b=2) for t in (ot, ot_lo, ot_hi))
        base[0] = 2 * (W_WORDS + OT_WORDS)
        x_res = early(2 * D).rearrange("p (b n) -> p b n", b=2)
        pos_row_res = early(D).rearrange("p (b n) -> p b n", b=2)
        pos_col_res = early(D // 2)
        y_out = early(2 * D).rearrange("p (b n) -> p b n", b=2)
        gate_post = early(2 * D).rearrange("p (b n) -> p b n", b=2)
        post_b = y_junk = early(D)
        assert base[0] <= at["ident"]
        y_ss = small[:, 0:8]

        SECTION = {"z": 3 * D, "gate": OFF_RG, "k": D, "q": 0, "v": 2 * D, "rx": OFF_RX}
        TILES = ["z", "gate", "k", "q", "rx", "v"]
        w_in2, w_out2 = w_in[0], w_out[0]
        bd = bass.ds

        def w_tile(name, head):
            return w_in2[:, bd(P * (head + SECTION[name] // P) + SECTION[name] % P, P)].rearrange("(k p) n -> p k n", p=P)

        block = ctx.enter_context(nc.Block())

        @block.sync
        def _(sp):
            sp.dma_start(rowsA[0:96, :], dn_conv_w[0].rearrange("j (t p) -> (j t) p", p=P)).then_inc(rows_in, 16)
            sp.dma_start(rowsA[96:128, :], rg_conv_w[0].rearrange("j (t p) -> (j t) p", p=P)).then_inc(rows_in, 16)
            for first, src in ((B_C, c_ctx.rearrange("(k p) -> k p", p=P)), (B_C + 8, c[0].rearrange("(k p) -> k p", p=P)),
                               (B_PRE, pre_norm_w[0].rearrange("(k p) -> k p", p=P)),
                               (B_CB, rg_conv_b[0].rearrange("(k p) -> k p", p=P)),
                               (B_BR, rg_b_r[0].rearrange("d (k p) -> (d k) p", p=P)),
                               (B_BI, rg_b_i[0].rearrange("d (k p) -> (d k) p", p=P)),
                               (B_LAM, rg_lam[0].rearrange("d (k p) -> (d k) p", p=P)),
                               (B_ST, state_rglru[0, 0].rearrange("d (k p) -> (d k) p", p=P)),
                               (B_NW, dn_norm_w)):
                sp.dma_start(rowsB[first:first + src.shape[0], :], src).then_inc(rows_in, 16)
            def load_ada(k):
                sp.dma_start(adaw[:, k, :], ada_w[0, k * P:(k + 1) * P, :]).then_inc(ada_in[k], 16)

            sp.dma_start(x_in[:, 0], x_prompt[0]).then_inc(x_loaded[0], 16)

            def load_x(buf, xs, ps, tile, s):
                sp.dma_start(xs[:, buf], x_sample[0, bd(P * tile, P), :]).then_inc(s[buf], 16)
                for half in range(2):
                    sp.dma_start(ps[64 * half:64 * half + 64, buf, 0:512],
                                 pos_row[bd(2 * tile + half, 1), :].to_broadcast([64, 512])).then_inc(s[buf], 16)

            load_x(1, x_in, pos, 0, x_loaded)
            load_ada(0)
            for b in range(2):
                for half in range(2):
                    sp.dma_start(pos[64 * half:64 * half + 64, b, 512:], pos_col).then_inc(pos_in, 16)
            load_ada(1)
            sp.dma_start(ada_brow[0:2, :], ada_b.to_broadcast([2, 3 * D])).then_inc(consts_in, 16)
            sp.dma_start(dt_bias, dn_dt_bias.rearrange("l d h -> l (d h)").to_broadcast([P, 16])).then_inc(consts_in, 16)
            sp.dma_start(a_log, dn_a_log.rearrange("l d h -> l (d h)").to_broadcast([P, 16])).then_inc(consts_in, 16)
            load_ada(2)
            for t in range(2, NCH):
                sp.wait_ge(x_turned, 2 * t - 2)
                load_x(t % 2, x_in, pos, t - 1, x_loaded)
                if t + 1 < KT:
                    load_ada(t + 1)
            sp.wait_ge(x_turned, 2 * NCH)
            sp.dma_start(w_ring[:, 0, :, 0:32], w_in2[:, OFF_B:OFF_RX].rearrange("(k p) n -> p k n", p=P)).then_inc(ba_w_in, 16)
            sp.wait_ge(mod_row_made, 6)
            sp.dma_start(scr_gate, mod_row[0:2, 2 * D:]).then_inc(gate_stored, 16)

            def load_w(slot, name, head):
                sp.dma_start(w_ring[:, slot], w_tile(name, head)).then_inc(w_in_slot[slot].sem, 16)

            load_w(2, "k", 0)
            sp.wait_ge(x_squared, NCH)
            load_w(1, "rx", 0)
            sp.wait_ge(ba_done, 1)
            load_w(0, "q", 0)
            sp.wait_ge(projected.sem, 3)
            load_w(2, "v", 0)
            sp.wait_ge(projected.sem, 6)
            load_w(0, "z", 0)

            g_rows = nmat.rearrange("p (d c) i -> p d (c i)", d=2)

            def load_rows(head):
                for d in range(DIRS):
                    sp.dma_start(g_rows[:, d], scr_G[d, bd(head, 1), :].to_broadcast([P, TOK])).then_inc(decay_in.sem, 16)

            def load_states(head):
                for d in range(DIRS):
                    sp.dma_start(S[:, d], state_delta[0, 0, d, bd(head, 1)].rearrange("a k v -> (a k) v"))\
                      .then_inc(S_in.sem, 16)

            def load_gates(head):
                for n, src in enumerate((rg_w_r[0, 0], rg_w_r[0, 1], rg_w_i[0, 0], rg_w_i[0, 1])):
                    sp.dma_start(wg[:, n], src[bd(head, 1)].rearrange("a k j -> (a k) j")).then_inc(wg_in.sem, 16)

            load_gates(0)
            for d in range(DIRS):
                sp.wait_ge(G_taken, 5 + 3 * d)
                sp.dma_start(scr_G[d], G_rows[0:HEADS, d]).then_inc(G_stored, 16)
            sp.wait_ge(G_stored, 32)
            load_rows(0)
            sp.wait_ge(projected.sem, 9)
            load_w(1, "gate", 0)
            load_states(0)

            def head_loads(h):
                def load_tile(j):
                    sp.wait_ge(projected.sem, projected.at(h, 3 * (j if j > 1 else j + 6) - 6))
                    load_w(j % 3, TILES[j], h + 1)

                load_tile(2)
                load_tile(3)
                sp.wait_ge(gated.sem, gated.at(h, 12))
                load_gates(h + 1)
                load_tile(4)
                load_tile(5)
                sp.wait_ge(Q_done.sem, Q_done.at(h, 12))
                load_rows(h + 1)
                load_tile(0)
                load_tile(1)
                sp.wait_ge(stepped.sem, stepped.at(h, 18))
                load_states(h + 1)

            with sp.Fori(0, HEADS - 1) as h:
                head_loads(h)
            h = HEADS - 1
            sp.wait_ge(projected.sem, projected.at(h, 6))
            sp.wait_ge(conv_done.sem, conv_done.at(h, 1))
            for q in range(4):
                sp.dma_start(wo[:, 4 * q:4 * q + 4, :],
                             w_out2[512 * q:512 * q + 512, :].rearrange("(k p) n -> p k n", p=P)).then_inc(w_out_in[q], 16)
            sp.wait_ge(oz_stored.sem, 16 * oz_stored.at(h, 1))
            sp.wait_ge(rg_stored.sem, 16 * rg_stored.at(h, 2))
            sp.wait_ge(prompt_S_stored.sem, 16 * prompt_S_stored.at(h, 1))

            def load_o(buf, tile):
                sp.dma_start(ot[:, buf].rearrange("p (k t) -> p k t", k=16),
                             scr_o[:, :, bd(P * tile, P)].rearrange("k p t -> p k t")).then_inc(ot_in[buf], 16)

            load_o(0, 0)
            load_o(1, 1)
            for s in range(2):
                sp.dma_start(gate_post[:, s], scr_gate[s:s + 1, :].to_broadcast([P, D])).then_inc(post_in, 16)
            sp.dma_start(post_b, post_norm_w.to_broadcast([P, D])).then_inc(post_in, 16)
            for half in range(2):
                sp.dma_start(pos_col_res[64 * half:64 * half + 64, :], pos_col).then_inc(post_in, 16)
            sp.dma_start(x_res[:, 0], x_prompt[0]).then_inc(xr_in[0], 16)
            load_x(1, x_res, pos_row_res, 0, xr_in)
            sp.wait_ge(states_taken, 1)
            sp.dma_start(new_rglru[0, 0].rearrange("d (b p) -> (d b) p", p=P), hc[0:16, 0:P]).then_inc(states_stored, 16)
            sp.wait_ge(y_made, 1)
            sp.dma_start(y_prompt[0], y_out[:, 0]).then_inc(y_stored[0], 16)
            load_o(0, 2)
            load_x(0, x_res, pos_row_res, 1, xr_in)

            def store_y(buf, tile):
                sp.dma_start(y_sample[0, bd(P * tile, P), :], y_out[:, buf]).then_inc(y_stored[buf], 16)

            with sp.Fori(0, 3) as i:
                sp.wait_ge(y_made, 2 * i + 2)
                store_y(1, 2 * i)
                load_o(1, 2 * i + 3)
                load_x(1, x_res, pos_row_res, 2 * i + 2, xr_in)
                sp.wait_ge(y_made, 2 * i + 3)
                store_y(0, 2 * i + 1)
                load_o(0, 2 * i + 4)
                load_x(0, x_res, pos_row_res, 2 * i + 3, xr_in)
            sp.wait_ge(y_made, 8)
            store_y(1, 6)
            sp.wait_ge(y_made, 9)
            store_y(0, 7)
            sp.wait_ge(y_stored[0], 16 * 5)
            sp.wait_ge(y_stored[1], 16 * 4)
            sp.wait_ge(states_stored, 16)
            sp.wait_ge(prompt_S_stored.sem, 16 * HEADS)

        @block.gpsimd
        def _(gp):
            own = Chain(gp, g_own)
            own(gp.memset(ident, 0.0))
            own(gp.affine_select(out=ident, in_=ident, compare_op=ALU.not_equal, fill=1.0, base=0,
                                 pattern=[[-1, P]], channel_multiplier=1))
            own(gp.memset(tri, 1.0))
            own(gp.affine_select(out=tri[:, 0], in_=tri[:, 0], compare_op=ALU.is_ge, fill=0.0, base=0,
                                 pattern=[[1, P]], channel_multiplier=-1))
            own(gp.affine_select(out=tri[:, 1], in_=tri[:, 1], compare_op=ALU.is_ge, fill=0.0, base=0,
                                 pattern=[[-1, P]], channel_multiplier=1))
            own(gp.memset(ones, 1.0))
            own(gp.memset(mask32, 0.0))
            for d in range(DIRS):
                for b in (0, 2):
                    r, cc = (b + 1, b) if d == 0 else (b, b + 1)
                    own(gp.memset(mask32[BLK * r:BLK * r + BLK, d, BLK * cc:BLK * cc + BLK], -1.0))
            gp.memset(hT[:, :, P:P + GAP], 0.0).then_inc(consts_made, 1)

            gp.wait_ge(ada_done, 6)
            gp.memset(raw, 0.0).then_inc(raw_cleared, 1)
            own(gp.memset(sub[0], 0.0))
            gp.memset(Z, 0.0).then_inc(grounds_made, 1)
            gp.wait_ge(mod_turned, 1)
            gp.wait_ge(gate_stored, 16)
            gp.memset(Zt, 0.0).then_inc(Zt_cleared.sem, 1)
            gp.wait_ge(cols_ready, 1)

            dview = decay.rearrange("p (d c) i -> p d c i", d=2)
            nview = nmat.rearrange("p (d c) i -> p d c i", d=2)
            chv = {n: cols[n].rearrange("p c (d h) -> p h d c", d=2) for n in ("cum", "eG", "gl")}
            runs = [(0, 0, P), (P, P + GAP, TOK - P)]

            def prepare(h):
                for n, to in (("cum", "ncum"), ("eG", "negeG"), ("gl", "gl")):
                    gp.tensor_copy(hcv[to], chv[n][:, bd(h, 1)].rearrange("p a d c -> p (a d) c"))\
                      .then_inc(head_cols_made.sem, 1)
                gp.tensor_copy(rg_cols, rg_tab[:, :, bd(h, 1)].rearrange("p n a -> p (n a)")).then_inc(head_cols_made.sem, 1)

            def mask(d):
                s = 1 if d == 0 else -1
                gp.affine_select(out=dview[:, d], in_=nview[:, d], compare_op=ALU.is_ge, fill=MASKED, base=0,
                                 pattern=[[0, NCH], [s, P]], channel_multiplier=-s).then_inc(masked.sem, 1)

            def head(h, last=False):
                gp.wait_ge(silu_done.sem, silu_done.at(h, -1))
                gp.wait_ge(eG_row.sem, eG_row.at(h, 0))
                for d in range(DIRS):
                    for a, b, n in runs:
                        gp.tensor_tensor(qd[:, d, a:a + n], eG_rows[:, d, a:a + n], qT[:, b:b + n], ALU.mult)\
                          .then_inc(qd_made.sem, 1)
                for d in range(DIRS):
                    gp.wait_ge(rg_root.sem, rg_root.at(h, d + 1))
                    gp.wait_ge(rg_ix_made.sem, rg_ix_made.at(h, d + 1))
                    gp.tensor_tensor(RB, RB, RC, ALU.mult).then_inc(rg_bx_made.sem, 1)
                    if d == 0:
                        gp.wait_ge(rk_root.sem, rk_root.at(h, 1))
                        gp.wait_ge(turn_taken_v.sem, turn_taken_v.at(h, 3))
                        gp.tensor_tensor(vtok, vtok, hcc["rkinv"].unsqueeze(2).to_broadcast([P, NCH, P]), ALU.mult)\
                          .then_inc(v_scaled.sem, 1)
                gp.wait_ge(rg_scanned.sem, rg_scanned.at(h, 6))
                own(gp.tensor_tensor(RH, RH, RC, ALU.add))
                gp.wait_ge(silu_done.sem, silu_done.at(h, 3))
                own(gp.tensor_tensor(RH, RH, sg, ALU.mult))
                for a, b, n in runs:
                    gp.dma_start(scr_o[bd(h + HEADS, 1), :, a:a + n].rearrange("a p t -> (a p) t"), RH[:, b:b + n])\
                      .then_inc(rg_stored.sem, 16)
                gp.wait_ge(S_made.sem, S_made.at(h, 2))
                gp.dma_start(new_delta[0, 0, :, bd(h, 1)].rearrange("d a k v -> k (d a) v"), S_new)\
                  .then_inc(prompt_S_stored.sem, 16)
                if not last:
                    gp.wait_ge(decay_in.sem, decay_in.at(h, 2) * 16)
                    gp.wait_ge(stepped.sem, stepped.at(h, 18))
                    gp.wait_ge(S_made.sem, S_made.at(h, 16))
                    gp.wait_ge(rhs_made.sem, rhs_made.at(h, 16))
                    gp.wait_ge(vnew_made.sem, vnew_made.at(h, 36))
                    prepare(h + 1)
                    for d in range(DIRS):
                        mask(d)
                gp.wait_ge(oz_made.sem, oz_made.at(h, 4))
                gp.dma_start(scr_o[bd(h, 1)].rearrange("a p t -> (a p) t"), oz).then_inc(oz_stored.sem, 16)
                own.settle()
                if not last:
                    gp.wait_ge(oz_stored.sem, oz_stored.at(h, 1) * 16)
                    own(gp.tensor_tensor(clear_mark, ident[:, 0:1], ident[:, 0:1], ALU.mult))
                    gp.memset(Zt, 0.0).then_inc(Zt_cleared.sem, 1)
                own.clear()

            gp.wait_ge(decay_in.sem, 32)
            prepare(0)
            for d in range(DIRS):
                mask(d)
            own.clear()
            with gp.Fori(0, HEADS - 1) as h:
                head(h)
            head(HEADS - 1, last=True)
            gp.wait_ge(post_in, 16 * 5)
            for s in range(2):
                gp.tensor_tensor(gate_post[:, s], gate_post[:, s], post_b, ALU.mult).then_inc(gate_post_made, 1)

            def residual(buf, n):
                gp.wait_ge(xr_in[buf], n)
                for half, add in enumerate((pos_row_res[:, buf], pos_col_res)):
                    cc = slice(512 * half, 512 * half + 512)
                    gp.tensor_tensor(x_res[:, buf, cc], x_res[:, buf, cc], add, ALU.add).then_inc(xr_added, 1)

            with gp.Fori(0, 4) as i:
                residual(1, i * 48 + 48)
                residual(0, i * 48 + 64)

        @block.tensor
        def _(pe):
            pe.wait_ge(consts_made, 1)
            pe.wait_ge(rows_in, 16 * 11)
            pe.transpose(banks[6][:, 0:P], rowsA, ident).then_inc(cols_turned, 1)
            pe.transpose(banks[7][:, 0:B_ROWS], rowsB[0:B_ROWS, :], ident[0:B_ROWS, 0:B_ROWS]).then_inc(cols_turned, 1)
            pe.wait_ge(silu_c_made, 1)
            for n in range(NCH):
                pe.wait_ge(x_normed, n + 1)
                for half in range(2):
                    if n:
                        pe.wait_ge((h_made_v, h_made_a)[half], 4 * n)
                    for k in range(4):
                        mm = pe.transpose(banks[6 + half][:, P * k:P * k + P],
                                          x_in[:, n % 2, P * (4 * half + k):P * (4 * half + k) + P], ident)
                    mm.then_inc(x_turned, 1)
                if n < KT:
                    pe.wait_ge(ada_in[n], 16)
                    for j in range(6):
                        mm = pe.matmul(banks[j][0:2, :], silu_c[:, :, n], adaw[:, n, 512 * j:512 * j + 512],
                                       start=(n == 0), stop=(n == KT - 1))
                        if n == KT - 1:
                            mm.then_inc(ada_done, 1)
            pe.wait_ge(h_made_v, 4 * NCH)
            for m in range(16):
                pe.wait_ge(mod_row_made, m // 4 + 1)
                mm = pe.transpose(banks[6][:, 2 * m:2 * m + 2], mod_row[0:2, P * m:P * m + P], ident[0:2, 0:2])
            mm.then_inc(mod_turned, 1)
            pe.wait_ge(mod_row_made, 6)
            pe.wait_ge(ba_w_in, 16)
            pe.wait_ge(h_modded_v, 2 * MOD_V)
            pe.wait_ge(h_modded_a, 2 * (KT - MOD_V))
            for g, (o, n) in enumerate(GROUPS):
                for k in range(KT):
                    mm = pe.matmul(banks[5 + g][0:32, 0:n], w_ring[:, 0, k, 0:32], hT[:, k, o:o + n],
                                   start=(k == 0), stop=(k == KT - 1))
                if g == 2:
                    mm.then_inc(ba_done, 1)

            def project(first, count, h=None):
                for u in range(first, first + count):
                    j, g, k = u // 24, u % 24 // 8, u % 8
                    n = u // 8
                    if u % 24 == 0:
                        slot = w_in_slot[j % 3]
                        if h is None:
                            pe.wait_ge(slot.sem, 16 if j < 5 else 32)
                        else:
                            pe.wait_ge(slot.sem, slot.at(h, j // 3 + 1) * 16)
                    if k == 0:
                        if h is not None:
                            pe.wait_ge(proj_taken.sem, proj_taken.at(h, n - 1))
                        elif n >= 8:
                            pe.wait_ge(proj_taken.sem, n - 7)
                    o, w = GROUPS[g]
                    mm = pe.matmul(banks[n % 2][:, 0:w], w_ring[:, j % 3, k], hT[:, k, o:o + w],
                                   start=(k == 0), stop=(k == KT - 1))
                    if k == KT - 1:
                        mm.then_inc(projected.sem, 1)

            project(48, 24)
            pe.wait_ge(baT_made, 3)
            for ch in range(NCH):
                mm = pe.transpose(banks[2][:, 32 * ch:32 * ch + 32], baT[0:32, col(ch):col(ch) + P], ident[0:32, 0:32])
            mm.then_inc(ba_turned, 1)
            project(72, 24)
            pe.wait_ge(g_made, 1)
            g = sp_e[:, 0:NCH * 16].rearrange("p (c n) -> p c n", n=16)
            G_ps = banks[3][:, 0:NCH * 16].rearrange("p (c n) -> p c n", n=16)
            for d in range(DIRS):
                pe.matmul(G_ps[:, :, 8 * d:8 * d + 8], tri[:, d], g[:, :, 8 * d:8 * d + 8], start=True, stop=True)\
                  .then_inc(G_summed, 1)
            pe.matmul(banks[4][:, 0:NCH * 16], ones, sp_e[:, 0:NCH * 16], start=True, stop=True).then_inc(G_summed, 1)
            row_banks = [[5, 6, 7], [2, 3, 4]]
            for d in range(DIRS):
                if d == 1:
                    pe.wait_ge(G_taken, 2)
                for ch in range(NCH):
                    mm = pe.matmul(banks[row_banks[d][ch // 4]][0:8, P * (ch % 4):P * (ch % 4) + P],
                                   g[:, ch, 8 * d:8 * d + 8], tri[:, d], start=True, stop=True)
                    if ch % 4 == 3 or ch == NCH - 1:
                        mm.then_inc(Grow_done, 1)
            project(96, 48)

            def turn(src, first_bank):
                for b in range(3):
                    for i in range(3):
                        ch = 3 * b + i
                        mm = pe.transpose(banks[first_bank + b][:, P * i:P * i + P], src[:, col(ch):col(ch) + P], ident)
                    mm.then_inc(turned.sem, 1)

            def head(h, last=False):
                cursor = [0]

                def fill(count):
                    first, cursor[0] = cursor[0], cursor[0] + count
                    if last:
                        count = max(0, min(count, 48 - first))
                    project(first, count, h)

                fill(8)
                pe.wait_ge(oz_made.sem, oz_made.at(h, 0))
                pe.wait_ge(silu_done.sem, silu_done.at(h, -1))
                turn(qT, 5)
                for f in range(5):
                    pe.wait_ge(turn_taken_a.sem, turn_taken_a.at(h, (4, 8, 12, 15, 18)[f]))
                    for i in range(2 if f < 4 else 1):
                        ch = 2 * f + i
                        mm = pe.matmul(banks[2 + f][:, 2 * P * i:2 * P * i + 2 * P].rearrange("p (j t) -> p j t", j=2),
                                       kT[:, col(ch):col(ch) + P], kq[:, :, col(ch):col(ch) + P], start=True, stop=True)
                    mm.then_inc(scored.sem, 1)
                fill(16)
                pe.wait_ge(wg_in.sem, wg_in.at(h, 0) * 16)
                pe.wait_ge(conv_done.sem, conv_done.at(h, 0))
                pe.wait_ge(turn_taken_a.sem, turn_taken_a.at(h, 21))
                for d in range(DIRS):
                    for gate in range(2):
                        if d == 0 and gate == 1:
                            fill(8)
                            pe.wait_ge(silu_done.sem, silu_done.at(h, 1))
                            turn(vT, 2)
                            fill(4)
                        for b, (o, n) in enumerate(GROUPS):
                            if d == 0 and gate == 0:
                                pe.wait_ge(scores_taken.sem, scores_taken.at(h, 28))
                            elif d == 0:
                                pe.wait_ge(turn_taken_v.sem, turn_taken_v.at(h, b + 1))
                            else:
                                pe.wait_ge(gate_tanh.sem, gate_tanh.at(h, 3 * gate + b + 1))
                            pe.matmul(banks[(2 if gate else 5) + b][:, 0:n], wg[:, 2 * gate + d], xf[:, o:o + n],
                                      start=True, stop=True).then_inc(gated.sem, 1)
                    if d == 0:
                        fill(4)
                fill(BEFORE_JOINS - cursor[0])
                pe.wait_ge(Z_placed.sem, Z_placed.at(h, 8))
                pe.wait_ge(Zt_placed.sem, Zt_placed.at(h, 8))
                pe.wait_ge(gate_tanh.sem, gate_tanh.at(h, 12))

                def q_products(level, g):
                    b = banks[2 if g % 2 == 0 else 5]
                    if g >= 2:
                        pe.wait_ge(Q_taken.sem, Q_taken.at(h, 6 * level + g - 1))
                    elif level:
                        pe.wait_ge(Q_taken.sem, Q_taken.at(h, 6))
                    if level:
                        pe.wait_ge(dZ_taken.sem, dZ_taken.at(h, 4 * g + 4))
                    for i in range(3):
                        m = 3 * g + i
                        mm = pe.matmul(b[:, P * i:P * i + P], nmat[:, m], Zt[:, m], start=True, stop=True)
                    mm.then_inc(Q_done.sem, 1)

                def join32(g):
                    b = 3 if g % 2 == 0 else 6
                    pe.wait_ge(Q_taken.sem, Q_taken.at(h, g + 1))
                    if g >= 2:
                        pe.wait_ge(dZ_taken.sem, dZ_taken.at(h, 4 * (g - 1)))
                    for i in range(3):
                        pe.matmul(banks[b][:, P * i:P * i + P], Z[:, 3 * g + i], Qb[:, g % 2, i], start=True, stop=True)
                    for i in range(3):
                        mm = pe.matmul(banks[b + 1][:, P * i:P * i + P], Qb[:, g % 2, i], Z[:, 3 * g + i],
                                       start=True, stop=True)
                    mm.then_inc(dZ_done.sem, 1)

                def join64(g):
                    b = banks[3 if g % 2 == 0 else 6]
                    pe.wait_ge(Q_taken.sem, Q_taken.at(h, 6 + g + 1))
                    pe.wait_ge(dZ_taken.sem, dZ_taken.at(h, 24 + g - 1 if g >= 2 else 24))
                    r = slice(64, P) if g < 3 else slice(0, 64)
                    for i in range(3):
                        mm = pe.matmul(b[:, P * i:P * i + P], Qb[r, g % 2, i], Z[r, 3 * g + i], start=True, stop=True)
                    mm.then_inc(dZ_done.sem, 1)

                for level, join in ((0, join32), (1, join64)):
                    for g in range(7):
                        if g < 6:
                            q_products(level, g)
                            fill(LEVEL_FILLS[6 * level + g])
                        if g > 0:
                            join(g - 1)
                pe.wait_ge(dZ_taken.sem, dZ_taken.at(h, 30))
                pe.wait_ge(v_scaled.sem, v_scaled.at(h, 1))
                pe.wait_ge(qd_made.sem, qd_made.at(h, 4))
                for step in range(NCH):
                    chunk = (step, step if step == 0 else NCH - step)
                    if step:
                        for d in range(DIRS):
                            if step == 1:
                                pe.wait_ge(S_in.sem, S_in.at(h, 0) * 16)
                            else:
                                pe.wait_ge(S_made.sem, S_made.at(h, 2 * step - 2 + d + 1))
                            pe.matmul(banks[2 + d][:, 0:P], kT[:, col(chunk[d]):col(chunk[d]) + P], S[:, d],
                                      start=True, stop=True).then_inc(KS_done.sem, 1)
                        for d in range(DIRS):
                            pe.wait_ge(o_made.sem, o_made.at(h, 1 if step == 1 else 2 * step - 2 + d))
                            pe.matmul(banks[6 + d][:, 0:P], qd[:, d, P * chunk[d]:P * chunk[d] + P], S[:, d],
                                      start=True, stop=False)
                        fill(1)
                    for d in range(DIRS):
                        if step:
                            pe.wait_ge(rhs_made.sem, rhs_made.at(h, 2 * step - 2 + d + 1))
                        rhs = rhs_v[:, d] if step else vtok[:, 0]
                        pe.matmul(banks[2 + d][:, P:2 * P], Z[:, d * NCH + chunk[d]], rhs, start=True, stop=True)\
                          .then_inc(solved.sem, 1)
                    fill(2)
                    if step < NCH - 1:
                        for d in range(DIRS):
                            pe.wait_ge(vnew_made.sem, vnew_made.at(h, 4 * step + d + 1))
                            if step == 1 and d == 0:
                                pe.wait_ge(S_made.sem, S_made.at(h, 2))
                            pe.matmul(banks[4 + d][:, 0:P], ktok[:, chunk[d]], vd[:, d], start=True, stop=True)\
                              .then_inc(S_done.sem, 1)
                    fill(SCAN_FILLS[step] - (3 if step else 2))
                    for d in range(DIRS):
                        pe.wait_ge(vnew_made.sem, vnew_made.at(h, 4 * step + 2 + d + 1))
                        pe.matmul(banks[6 + d if step else 6][:, 0:P], decay[:, d * NCH + chunk[d]], vt[:, d],
                                  start=(step == 0 and d == 0), stop=(step > 0 or d == 1)).then_inc(stepped.sem, 1)
                fill(5)
                if not last:
                    pe.wait_ge(silu_done.sem, silu_done.at(h, 5))
                    pe.wait_ge(o_made.sem, o_made.at(h, 17))
                    turn(kT, 2)
                fill(5)
                pe.wait_ge(o_normed.sem, o_normed.at(h, 1))
                for b in range(3):
                    for i in range(3):
                        mm = pe.transpose(banks[(6, 7, 5)[b]][:, P * i:P * i + P], o_tok[:, 3 * b + i], ident)
                    mm.then_inc(o_turned.sem, 1)

            pe.wait_ge(silu_done.sem, 2)
            pe.wait_ge(G_taken, 8)
            turn(kT, 2)

            with pe.Fori(0, HEADS - 1) as h:
                head(h)
            head(HEADS - 1, last=True)

            pe.wait_ge(oz_made.sem, oz_made.at(HEADS - 1, 4))
            pe.wait_ge(rg_scanned.sem, rg_scanned.at(HEADS - 1, 6))
            pe.transpose(banks[7][0:16, 0:P], hc[:, 244:260], ident).then_inc(states_turned, 1)

            def out_tile(buf, n, first=False):
                pe.wait_ge(ot_hi_made, n + 1)
                pe.wait_ge(ot_lo_made, n + 1)
                if not isinstance(n, int) or n >= 2:
                    pe.wait_ge(y_made, n - 1)
                for half in range(2):
                    for k in range(16):
                        if first and half == 0:
                            pe.wait_ge(wo_hi_made, k + 1)
                            pe.wait_ge(wo_lo_made, k + 1)
                        kk, cc = slice(P * k, P * k + P), slice(512 * half, 512 * half + 512)
                        for i, (a, b) in enumerate(((ot_hi, wo_hi), (ot_hi, wo_lo), (ot_lo, wo_hi))):
                            mm = pe.matmul(banks[2 * buf + half][:, :], a[:, buf, kk], b[:, k, cc],
                                           start=(k == 0 and i == 0), stop=(k == 15 and i == 2))
                mm.then_inc(y_done, 1)

            out_tile(0, 0, first=True)
            out_tile(1, 1)
            with pe.Fori(0, 3) as i:
                out_tile(0, 2 * i + 2)
                out_tile(1, 2 * i + 3)
            out_tile(0, 8)

        @block.scalar
        def _(act):
            own = Chain(act, a_own)
            act.wait_ge(cols_made, 2)
            act.activation(silu_c, colsB[:, 0:16].rearrange("p (s k) -> p s k", s=2), ACT.Tanh, scale=0.5).then_inc(c_tanh, 1)

            def x_tile(buf, n):
                if isinstance(n, int) and n == 0:
                    act.wait_ge(x_loaded[0], 16)
                else:
                    act.wait_ge(x_added, n)
                    act.wait_ge(x_squared, n)
                act.activation(square_out, x_in[:, buf], ACT.Square, accum_out=x_ss[:, buf:buf + 1]).then_inc(x_squared, 1)
                act.wait_ge(x_meaned, n + 1)
                act.activation(x_ss[:, buf:buf + 1], x_ss[:, buf:buf + 1], ACT.Sqrt).then_inc(x_rooted, 1)
                act.wait_ge(x_turned, 2 * n + 2)
                first = 0 if isinstance(n, int) and n == 0 else GAP + P * n
                for k in range(4):
                    act.activation(hT[:, 4 + k, bd(first, P)], banks[7][:, P * k:P * k + P], ACT.Copy).then_inc(h_made_a, 1)

            x_tile(0, 0)
            x_tile(1, 1)
            with act.Fori(0, 3) as i:
                x_tile(0, 2 * i + 2)
                x_tile(1, 2 * i + 3)
            x_tile(0, 8)
            act.wait_ge(mod_made, 3)
            act.wait_ge(h_made_a, 4 * NCH)
            act.wait_ge(h_made_v, 4 * NCH)
            for k in range(MOD_V, KT):
                for s, cc in enumerate((slice(0, P), slice(P + GAP, TW))):
                    act.activation(hT[:, k, cc], hT[:, k, cc], ACT.Identity, bias=mod_ab[:, 2 + s, k:k + 1],
                                   scale=mod_ab[:, s, k:k + 1]).then_inc(h_modded_a, 1)
            act.wait_ge(consts_in, 48)
            act.activation(a_log, a_log, ACT.Exp).then_inc(sp_exped, 1)

            def take_projection(n, h=None):
                j, g = n // 3, n % 3
                o, w = GROUPS[g]
                if h is None:
                    act.wait_ge(projected.sem, n - 5)
                else:
                    act.wait_ge(projected.sem, projected.at(h, n + 1))
                    if j >= 2 and g == 0:
                        act.wait_ge(conv_done.sem, conv_done.at(h, j - 4))
                if j < 2:
                    act.activation((sz, sg)[j][:, o:o + w], banks[n % 2][:, 0:w], ACT.Copy, scale=0.5)\
                       .then_inc(proj_taken.sem, 1)
                else:
                    act.activation(raw[:, j - 2, 2 + o:2 + o + w], banks[n % 2][:, 0:w], ACT.Copy)\
                       .then_inc(proj_taken.sem, 1)

            act.wait_ge(raw_cleared, 1)
            for n in range(6, 9):
                take_projection(n)
            act.wait_ge(ba_made, 1)
            act.activation(cols["beta"], ba[:, :, 0:16], ACT.Exp, scale=-1.0).then_inc(sp_exped, 1)
            act.wait_ge(sp_ready, 2)
            own(act.activation(sp_e, sp_y, ACT.Abs))
            act.activation(sp_e, sp_e, ACT.Exp, scale=-1.0).then_inc(sp_exped, 1)
            for n in range(9, 12):
                take_projection(n)
            act.wait_ge(G_exp_in, 1)
            act.activation(cols["eG"], cols["cum"], ACT.Exp).then_inc(G_exped, 1)
            act.activation(cols["gl"], cols["tot"], ACT.Exp).then_inc(G_exped, 1)
            act.activation(cols["edec"], cols["edec"], ACT.Exp).then_inc(G_exped, 1)
            act.wait_ge(gate_stored, 16)
            for n in range(12, 18):
                take_projection(n)
                if n == 14:
                    for to, src in ((qT, RB), (kT, RA)):
                        act.wait_ge(conv_done.sem, 2)
                        act.activation(to, src, ACT.Tanh).then_inc(tanh_done.sem, 1)
            act.wait_ge(decay_in.sem, 32)
            act.wait_ge(grounds_made, 1)
            act.activation(view("sub", 0, 2 * TOK), view("nmat"), ACT.Exp).then_inc(eG_row.sem, 1)

            def head(h, last=False):
                act.wait_ge(head_cols_made.sem, head_cols_made.at(h, 0))
                for d in range(DIRS):
                    act.wait_ge(masked.sem, masked.at(h, d - 1))
                    for ch in range(NCH):
                        m = NCH * d + ch
                        act.activation(decay[:, m], decay[:, m], ACT.Exp, bias=hcv["ncum"][:, d, ch:ch + 1])\
                           .then_inc(decay_exped.sem, 1)
                for b in range(3):
                    act.wait_ge(turned.sem, turned.at(h, b - 2))
                    act.activation(ktok[:, 3 * b:3 * b + 3], banks[2 + b][:, 0:3 * P].rearrange("p (c d) -> p c d", d=P),
                                   ACT.Copy).then_inc(turn_taken_a.sem, 1)
                    for i in range(3):
                        c1 = 3 * b + i
                        act.activation(RC[:, P * c1:P * c1 + P], banks[2 + b][:, P * i:P * i + P], ACT.Square,
                                       accum_out=hcc["ssk"][:, c1:c1 + 1]).then_inc(turn_taken_a.sem, 1)
                act.wait_ge(oz_made.sem, oz_made.at(h, 0))
                take_projection(0, h)
                for b in range(3):
                    act.wait_ge(turned.sem, turned.at(h, b + 1))
                    for i in range(3):
                        c1 = 3 * b + i
                        act.activation(RH[:, P * c1:P * c1 + P], banks[5 + b][:, P * i:P * i + P], ACT.Square,
                                       accum_out=hcc["ssq"][:, c1:c1 + 1]).then_inc(turn_taken_a.sem, 1)
                take_projection(1, h)
                act.wait_ge(conv_done.sem, conv_done.at(h, 1))
                act.activation(tanh_v, vT, ACT.Tanh).then_inc(tanh_done.sem, 1)
                take_projection(2, h)
                act.wait_ge(silu_done.sem, silu_done.at(h, 0))
                for d in range(DIRS):
                    if d == 1:
                        act.wait_ge(rg_scanned.sem, rg_scanned.at(h, 3))
                    for b, (o, n) in enumerate(GROUPS):
                        act.wait_ge(gated.sem, gated.at(h, 6 * d + b + 1))
                        act.activation(RA[:, o:o + n], banks[5 + b][:, 0:n], ACT.Tanh, scale=0.5,
                                       bias=br_h[:, d:d + 1]).then_inc(gate_tanh.sem, 1)
                    act.wait_ge(gate_tanh.sem, gate_tanh.at(h, 6 * d + 3))
                    act.activation(RB, RA, ACT.Tanh, scale=nc8_h[:, d:d + 1], bias=nc8_h[:, d:d + 1])\
                       .then_inc(rg_t_made.sem, 1)
                    act.wait_ge(rg_t_made.sem, rg_t_made.at(h, 3 * d + 1))
                    act.activation(RA, RA, ACT.Exp, scale=c8_h[:, d:d + 1], bias=c8_h[:, d:d + 1])\
                       .then_inc(rg_t_made.sem, 1)
                    act.wait_ge(rg_t_made.sem, rg_t_made.at(h, 3 * d + 2))
                    act.activation(RC, RA, ACT.Square).then_inc(rg_t_made.sem, 1)
                    if d == 1:
                        take_projection(5, h)
                    act.wait_ge(rg_u_made.sem, rg_u_made.at(h, d + 1))
                    for b, (o, n) in enumerate(GROUPS):
                        act.wait_ge(gated.sem, gated.at(h, 6 * d + 3 + b + 1))
                        act.activation(RC[:, o:o + n], banks[2 + b][:, 0:n], ACT.Tanh, scale=0.5,
                                       bias=bi_h[:, d:d + 1]).then_inc(gate_tanh.sem, 1)
                    act.activation(RB, RB, ACT.Sqrt, scale=0.25).then_inc(rg_root.sem, 1)
                    if d == 0:
                        act.wait_ge(ss_done.sem, ss_done.at(h, 1))
                        act.activation(hcc["rkinv"], hcc["ssk"], ACT.Sqrt).then_inc(rk_root.sem, 1)
                        for n in (3, 4):
                            take_projection(n, h)
                if not last:
                    for n in range(6, BEFORE_JOINS // 8):
                        take_projection(n, h)
                act.wait_ge(Zt_cleared.sem, Zt_cleared.at(h, 0))
                for d in range(DIRS):
                    src = block_T if d else block_in
                    act.wait_ge(unblocked.sem, unblocked.at(h, 2))
                    for q in range(4):
                        r = slice(BLK * q, BLK * q + BLK)
                        act.activation(Zt[r, NCH * d:NCH * d + NCH, r], src[r, NCH * d:NCH * d + NCH, :], ACT.Copy)\
                           .then_inc(Zt_placed.sem, 1)
                done = [BEFORE_JOINS // 8, BEFORE_JOINS]

                def given(count):
                    done[1] += count
                    while 8 * (done[0] + 1) <= done[1]:
                        if not last:
                            take_projection(done[0], h)
                        done[0] += 1

                for g in range(6):
                    act.wait_ge(dZ_done.sem, dZ_done.at(h, g + 1))
                    m = slice(3 * g, 3 * g + 3)
                    for to, bank, below in ((Zt, 3, g < 3), (Z, 4, g >= 3)):
                        ps = banks[bank + 3 * (g % 2)][:, 0:3 * P].rearrange("p (m i) -> p m i", i=P)
                        for b in (0, 2):
                            r, cc = (b + 1, b) if below else (b, b + 1)
                            r, cc = slice(BLK * r, BLK * r + BLK), slice(BLK * cc, BLK * cc + BLK)
                            act.activation(to[r, m, cc], ps[r, :, cc], ACT.Copy).then_inc(dZ_taken.sem, 1)
                    given(LEVEL_FILLS[g])
                act.wait_ge(Z_placed.sem, Z_placed.at(h, 8))
                act.wait_ge(Zt_placed.sem, Zt_placed.at(h, 8))
                act.wait_ge(proj_taken.sem, proj_taken.at(h, 6))
                for to, src in ((tanh_z, sz), (tanh_g, sg)):
                    act.activation(to, src, ACT.Tanh).then_inc(tanh_done.sem, 1)
                for g in range(6):
                    act.wait_ge(dZ_done.sem, dZ_done.at(h, 6 + g + 1))
                    ps = banks[3 + 3 * (g % 2)][:, 0:3 * P].rearrange("p (m i) -> p m i", i=P)
                    r, cc = (slice(0, 64), slice(64, P)) if g < 3 else (slice(64, P), slice(0, 64))
                    act.activation(Z[r, 3 * g:3 * g + 3, cc], ps[r, :, cc], ACT.Copy).then_inc(dZ_taken.sem, 1)
                    given(LEVEL_FILLS[6 + g])

                def square_o(chunks):
                    for ch in chunks:
                        act.activation(RC[:, P * ch:P * ch + P], o_tok[:, ch], ACT.Square,
                                       accum_out=hcc["sso"][:, ch:ch + 1]).then_inc(o_squared.sem, 1)

                for step in range(NCH):
                    chunk = (step, step if step == 0 else NCH - step)
                    for to, scale in ((vd, "Pdec"), (vt, "Pk")):
                        for d in range(DIRS):
                            act.wait_ge(solved.sem, solved.at(h, 2 * step + d + 1))
                            c1 = slice(chunk[d], chunk[d] + 1)
                            act.activation(to[:, d], banks[2 + d][:, P:2 * P], ACT.Copy, scale=hcv[scale][:, d, c1])\
                               .then_inc(vnew_made.sem, 1)
                    given(SCAN_FILLS[step])
                    if step == 4 and not last:
                        act.wait_ge(conv_done.sem, conv_done.at(h, 3))
                        act.activation(qT, RB, ACT.Tanh).then_inc(tanh_done.sem, 1)
                        act.wait_ge(silu_done.sem, silu_done.at(h, 3))
                        act.wait_ge(decay_in.sem, decay_in.at(h, 2) * 16)
                        act.activation(view("sub", 0, 2 * TOK), view("nmat"), ACT.Exp).then_inc(eG_row.sem, 1)
                    if step == 7:
                        act.wait_ge(o_made.sem, o_made.at(h, 13))
                        act.wait_ge(rg_stored.sem, rg_stored.at(h, 2) * 16)
                        square_o((0, 3, 4, 5, 6))
                if not last:
                    act.wait_ge(conv_done.sem, conv_done.at(h, 2))
                    act.wait_ge(KS_done.sem, KS_done.at(h, 16))
                    act.activation(kT, RA, ACT.Tanh).then_inc(tanh_done.sem, 1)
                act.wait_ge(o_made.sem, o_made.at(h, 15))
                square_o((2, 7))
                act.wait_ge(o_made.sem, o_made.at(h, 17))
                square_o((1, 8))
                act.wait_ge(o_meaned.sem, o_meaned.at(h, 1))
                act.activation(hcc["rstd"], hcc["rstd"], ACT.Sqrt).then_inc(o_rooted.sem, 1)
                if not last:
                    for n in (16, 17):
                        if n >= done[0]:
                            take_projection(n, h)

            with act.Fori(0, HEADS - 1) as h:
                head(h)
            head(HEADS - 1, last=True)

            def high_part(buf, n, loaded):
                act.wait_ge(ot_in[buf], loaded)
                if not isinstance(n, int) or n >= 2:
                    act.wait_ge(y_done, n - 1)
                act.activation(ot_hi[:, buf], ot[:, buf], ACT.Copy).then_inc(ot_hi_made, 1)

            def y_tile(buf, n):
                act.wait_ge(y_done, n + 1)
                for half in range(2):
                    if not (isinstance(n, int) and n == 0 and half == 0):
                        act.wait_ge(y_squared, 2 * n + half)
                    act.activation(y_junk[:, 512 * half:512 * half + 512], banks[2 * buf + half][:, :], ACT.Square,
                                   accum_out=y_ss[:, 4 * buf + half:4 * buf + half + 1]).then_inc(y_squared, 1)
                act.wait_ge(y_meaned, n + 1)
                act.activation(y_ss[:, 4 * buf + 2:4 * buf + 3], y_ss[:, 4 * buf + 2:4 * buf + 3], ACT.Sqrt)\
                   .then_inc(y_rooted, 1)

            act.wait_ge(oz_made.sem, oz_made.at(HEADS - 1, 4))
            for k in range(16):
                if k == 4:
                    high_part(0, 0, 16)
                act.wait_ge(w_out_in[k // 4], 16)
                act.activation(wo_hi[:, k], wo[:, k], ACT.Copy).then_inc(wo_hi_made, 1)
            act.wait_ge(gate_post_made, 2)
            high_part(1, 1, 16)
            y_tile(0, 0)
            high_part(0, 2, 32)
            y_tile(1, 1)
            with act.Fori(0, 3) as i:
                high_part(1, 2 * i + 3, 16 * i + 32)
                y_tile(0, 2 * i + 2)
                high_part(0, 2 * i + 4, 16 * i + 48)
                y_tile(1, 2 * i + 3)
            y_tile(0, 8)

        @block.vector
        def _(dve):
            own = Chain(dve, v_own)
            dve.wait_ge(cols_turned, 2)
            dve.tensor_copy(colsA, banks[6][:, 0:P]).then_inc(cols_made, 1)
            dve.tensor_copy(colsB[:, 0:B_ROWS], banks[7][:, 0:B_ROWS]).then_inc(cols_made, 1)
            dve.wait_ge(c_tanh, 1)
            c_cols = colsB[:, 0:16].rearrange("p (s k) -> p s k", s=2)
            own(dve.scalar_tensor_tensor(silu_c, silu_c, 1.0, c_cols, ALU.add, ALU.mult))
            dve.tensor_scalar(silu_c, silu_c, 0.5, None, ALU.mult).then_inc(silu_c_made, 1)
            own(dve.tensor_scalar(colsA[:, 0:96], colsA[:, 0:96], 0.5, None, ALU.mult))
            own(dve.tensor_scalar(hc[:, 180:212], colsB[:, B_BR:B_BR + 32], 0.5, None, ALU.mult))
            id4 = ident.rearrange("p (q m) -> p q m", q=4)
            for to, first in ((pf, 0), (pb, NCH)):
                own(dve.tensor_reduce(to, id4[:, :, first:first + NCH], AX.XY, ALU.add))
                own(dve.tensor_scalar(to, to, -1.0, None, ALU.mult))
            def x_tile(buf, n, loaded):
                prompt = isinstance(n, int) and n == 0
                dve.wait_ge(x_loaded[buf], loaded)
                if not prompt:
                    dve.tensor_tensor(x_in[:, buf], x_in[:, buf], pos[:, buf], ALU.add).then_inc(x_added, 1)
                dve.wait_ge(x_squared, n + 1)
                dve.tensor_scalar(x_ss[:, buf:buf + 1], x_ss[:, buf:buf + 1], 1.0 / D, EPS, ALU.mult, ALU.add)\
                   .then_inc(x_meaned, 1)
                dve.wait_ge(x_rooted, n + 1)
                own(dve.reciprocal(x_ss[:, buf:buf + 1], x_ss[:, buf:buf + 1]))
                dve.tensor_scalar(x_in[:, buf], x_in[:, buf], x_ss[:, buf:buf + 1], None, ALU.mult).then_inc(x_normed, 1)
                dve.wait_ge(x_turned, 2 * n + 1)
                first = 0 if prompt else GAP + P * n
                for k in range(4):
                    dve.tensor_copy(hT[:, k, bd(first, P)], banks[6][:, P * k:P * k + P]).then_inc(h_made_v, 1)

            x_tile(0, 0, 16)
            dve.wait_ge(pos_in, 64)
            x_tile(1, 1, 48)
            own.clear()
            with dve.Fori(0, 3) as i:
                x_tile(0, 2 * i + 2, 48 * i + 64)
                x_tile(1, 2 * i + 3, 48 * i + 96)
                own.clear()
            x_tile(0, 8, 16 + 48 * 4)
            dve.wait_ge(ada_done, 6)
            dve.wait_ge(consts_in, 48)
            for n in range(6):
                dve.tensor_tensor(mod_row[0:2, 512 * n:512 * n + 512], banks[n][0:2, :],
                                  ada_brow[0:2, 512 * n:512 * n + 512], ALU.add).then_inc(mod_row_made, 1)
            dve.wait_ge(mod_turned, 1)
            m_ps = banks[6][:, 0:32].rearrange("p (m s) -> p s m", s=2)
            for s in range(2):
                dve.scalar_tensor_tensor(mod_ab[:, s], m_ps[:, s, 8:16], 1.0, colsB[:, B_PRE:B_PRE + 8],
                                         ALU.add, ALU.mult).then_inc(mod_made, 1)
            dve.tensor_copy(mod_ab[:, 2:4], m_ps[:, :, 0:8]).then_inc(mod_made, 1)
            dve.wait_ge(mod_made, 3)
            dve.wait_ge(h_made_v, 4 * NCH)
            dve.wait_ge(h_made_a, 4 * NCH)
            for k in range(MOD_V):
                for s, cc in enumerate((slice(0, P), slice(P + GAP, TW))):
                    dve.tensor_scalar(hT[:, k, cc], hT[:, k, cc], mod_ab[:, s, k:k + 1], mod_ab[:, 2 + s, k:k + 1],
                                      ALU.mult, ALU.add).then_inc(h_modded_v, 1)
            dve.wait_ge(ba_done, 1)
            for g, (o, n) in enumerate(GROUPS):
                dve.tensor_copy(baT[0:32, o:o + n], banks[5 + g][0:32, 0:n]).then_inc(baT_made, 1)
            dve.tensor_scalar(sp_y[:, NCH * 16:], colsB[:, B_LAM:B_LAM + 16], -1.0, None, ALU.mult).then_inc(sp_ready, 1)
            dve.wait_ge(ba_turned, 1)
            dve.tensor_copy(ba, banks[2][:, 0:NCH * 32].rearrange("p (c n) -> p c n", n=32)).then_inc(ba_made, 1)
            dve.wait_ge(ba_made, 1)
            by_tok = lambda a: a[:, 0:NCH * 16].rearrange("p (c n) -> p c n", n=16)
            dve.tensor_tensor(by_tok(sp_y), ba[:, :, 16:32], dt_bias.unsqueeze(1).to_broadcast([P, NCH, 16]), ALU.add)\
               .then_inc(sp_ready, 1)
            dve.wait_ge(sp_exped, 3)
            own(dve.tensor_scalar(sp_z, sp_e, 2.0, None, ALU.add))
            own(dve.reciprocal(sp_z, sp_z))
            own(dve.tensor_tensor(sp_z, sp_z, sp_e, ALU.mult))
            own(dve.tensor_tensor(sp_z2, sp_z, sp_z, ALU.mult))
            own(dve.tensor_scalar(sp_p, sp_z2, 1.0 / 15, None, ALU.mult))
            for n in (13, 11, 9, 7, 5, 3):
                own(dve.scalar_tensor_tensor(sp_p, sp_p, 1.0 / n, sp_z2, ALU.add, ALU.mult))
            own(dve.scalar_tensor_tensor(sp_p, sp_p, 1.0, sp_z, ALU.add, ALU.mult))
            own(dve.tensor_scalar(sp_r, sp_y, 0.0, None, ALU.max))
            own(dve.scalar_tensor_tensor(sp_r, sp_p, 2.0, sp_r, ALU.mult, ALU.add))
            dve.scalar_tensor_tensor(by_tok(sp_e), by_tok(sp_r), -1.0, a_log.unsqueeze(1).to_broadcast([P, NCH, 16]),
                                     ALU.mult, ALU.mult).then_inc(g_made, 1)
            own(dve.tensor_scalar(hc[:, 212:228], sp_r[:, NCH * 16:], -4.0, None, ALU.mult))
            own(dve.tensor_scalar(hc[:, 228:244], sp_r[:, NCH * 16:], 4.0, None, ALU.mult))
            own(dve.tensor_scalar(cols["beta"], cols["beta"], 1.0, None, ALU.add))
            own(dve.reciprocal(cols["beta"], cols["beta"]))
            dve.wait_ge(G_summed, 3)
            dve.tensor_copy(cols["cum"], by_tok(banks[3])).then_inc(G_taken, 1)
            dve.tensor_copy(cols["tot"], by_tok(banks[4])).then_inc(G_taken, 1)
            dve.wait_ge(G_taken, 2)
            dve.tensor_tensor(cols["edec"], cols["tot"], cols["cum"], ALU.subtract).then_inc(G_exp_in, 1)
            for d in range(DIRS):
                for b in range(3):
                    dve.wait_ge(Grow_done, 3 * d + b + 1)
                    n = min(4 * P, TOK - 4 * P * b)
                    dve.tensor_copy(G_rows[0:HEADS, d, 4 * P * b:4 * P * b + n], banks[(5, 2)[d] + b][0:HEADS, 0:n])\
                       .then_inc(G_taken, 1)
            dve.wait_ge(G_exped, 3)
            own(dve.tensor_scalar(cols["cum"], cols["cum"], -1.0, None, ALU.mult))
            dve.tensor_scalar(cols["eG"], cols["eG"], -1.0, None, ALU.mult).then_inc(cols_ready, 1)
            dve.wait_ge(grounds_made, 1)
            dve.wait_ge(G_stored, 32)
            dve.wait_ge(gate_stored, 16)
            dve.wait_ge(cols_ready, 1)
            own.clear()

            chv = {n: cols[n].rearrange("p c (d h) -> p h d c", d=2) for n in ("beta", "edec")}
            dview = decay.rearrange("p (d c) i -> p d c i", d=2)
            nview = nmat.rearrange("p (d c) i -> p d c i", d=2)
            X = sub[1].rearrange("p (a b) -> p a b", b=BLK)
            RG_AT = {1: ("silu_v", 0), 3: ("u", 0), 5: ("take_v", 0), 9: ("ix", 0), 14: ("scan", 0), 22: ("u", 1), 26: ("ix", 1)}
            RG_AFTER = (("scan", 1),)
            TAPS = [[(1, 0)], [(1, 1)], [(1, 2)], [(1, 3)], [], [(2, 0)], [(2, 1)], [(2, 2)], [(2, 3)]]
            prompt, sample = slice(0, P), slice(P + GAP, TW)
            runs = [(0, 0, P), (P, P + GAP, TOK - P)]

            def conv(j, dest, h, t):
                w = rconvw[:, t, bd(h, 1)] if j == 2 else convw[:, t, bd(h + (8, 0, 0, 16)[j], 1)]
                if t == 0 and j == 2:
                    own(dve.tensor_scalar(dest, raw[:, j, 0:TW], w, colsB[:, bd(B_CB + h, 1)], ALU.mult, ALU.add))
                elif t == 0:
                    own(dve.tensor_scalar(dest, raw[:, j, 0:TW], w, None, ALU.mult))
                else:
                    step = dve.scalar_tensor_tensor(dest, raw[:, j, t:t + TW], w, dest, ALU.mult, ALU.add)
                    if t == 3:
                        step.then_inc(conv_done.sem, 1)
                    else:
                        own(step)

            def silu(a, b, out):
                dve.scalar_tensor_tensor(out, a, 1.0, b, ALU.add, ALU.mult).then_inc(silu_done.sem, 1)

            for j, dest in enumerate((RA, RB, xf)):
                if j == 2:
                    for n, (t, x) in enumerate(((qT, RB), (kT, RA))):
                        dve.wait_ge(tanh_done.sem, n + 1)
                        silu(t, x, t)
                dve.wait_ge(proj_taken.sem, 3 * j + 3)
                for t in range(4):
                    conv(j, dest, 0, t)
            dve.sem_inc(oz_made.sem, 1)
            own.clear()

            def head(h, last=False):
                dve.wait_ge(proj_taken.sem, proj_taken.at(h, 0))
                for t in range(4):
                    conv(3, vT, h, t)
                dve.wait_ge(turn_taken_a.sem, turn_taken_a.at(h, 12))
                dve.wait_ge(head_cols_made.sem, head_cols_made.at(h, 0))
                own(dve.tensor_scalar(hcc["ssk"], hcc["ssk"], EPS, None, ALU.add))
                own(dve.reciprocal(hcc["rk2"], hcc["ssk"]))
                own(dve.tensor_tensor(hcv["Pk"], chv["beta"][:, bd(h, 1)].rearrange("p a d c -> p (a d) c"),
                                      hcc["rk2"].unsqueeze(1).to_broadcast([P, DIRS, NCH]), ALU.mult))
                dve.tensor_tensor(hcv["Pdec"], hcv["Pk"], chv["edec"][:, bd(h, 1)].rearrange("p a d c -> p (a d) c"),
                                  ALU.mult).then_inc(ss_done.sem, 1)
                dve.wait_ge(turn_taken_a.sem, turn_taken_a.at(h, 21))
                dve.tensor_scalar(hcc["epsq"], hcc["ssq"], P * EPS, P * EPS * EPS, ALU.mult, ALU.add)\
                   .then_inc(ss_done.sem, 1)
                for f in range(5):
                    dve.wait_ge(scored.sem, scored.at(h, f + 1))
                    n = 2 if f < 4 else 1
                    ps = banks[2 + f][:, 0:2 * P * n].rearrange("p (c j t) -> p c j t", j=2, t=P)
                    cs = slice(2 * f, 2 * f + n)
                    for d in range(DIRS):
                        for i in range(n):
                            m = NCH * d + 2 * f + i
                            dve.wait_ge(decay_exped.sem, decay_exped.at(h, m + 1))
                            dve.scalar_tensor_tensor(nmat[:, m], ps[:, i, 0], hcv["Pk"][:, d, 2 * f + i:2 * f + i + 1],
                                                     decay[:, m], ALU.mult, ALU.mult).then_inc(scores_taken.sem, 1)
                    dve.wait_ge(scores_taken.sem, scores_taken.at(h, 6 * f + 2 * n))
                    for d in range(DIRS):
                        dve.tensor_tensor(dview[:, d, cs], ps[:, :, 1], dview[:, d, cs], ALU.mult).then_inc(scores_taken.sem, 1)
                def rg_piece(what, d):
                    if what == "silu_v":
                        dve.wait_ge(tanh_done.sem, tanh_done.at(h, 1))
                        silu(tanh_v, vT, vT)
                    elif what == "take_v":
                        for b in range(3):
                            dve.wait_ge(turned.sem, turned.at(h, 3 + b + 1))
                            dve.tensor_copy(vtok[:, 3 * b:3 * b + 3],
                                            banks[2 + b][:, 0:3 * P].rearrange("p (c d) -> p c d", d=P)).then_inc(turn_taken_v.sem, 1)
                    elif what == "u":
                        dve.wait_ge(rg_t_made.sem, rg_t_made.at(h, 3 * d + 3))
                        dve.scalar_tensor_tensor(RB, RC, 1.0, RB, ALU.add, ALU.mult).then_inc(rg_u_made.sem, 1)
                    elif what == "ix":
                        dve.wait_ge(gate_tanh.sem, gate_tanh.at(h, 6 * d + 6))
                        dve.scalar_tensor_tensor(RC, RC, 1.0, xf, ALU.add, ALU.mult).then_inc(rg_ix_made.sem, 1)
                    else:
                        dve.wait_ge(rg_bx_made.sem, rg_bx_made.at(h, d + 1))
                        out = RC if d else RH
                        way = (lambda a: a[:, P - 1::-1], lambda a: a[:, TW - 1:P + GAP - 1:-1]) if d else \
                            (lambda a: a[:, prompt], lambda a: a[:, sample])
                        for run, first in zip(way, (0.0, colsB[:, bd(B_ST + 8 * d + h, 1)])):
                            dve.tensor_tensor_scan(run(out), run(RA), run(RB), first, ALU.mult, ALU.add)\
                               .then_inc(rg_scanned.sem, 1)
                        dve.wait_ge(rg_scanned.sem, rg_scanned.at(h, 3 * d + 1))
                        end = 0 if d else P - 1
                        dve.tensor_copy(st_rg[:, d, bd(h, 1)], out[:, end:end + 1]).then_inc(rg_scanned.sem, 1)

                dve.wait_ge(scores_taken.sem, scores_taken.at(h, 28))
                dve.wait_ge(qd_made.sem, qd_made.at(h, 4))
                for q in range(4):
                    r = slice(BLK * q, BLK * q + BLK)
                    own.later(dve.tensor_copy(block_in[r, 0:INST, :], nmat[r, :, r]))
                own.settle()
                own(dve.transpose(sub[1].rearrange("p (c r) -> p c r", c=BLK), sub[0].rearrange("p (m c) -> p c m", c=BLK)))
                own(dve.transpose(sub[2].rearrange("p (r c) -> p c r", c=BLK), sub[0].rearrange("p (m c) -> p c m", c=BLK)))
                own(dve.tensor_scalar(sub[2], sub[2], pb, None, ALU.mult))
                own(dve.scalar_tensor_tensor(sub[1], sub[1], pf, sub[2], ALU.mult, ALU.add))
                own(dve.memset(sub[1][:, 0:SQ:BLK + 1], 1.0))
                for k in range(1, BLK - 1):
                    if k in RG_AT:
                        rg_piece(*RG_AT[k])
                    rows = BLK - 1 - k
                    tmp = view("sub_tmp", 0, rows * k).rearrange("p (a b) -> p a b", b=k)
                    own(dve.tensor_tensor(tmp, X[:, k + 1:, k:k + 1].to_broadcast([P, rows, k]),
                                          X[:, k:k + 1, 0:k].to_broadcast([P, rows, k]), ALU.mult))
                    own(dve.tensor_tensor(X[:, k + 1:, 0:k], X[:, k + 1:, 0:k], tmp, ALU.add))
                dve.transpose(sub[2].rearrange("p (m a) -> p a m", a=BLK), X).then_inc(unblocked.sem, 1)
                dve.transpose(sub[0].rearrange("p (m b) -> p b m", b=BLK), X.rearrange("p a b -> p b a"))\
                   .then_inc(unblocked.sem, 1)
                dve.wait_ge(unblocked.sem, unblocked.at(h, 2))
                for d in range(DIRS):
                    for q in range(4):
                        r = slice(BLK * q, BLK * q + BLK)
                        dve.tensor_copy(Z[r, NCH * d:NCH * d + NCH, r], (block_in if d else block_T)[r, NCH * d:NCH * d + NCH, :])\
                           .then_inc(Z_placed.sem, 1)
                for piece in RG_AFTER:
                    rg_piece(*piece)
                for g in range(6):
                    dve.wait_ge(Q_done.sem, Q_done.at(h, g + 1))
                    if g >= 2:
                        dve.wait_ge(dZ_done.sem, dZ_done.at(h, g - 1))
                    ps = banks[2 + 3 * (g % 2)][:, 0:3 * P].rearrange("p (m i) -> p m i", i=P)
                    dve.tensor_tensor(Qb[:, g % 2], ps, mask32[:, g // 3].unsqueeze(1).to_broadcast([P, 3, P]), ALU.mult)\
                       .then_inc(Q_taken.sem, 1)
                    if g >= 2 and not last:
                        if g == 2:
                            dve.wait_ge(proj_taken.sem, proj_taken.at(h, 9))
                        conv(0, RA, h + 1, g - 2)
                for g in range(6):
                    dve.wait_ge(Q_done.sem, Q_done.at(h, 6 + g + 1))
                    dve.wait_ge(dZ_done.sem, dZ_done.at(h, 6 + g - 1))
                    ps = banks[2 + 3 * (g % 2)][:, 0:3 * P].rearrange("p (m i) -> p m i", i=P)
                    r = slice(64, P) if g < 3 else slice(0, 64)
                    dve.tensor_scalar(Qb[r, g % 2], ps[r], -1.0, None, ALU.mult).then_inc(Q_taken.sem, 1)
                    if g >= 4:
                        t, x = (tanh_z, sz) if g == 4 else (tanh_g, sg)
                        dve.wait_ge(tanh_done.sem, tanh_done.at(h, g - 2))
                        silu(t, x, x)
                dve.wait_ge(v_scaled.sem, v_scaled.at(h, 1))
                def silu_k():
                    dve.wait_ge(tanh_done.sem, tanh_done.at(h, 5))
                    silu(kT, RA, kT)

                def next_taps(step):
                    if last:
                        return
                    for j, t in TAPS[step]:
                        if j == 2 and t == 3:
                            silu_k()
                        if t == 0:
                            dve.wait_ge(proj_taken.sem, proj_taken.at(h, 9 + 3 * j))
                        conv(j, (RA, RB, xf)[j], h + 1, t)
                    if step == 5:
                        dve.wait_ge(tanh_done.sem, tanh_done.at(h, 4))
                        silu(qT, RB, qT)

                for step in range(NCH):
                    chunk = (step, step if step == 0 else NCH - step)
                    if step:
                        for d in range(DIRS):
                            dve.wait_ge(KS_done.sem, KS_done.at(h, 2 * step - 2 + d + 1))
                            c1 = slice(chunk[d], chunk[d] + 1)
                            dve.scalar_tensor_tensor(rhs_v[:, d], banks[2 + d][:, 0:P], hcv["negeG"][:, d, c1],
                                                     vtok[:, chunk[d]], ALU.mult, ALU.add).then_inc(rhs_made.sem, 1)
                    if step < NCH - 1:
                        next_taps(step)
                    if step == 0:
                        for d in range(DIRS):
                            dve.wait_ge(S_done.sem, S_done.at(h, d + 1))
                            dve.tensor_copy(S_new[:, d], banks[4 + d][:, 0:P]).then_inc(S_made.sem, 1)
                        dve.wait_ge(stepped.sem, stepped.at(h, 2))
                        dve.tensor_copy(o_tok[:, 0], banks[6][:, 0:P]).then_inc(o_made.sem, 1)
                        continue
                    if step < NCH - 1:
                        for d in range(DIRS):
                            dve.wait_ge(S_done.sem, S_done.at(h, 2 * step + d + 1))
                            if step == 1:
                                dve.wait_ge(S_in.sem, S_in.at(h, 0) * 16)
                            else:
                                dve.wait_ge(S_made.sem, S_made.at(h, 2 * step - 2 + d + 1))
                            ch = chunk[d]
                            dve.scalar_tensor_tensor(S[:, d], S[:, d], hcv["gl"][:, d, ch:ch + 1], banks[4 + d][:, 0:P],
                                                     ALU.mult, ALU.add).then_inc(S_made.sem, 1)
                    for d in range(DIRS):
                        ch = chunk[d]
                        dve.wait_ge(stepped.sem, stepped.at(h, 2 * step + d + 1))
                        if step <= 4:
                            dve.tensor_copy(o_tok[:, ch], banks[6 + d][:, 0:P]).then_inc(o_made.sem, 1)
                        else:
                            dve.wait_ge(o_made.sem, o_made.at(h, 2 * step - 1))
                            dve.tensor_tensor(o_tok[:, ch], banks[6 + d][:, 0:P], o_tok[:, ch], ALU.add)\
                               .then_inc(o_made.sem, 1)
                    if step == NCH - 1:
                        next_taps(step)
                dve.wait_ge(o_squared.sem, o_squared.at(h, NCH))
                dve.scalar_tensor_tensor(hcc["rstd"], hcc["sso"], 1.0 / P, hcc["epsq"], ALU.mult, ALU.add)\
                   .then_inc(o_meaned.sem, 1)
                dve.wait_ge(o_rooted.sem, o_rooted.at(h, 1))
                own(dve.reciprocal(hcc["rstd"], hcc["rstd"]))
                dve.tensor_tensor(o_tok, o_tok, hcc["rstd"].unsqueeze(2).to_broadcast([P, NCH, P]), ALU.mult)\
                   .then_inc(o_normed.sem, 1)
                for b, bank, a, to, z0, n in ((0, 6, 0, 0, 0, P), (0, 6, P, P, P + GAP, 2 * P),
                                              (1, 7, 0, 3 * P, 3 * P + GAP, 3 * P), (2, 5, 0, 6 * P, 6 * P + GAP, 3 * P)):
                    dve.wait_ge(o_turned.sem, o_turned.at(h, b + 1))
                    dve.scalar_tensor_tensor(oz[:, to:to + n], banks[bank][:, a:a + n], colsB[:, B_NW:B_NW + 1],
                                             sz[:, z0:z0 + n], ALU.mult, ALU.mult).then_inc(oz_made.sem, 1)
                own.clear()
                dve.wait_ge(prompt_S_stored.sem, prompt_S_stored.at(h, 1) * 16)

            with dve.Fori(0, HEADS - 1) as h:
                head(h)
            head(HEADS - 1, last=True)
            dve.wait_ge(states_turned, 1)
            dve.tensor_copy(hc[0:16, 0:P], banks[7][0:16, 0:P]).then_inc(states_taken, 1)

            def y_tile(buf, n, s):
                first = isinstance(n, int) and n < 2
                ss = lambda i: y_ss[:, 4 * buf + i:4 * buf + i + 1]
                dve.wait_ge(y_squared, 2 * n + 2)
                own(dve.tensor_tensor(ss(2), ss(0), ss(1), ALU.add))
                dve.tensor_scalar(ss(2), ss(2), 1.0 / D, EPS, ALU.mult, ALU.add).then_inc(y_meaned, 1)
                dve.wait_ge(y_rooted, n + 1)
                own(dve.reciprocal(ss(3), ss(2)))
                if not first:
                    dve.wait_ge(y_stored[buf], 8 * n if buf == 0 else 8 * n - 8)
                for half in range(2):
                    cc = slice(512 * half, 512 * half + 512)
                    own.later(dve.scalar_tensor_tensor(y_out[:, buf, cc], banks[2 * buf + half][:, :], ss(3),
                                                       gate_post[:, s, cc], ALU.mult, ALU.mult))
                own.settle()
                if isinstance(n, int) and n == 0:
                    dve.wait_ge(xr_in[0], 16)
                else:
                    dve.wait_ge(xr_added, 2 * n)
                dve.tensor_tensor(y_out[:, buf], y_out[:, buf], x_res[:, buf], ALU.add).then_inc(y_made, 1)

            def low_part(buf, n):
                dve.wait_ge(ot_hi_made, n + 1)
                dve.tensor_tensor(ot_lo[:, buf], ot[:, buf], ot_hi[:, buf].bitcast(F32), ALU.subtract).then_inc(ot_lo_made, 1)

            for k in range(16):
                if k == 4:
                    low_part(0, 0)
                dve.wait_ge(wo_hi_made, k + 1)
                dve.tensor_tensor(wo_lo[:, k], wo[:, k], wo_hi[:, k].bitcast(F32), ALU.subtract).then_inc(wo_lo_made, 1)
            dve.wait_ge(gate_post_made, 2)
            low_part(1, 1)
            y_tile(0, 0, 0)
            low_part(0, 2)
            y_tile(1, 1, 1)
            own.clear()
            with dve.Fori(0, 3) as i:
                low_part(1, 2 * i + 3)
                y_tile(0, 2 * i + 2, 1)
                low_part(0, 2 * i + 4)
                y_tile(1, 2 * i + 3, 1)
                own.clear()
            y_tile(0, 8, 1)


_INS = ["x_prompt", "x_sample", "state_delta", "state_rglru", "c", "c_ctx", "ada_w", "ada_b", "pre_norm_w",
        "post_norm_w", "w_in", "w_out", "dn_conv_w", "dn_a_log", "dn_dt_bias", "dn_norm_w", "rg_conv_w", "rg_conv_b",
        "rg_w_r", "rg_b_r", "rg_w_i", "rg_b_i", "rg_lam"]
_OUTS = [("y_prompt", (1, P, D)), ("y_sample", (1, TOK - P, D)), ("new_delta", (1, 1, DIRS, HEADS, P, P)),
         ("new_rglru", (1, 1, DIRS, D))]


def positions():
    quarter, width = D // 4, 64
    freqs = np.exp(np.float32(-math.log(10000.0)) * np.arange(quarter, dtype=np.float32) / np.float32(quarter))
    table = []
    for n in ((TOK - P) // width, width):
        angle = np.arange(n, dtype=np.float32)[:, None] * freqs[None]
        table.append(np.concatenate([np.sin(angle), np.cos(angle)], axis=1).astype(np.float32))
    return table


def build(nc):
    shapes = {
        "x_prompt": (1, P, D), "x_sample": (1, TOK - P, D), "state_delta": (1, 1, DIRS, HEADS, P, P),
        "state_rglru": (1, 1, DIRS, D), "c": (1, D), "c_ctx": (D,), "ada_w": (1, D, 3 * D), "ada_b": (1, 3 * D),
        "pre_norm_w": (1, D), "post_norm_w": (1, D), "w_in": (1, D, OFF_RG + D), "w_out": (1, 2 * D, D),
        "dn_conv_w": (1, 4, 3 * D), "dn_a_log": (1, DIRS, HEADS), "dn_dt_bias": (1, DIRS, HEADS), "dn_norm_w": (1, P),
        "rg_conv_w": (1, 4, D), "rg_conv_b": (1, D), "rg_w_r": (1, DIRS, HEADS, P, P), "rg_b_r": (1, DIRS, D),
        "rg_w_i": (1, DIRS, HEADS, P, P), "rg_b_i": (1, DIRS, D), "rg_lam": (1, DIRS, D)}
    args = [nc.dram_tensor(n, shapes[n], F32, kind="ExternalInput").ap() for n in _INS]
    args += [nc.dram_tensor(n, s, F32, kind="ExternalInput").ap() for n, s in (("pos_row", (16, 512)), ("pos_col", (64, 512)))]
    args += [nc.dram_tensor(n, s, F32, kind="ExternalOutput").ap() for n, s in _OUTS]
    hybrid_layer(nc, *args)


def kernel(**inputs):
    import concourse.bacc as bacc
    from concourse.bass_utils import run_bass_kernel_spmd

    nc = bacc.Bacc("TRN2", target_bir_lowering=False, num_devices=1)
    arrays = {n: np.ascontiguousarray(inputs[n]) for n in _INS}
    arrays["pos_row"], arrays["pos_col"] = positions()
    build(nc)
    got = run_bass_kernel_spmd(nc, [arrays], core_ids=[0]).results[0]
    return tuple(got[n] for n, _ in _OUTS)
```
